# Optimizing a Trainium2 kernel written in Bass

```python
import math
import jax, jax.numpy as jnp
from jax import lax
import numpy as np
import jax
import jax.numpy as jnp

D_MODEL = 1024
BATCH = 1
SEQ = 256
DEPTH = 1

HEAD_DIM = 64
SB_HEADS = (D_MODEL // 2) // HEAD_DIM
DIFF_HEADS = (D_MODEL // 2) // (2 * HEAD_DIM)
SB_WIDTH = SB_HEADS * HEAD_DIM
DIFF_WIDTH = DIFF_HEADS * 2 * HEAD_DIM
MIX_WIDTH = SB_WIDTH + DIFF_WIDTH
IN_WIDTH = 3 * MIX_WIDTH
D_FF = -(-8 * D_MODEL // (3 * 256)) * 256
Q_BLOCK = 128
ROPE_THETA = 10000.0
NORM_EPS = 1e-6
SUBLN_EPS = 1e-5


def rmsnorm(x, g, eps=NORM_EPS):
    xf = x.astype(jnp.float32)
    y = xf * lax.rsqrt(jnp.mean(xf * xf, axis=-1, keepdims=True) + eps) * g.astype(jnp.float32)
    return y.astype(x.dtype)

def rope(x, pos):
    half = HEAD_DIM // 2
    inv_freq = ROPE_THETA ** (-jnp.arange(half, dtype=jnp.float32) / half)
    ang = pos.astype(jnp.float32)[:, None] * inv_freq[None, :]
    cos, sin = jnp.cos(ang), jnp.sin(ang)
    xf = x.astype(jnp.float32)
    x1, x2 = xf[..., :half], xf[..., half:]
    return jnp.concatenate([x1 * cos - x2 * sin, x1 * sin + x2 * cos], axis=-1).astype(x.dtype)

def stick_breaking_attention(q, k, v):
    S = q.shape[2]
    scale = HEAD_DIM ** -0.5
    outs = []
    for start in range(0, S, Q_BLOCK):
        end = start + Q_BLOCK
        z = jnp.einsum('bhqd,bhkd->bhqk', q[:, :, start:end], k[:, :, :end]).astype(jnp.float32) * scale
        past = jnp.arange(end)[None, :] < jnp.arange(start, end)[:, None]
        log_beta = jax.nn.log_sigmoid(z)
        log_1m = jnp.where(past, jax.nn.log_sigmoid(-z), 0.0)
        acc = lax.cumsum(log_1m, axis=3, reverse=True) - log_1m
        w = jnp.where(past, jnp.exp(log_beta + acc), 0.0)
        outs.append(jnp.einsum('bhqk,bhkd->bhqd', w.astype(v.dtype), v[:, :, :end]))
    return jnp.concatenate(outs, axis=2)

def differential_attention(q, k, v, lam):
    S = q.shape[3]
    scale = HEAD_DIM ** -0.5
    outs = []
    for start in range(0, S, Q_BLOCK):
        end = start + Q_BLOCK
        s = jnp.einsum('bhcqd,bhckd->bhcqk', q[:, :, :, start:end], k[:, :, :, :end]).astype(jnp.float32) * scale
        causal = jnp.arange(end)[None, :] <= jnp.arange(start, end)[:, None]
        p = jax.nn.softmax(jnp.where(causal, s, -jnp.inf), axis=-1)
        a = p[:, :, 0] - lam * p[:, :, 1]
        outs.append(jnp.einsum('bhqk,bhkd->bhqd', a.astype(v.dtype), v[:, :, :end]))
    return jnp.concatenate(outs, axis=2)

def first_inputs(seed: int = 0) -> dict:
    key = jax.random.key(seed)
    ks = jax.random.split(key, 16)
    f32 = jnp.float32
    nrm = lambda k, shape, s: jax.random.normal(k, shape, f32) * s
    return {
        "x": nrm(ks[0], (BATCH, SEQ, D_MODEL), 1.0),
        "attn_norm_g": 1.0 + nrm(ks[1], (DEPTH, D_MODEL), 0.02),
        "w_in": nrm(ks[2], (DEPTH, D_MODEL, IN_WIDTH), D_MODEL ** -0.5),
        "diff_q_norm_g": 1.0 + nrm(ks[3], (DEPTH, HEAD_DIM), 0.02),
        "diff_k_norm_g": 1.0 + nrm(ks[4], (DEPTH, HEAD_DIM), 0.02),
        "lambda_q1": nrm(ks[5], (DEPTH, HEAD_DIM), 0.1),
        "lambda_k1": nrm(ks[6], (DEPTH, HEAD_DIM), 0.1),
        "lambda_q2": nrm(ks[7], (DEPTH, HEAD_DIM), 0.1),
        "lambda_k2": nrm(ks[8], (DEPTH, HEAD_DIM), 0.1),
        "diff_subln_g": 1.0 + nrm(ks[9], (DEPTH, 2 * HEAD_DIM), 0.02),
        "w_o": nrm(ks[10], (DEPTH, MIX_WIDTH, D_MODEL), MIX_WIDTH ** -0.5),
        "ffn_norm_g": 1.0 + nrm(ks[11], (DEPTH, D_MODEL), 0.02),
        "w_gate": nrm(ks[12], (DEPTH, D_MODEL, D_FF), D_MODEL ** -0.5),
        "w_up": nrm(ks[13], (DEPTH, D_MODEL, D_FF), D_MODEL ** -0.5),
        "w_down": nrm(ks[14], (DEPTH, D_FF, D_MODEL), D_FF ** -0.5),
    }

def first_block(x, attn_norm_g, w_in, diff_q_norm_g, diff_k_norm_g, lambda_q1, lambda_k1,
              lambda_q2, lambda_k2, diff_subln_g, w_o, ffn_norm_g, w_gate, w_up, w_down):
    B, S, _ = x.shape
    pos = jnp.arange(S, dtype=jnp.int32)
    for layer in range(DEPTH):
        lambda_init = 0.8 - 0.6 * math.exp(-0.3 * layer)
        h = rmsnorm(x, attn_norm_g[layer])
        proj = h @ w_in[layer]
        sb_q, sb_k, sb_v, d_q, d_k, d_v = jnp.split(
            proj, [SB_WIDTH, 2 * SB_WIDTH, 3 * SB_WIDTH,
                   3 * SB_WIDTH + DIFF_WIDTH, 3 * SB_WIDTH + 2 * DIFF_WIDTH], axis=-1)

        to_heads = lambda t: t.reshape(B, S, SB_HEADS, HEAD_DIM).transpose(0, 2, 1, 3)
        sb_out = stick_breaking_attention(to_heads(sb_q), to_heads(sb_k), to_heads(sb_v))
        sb_out = sb_out.transpose(0, 2, 1, 3).reshape(B, S, SB_WIDTH)

        to_pair = lambda t: t.reshape(B, S, DIFF_HEADS, 2, HEAD_DIM).transpose(0, 2, 3, 1, 4)
        dq = rope(rmsnorm(to_pair(d_q), diff_q_norm_g[layer]), pos)
        dk = rope(rmsnorm(to_pair(d_k), diff_k_norm_g[layer]), pos)
        dv = d_v.reshape(B, S, DIFF_HEADS, 2 * HEAD_DIM).transpose(0, 2, 1, 3)
        lam = (jnp.exp(jnp.sum(lambda_q1[layer].astype(jnp.float32) * lambda_k1[layer].astype(jnp.float32)))
               - jnp.exp(jnp.sum(lambda_q2[layer].astype(jnp.float32) * lambda_k2[layer].astype(jnp.float32)))
               + lambda_init)
        d_out = differential_attention(dq, dk, dv, lam)
        d_out = rmsnorm(d_out, diff_subln_g[layer], SUBLN_EPS) * (1.0 - lambda_init)
        d_out = d_out.transpose(0, 2, 1, 3).reshape(B, S, DIFF_WIDTH)

        mix = jnp.concatenate([sb_out, d_out.astype(sb_out.dtype)], axis=-1)
        x = x + mix @ w_o[layer]

        h2 = rmsnorm(x, ffn_norm_g[layer])
        x = x + (jax.nn.silu(h2 @ w_gate[layer]) * (h2 @ w_up[layer])) @ w_down[layer]
    return x


DEPTH_2 = 2

N_Q_HEADS = 8
N_KV_HEADS = 2
Q_PER_KV = N_Q_HEADS // N_KV_HEADS
WINDOW = 128
ATTN_BLOCK = 128
ATTN_Q_WIDTH = N_Q_HEADS * HEAD_DIM
ATTN_KV_WIDTH = N_KV_HEADS * HEAD_DIM
N_RET_HEADS = 8
RET_KEY_DIM = 32
RET_VAL_DIM = 64
RET_CHUNK = 128
RET_QK_WIDTH = N_RET_HEADS * RET_KEY_DIM
RET_V_WIDTH = N_RET_HEADS * RET_VAL_DIM
D_FF_DENSE = 2816
N_EXPERTS = 8
TOP_K = 2
D_FF_EXPERT = 1408
N_DENSE_LAYERS = (DEPTH_2 + 1) // 2
N_MOE_LAYERS = DEPTH_2 // 2
IN_SIZES = (ATTN_Q_WIDTH, ATTN_KV_WIDTH, ATTN_KV_WIDTH,
            RET_QK_WIDTH, RET_QK_WIDTH, RET_V_WIDTH, RET_V_WIDTH, RET_V_WIDTH,
            2 * D_MODEL)
IN_WIDTH_2 = sum(IN_SIZES)
DEEPNORM_ALPHA = (2 * DEPTH_2) ** 0.25
DEEPNORM_BETA = (8 * DEPTH_2) ** -0.25
LN_EPS = 1e-5
GN_EPS = 1e-5
NEG_INF = -1e30


def layer_norm(x, g, b):
    xf = x.astype(jnp.float32)
    mu = jnp.mean(xf, axis=-1, keepdims=True)
    var = jnp.mean(jnp.square(xf - mu), axis=-1, keepdims=True)
    return ((xf - mu) * lax.rsqrt(var + LN_EPS)).astype(x.dtype) * g + b

def split_columns(proj, sizes):
    parts, start = [], 0
    for size in sizes:
        parts.append(proj[..., start:start + size])
        start += size
    return parts

def alibi_slopes(n_heads):
    return jnp.exp2(-8.0 * jnp.arange(1, n_heads + 1, dtype=jnp.float32) / n_heads)

def windowed_gqa(q, k, v, sink_logits):
    B, S, _ = q.shape
    C = ATTN_BLOCK
    nb = S // C
    qb = q.reshape(B, nb, C, N_KV_HEADS, Q_PER_KV, HEAD_DIM)
    pad = ((0, 0), (C, C), (0, 0))
    kp = jnp.pad(k, pad).reshape(B, nb + 2, C, N_KV_HEADS, HEAD_DIM)
    vp = jnp.pad(v, pad).reshape(B, nb + 2, C, N_KV_HEADS, HEAD_DIM)
    kw = jnp.concatenate([kp[:, :-2], kp[:, 1:-1], kp[:, 2:]], axis=2)
    vw = jnp.concatenate([vp[:, :-2], vp[:, 1:-1], vp[:, 2:]], axis=2)
    scores = jnp.einsum('bnqgrd,bnkgd->bngrqk', qb, kw,
                        preferred_element_type=jnp.float32) * (HEAD_DIM ** -0.5)
    qi = jnp.arange(C)
    kj = jnp.arange(3 * C)
    dist = jnp.abs(qi[:, None] - kj[None, :] + C)
    key_pos = (jnp.arange(nb)[:, None] - 1) * C + kj[None, :]
    valid = (dist <= WINDOW)[None] & ((key_pos >= 0) & (key_pos < S))[:, None, :]
    slopes = alibi_slopes(N_Q_HEADS).reshape(N_KV_HEADS, Q_PER_KV)
    scores = scores - slopes[:, :, None, None] * dist.astype(jnp.float32)
    scores = jnp.where(valid[None, :, None, None], scores, NEG_INF)
    sink = jnp.broadcast_to(
        sink_logits.astype(jnp.float32).reshape(N_KV_HEADS, Q_PER_KV)[:, :, None, None],
        scores.shape[:-1] + (1,))
    probs = jax.nn.softmax(jnp.concatenate([scores, sink], axis=-1), axis=-1)[..., :-1]
    out = jnp.einsum('bngrqk,bnkgd->bnqgrd', probs.astype(v.dtype), vw)
    return out.reshape(B, S, ATTN_Q_WIDTH)

def head_group_norm(y):
    mu = jnp.mean(y, axis=-1, keepdims=True)
    var = jnp.mean(jnp.square(y - mu), axis=-1, keepdims=True)
    return (y - mu) * lax.rsqrt(var + GN_EPS)

def retention_one_direction(q, k, v, log_gamma, include_diag):
    B, S, H, dk = q.shape
    dv = v.shape[-1]
    C = RET_CHUNK
    nc = S // C
    qc = q.reshape(B, nc, C, H, dk)
    kc = k.reshape(B, nc, C, H, dk)
    vc = v.reshape(B, nc, C, H, dv)
    pos_i = jnp.arange(C)
    diff_i = pos_i[:, None] - pos_i[None, :]
    mask = (diff_i >= 0) if include_diag else (diff_i > 0)
    pos = pos_i.astype(jnp.float32)
    diff = jnp.maximum(diff_i, 0).astype(jnp.float32)
    intra_decay = jnp.where(mask[None], jnp.exp(diff[None] * log_gamma[:, None, None]), 0.0)
    q_decay = jnp.exp((pos + 1.0)[None] * log_gamma[:, None])
    k_decay = jnp.exp((C - 1.0 - pos)[None] * log_gamma[:, None])
    chunk_decay = jnp.exp(C * log_gamma)
    qk = jnp.einsum('bnqhd,bnkhd->bnhqk', qc, kc) * intra_decay
    intra = jnp.einsum('bnhqk,bnkhe->bnqhe', qk, vc)
    chunk_kv = jnp.einsum('bnkhd,hk,bnkhe->bnhde', kc, k_decay, vc)

    def step(state, kv):
        return chunk_decay[None, :, None, None] * state + kv, state

    init = jnp.zeros((B, H, dk, dv), jnp.float32)
    _, prev = lax.scan(step, init, jnp.moveaxis(chunk_kv, 1, 0))
    prev = jnp.moveaxis(prev, 0, 1)
    cross = jnp.einsum('bnqhd,bnhde,hq->bnqhe', qc, prev, q_decay)
    return (intra + cross).reshape(B, S, H, dv)

def bidirectional_retention(q, k, v, g_f, g_b, decay_fwd, decay_bwd):
    B, S, _ = q.shape
    qh = q.reshape(B, S, N_RET_HEADS, RET_KEY_DIM).astype(jnp.float32)
    kh = k.reshape(B, S, N_RET_HEADS, RET_KEY_DIM).astype(jnp.float32) * (RET_KEY_DIM ** -0.5)
    vh = v.reshape(B, S, N_RET_HEADS, RET_VAL_DIM).astype(jnp.float32)
    lg_f = jax.nn.log_sigmoid(decay_fwd.astype(jnp.float32))
    lg_b = jax.nn.log_sigmoid(decay_bwd.astype(jnp.float32))
    y_f = retention_one_direction(qh, kh, vh, lg_f, True)
    y_b = jnp.flip(retention_one_direction(jnp.flip(qh, 1), jnp.flip(kh, 1), jnp.flip(vh, 1),
                                           lg_b, False), axis=1)
    n_f = head_group_norm(y_f).reshape(B, S, RET_V_WIDTH).astype(g_f.dtype)
    n_b = head_group_norm(y_b).reshape(B, S, RET_V_WIDTH).astype(g_b.dtype)
    return jax.nn.silu(g_f) * n_f + jax.nn.silu(g_b) * n_b

def hybrid_mixer(h, w_in, b_gate, sink_logits, decay_fwd, decay_bwd, w_o_attn, w_o_ret, w_out):
    q_a, k_a, v_a, q_r, k_r, v_r, g_f, g_b, gate_logits = split_columns(h @ w_in, IN_SIZES)
    y_attn = windowed_gqa(q_a, k_a, v_a, sink_logits) @ w_o_attn
    y_ret = bidirectional_retention(q_r, k_r, v_r, g_f, g_b, decay_fwd, decay_bwd) @ w_o_ret
    gates = jax.nn.sigmoid(gate_logits + b_gate)
    merged = gates[..., :D_MODEL] * y_attn + gates[..., D_MODEL:] * y_ret
    return merged @ w_out

def swiglu(x, w1, w3, w2):
    return (jax.nn.silu(x @ w1) * (x @ w3)) @ w2

def moe_swiglu(x, router_w, router_b, w1, w3, w2):
    logits = (x @ router_w).astype(jnp.float32) + router_b.astype(jnp.float32)
    top_vals, top_idx = lax.top_k(logits, TOP_K)
    top_w = jax.nn.softmax(top_vals, axis=-1)
    gate = jnp.sum(jax.nn.one_hot(top_idx, N_EXPERTS, dtype=jnp.float32) * top_w[..., None], axis=-2)
    gate = gate.astype(x.dtype)
    out = jnp.zeros_like(x)
    for e in range(N_EXPERTS):
        out = out + gate[..., e:e + 1] * swiglu(x, w1[e], w3[e], w2[e])
    return out

def second_inputs(seed: int = 0) -> dict:
    key = jax.random.key(seed)
    ks = jax.random.split(key, 24)
    f32 = jnp.float32
    beta = DEEPNORM_BETA

    def normal(k, shape, scale):
        return jax.random.normal(k, shape, f32) * scale

    col_mult = (1.0, 1.0, beta, 1.0, 1.0, beta, 1.0, 1.0, 1.0)
    col_scale = jnp.concatenate([jnp.full((s,), c, f32) for s, c in zip(IN_SIZES, col_mult)])
    base_gamma = 1.0 - jnp.exp2(-5.0 - jnp.arange(N_RET_HEADS, dtype=f32))
    base_logit = jnp.log(base_gamma) - jnp.log1p(-base_gamma)
    return {
        'x': normal(ks[0], (BATCH, SEQ, D_MODEL), 1.0),
        'ln_emb_g': 1.0 + normal(ks[1], (D_MODEL,), 0.02),
        'ln_emb_b': normal(ks[2], (D_MODEL,), 0.02),
        'w_in': normal(ks[3], (DEPTH_2, D_MODEL, IN_WIDTH_2), D_MODEL ** -0.5) * col_scale,
        'b_gate': normal(ks[4], (DEPTH_2, 2 * D_MODEL), 0.02),
        'sink_logits': normal(ks[5], (DEPTH_2, N_Q_HEADS), 0.5),
        'decay_fwd': base_logit + normal(ks[6], (DEPTH_2, N_RET_HEADS), 0.1),
        'decay_bwd': base_logit + normal(ks[7], (DEPTH_2, N_RET_HEADS), 0.1),
        'w_o_attn': normal(ks[8], (DEPTH_2, ATTN_Q_WIDTH, D_MODEL), beta * ATTN_Q_WIDTH ** -0.5),
        'w_o_ret': normal(ks[9], (DEPTH_2, RET_V_WIDTH, D_MODEL), beta * RET_V_WIDTH ** -0.5),
        'w_out': normal(ks[10], (DEPTH_2, D_MODEL, D_MODEL), beta * D_MODEL ** -0.5),
        'ln1_g': 1.0 + normal(ks[11], (DEPTH_2, D_MODEL), 0.02),
        'ln1_b': normal(ks[12], (DEPTH_2, D_MODEL), 0.02),
        'ffn_w1': normal(ks[13], (N_DENSE_LAYERS, D_MODEL, D_FF_DENSE), beta * D_MODEL ** -0.5),
        'ffn_w3': normal(ks[14], (N_DENSE_LAYERS, D_MODEL, D_FF_DENSE), beta * D_MODEL ** -0.5),
        'ffn_w2': normal(ks[15], (N_DENSE_LAYERS, D_FF_DENSE, D_MODEL), beta * D_FF_DENSE ** -0.5),
        'router_w': normal(ks[16], (N_MOE_LAYERS, D_MODEL, N_EXPERTS), D_MODEL ** -0.5),
        'router_b': normal(ks[17], (N_MOE_LAYERS, N_EXPERTS), 0.01),
        'moe_w1': normal(ks[18], (N_MOE_LAYERS, N_EXPERTS, D_MODEL, D_FF_EXPERT), beta * D_MODEL ** -0.5),
        'moe_w3': normal(ks[19], (N_MOE_LAYERS, N_EXPERTS, D_MODEL, D_FF_EXPERT), beta * D_MODEL ** -0.5),
        'moe_w2': normal(ks[20], (N_MOE_LAYERS, N_EXPERTS, D_FF_EXPERT, D_MODEL), beta * D_FF_EXPERT ** -0.5),
        'ln2_g': 1.0 + normal(ks[21], (DEPTH_2, D_MODEL), 0.02),
        'ln2_b': normal(ks[22], (DEPTH_2, D_MODEL), 0.02),
    }

def second_block(x, ln_emb_g, ln_emb_b, w_in, b_gate, sink_logits, decay_fwd, decay_bwd,
              w_o_attn, w_o_ret, w_out, ln1_g, ln1_b, ffn_w1, ffn_w3, ffn_w2,
              router_w, router_b, moe_w1, moe_w3, moe_w2, ln2_g, ln2_b):
    x = layer_norm(x, ln_emb_g, ln_emb_b)
    for layer in range(DEPTH_2):
        mix = hybrid_mixer(x, w_in[layer], b_gate[layer], sink_logits[layer],
                           decay_fwd[layer], decay_bwd[layer],
                           w_o_attn[layer], w_o_ret[layer], w_out[layer])
        x = layer_norm(DEEPNORM_ALPHA * x + mix, ln1_g[layer], ln1_b[layer])
        i = layer // 2
        if layer % 2 == 0:
            ffn = swiglu(x, ffn_w1[i], ffn_w3[i], ffn_w2[i])
        else:
            ffn = moe_swiglu(x, router_w[i], router_b[i], moe_w1[i], moe_w3[i], moe_w2[i])
        x = layer_norm(DEEPNORM_ALPHA * x + ffn, ln2_g[layer], ln2_b[layer])
    return x


def setup_inputs(seed=0):
    out = dict(first_inputs(seed))
    for name, value in second_inputs(seed + 1).items():
        if name != "x":
            out[name + "_2"] = value
    return out


def reference(
    x, attn_norm_g, w_in, diff_q_norm_g, diff_k_norm_g, lambda_q1, lambda_k1, lambda_q2,
    lambda_k2, diff_subln_g, w_o, ffn_norm_g, w_gate, w_up, w_down, ln_emb_g_2, ln_emb_b_2,
    w_in_2, b_gate_2, sink_logits_2, decay_fwd_2, decay_bwd_2, w_o_attn_2, w_o_ret_2, w_out_2,
    ln1_g_2, ln1_b_2, ffn_w1_2, ffn_w3_2, ffn_w2_2, router_w_2, router_b_2, moe_w1_2, moe_w3_2,
    moe_w2_2, ln2_g_2, ln2_b_2,
):
    x = first_block(
        x, attn_norm_g, w_in, diff_q_norm_g, diff_k_norm_g, lambda_q1, lambda_k1, lambda_q2,
        lambda_k2, diff_subln_g, w_o, ffn_norm_g, w_gate, w_up, w_down,
    )
    return second_block(
        x, ln_emb_g_2, ln_emb_b_2, w_in_2, b_gate_2, sink_logits_2, decay_fwd_2, decay_bwd_2,
        w_o_attn_2, w_o_ret_2, w_out_2, ln1_g_2, ln1_b_2, ffn_w1_2, ffn_w3_2, ffn_w2_2,
        router_w_2, router_b_2, moe_w1_2, moe_w3_2, moe_w2_2, ln2_g_2, ln2_b_2,
    )


_drawn_inputs = setup_inputs


def setup_inputs(seed=0):
    import zlib

    import numpy as np

    out = dict(_drawn_inputs(seed))
    spreads = {}
    factors = {'diff_q_norm_g': 4.317,
     'diff_k_norm_g': 5.42,
     'lambda_q1': 55.884,
     'lambda_k2': 2.822,
     'diff_subln_g': 4.792,
     'ffn_norm_g': 4.291,
     'ln_emb_g_2': 2.692,
     'ln_emb_b_2': 2.697,
     'b_gate_2': 52.355,
     'sink_logits_2': 61.75,
     'decay_fwd_2': 21.896,
     'decay_bwd_2': 22.016,
     'w_o_attn_2': 2.729,
     'router_b_2': 52.558}
    for name, (base, spread) in spreads.items():
        noise = np.random.default_rng([zlib.crc32(name.encode()), seed]).standard_normal(out[name].shape)
        drawn = base * np.exp(spread * noise) if base else spread * noise
        out[name] = jnp.asarray(drawn.astype(out[name].dtype))
    for name, factor in factors.items():
        out[name] = (out[name] * factor).astype(out[name].dtype)
    return out
```

```python
import math
from contextlib import ExitStack

import numpy as np

import concourse.bass as bass
from concourse import mybir

F32 = mybir.dt.float32
F32R = mybir.dt.float32r
U32 = mybir.dt.uint32
ALU = mybir.AluOpType
ACT = mybir.ActivationFunctionType
AX = mybir.AxisListType

P = 128
T = 256
TT = T // P
D = 1024
KT = D // P
F_DENSE = 2816
F_EXPERT = 1408
EXPERTS = 8
FT_DENSE = F_DENSE // P
FT_EXPERT = F_EXPERT // P
RING = 3
UNIT = 2048
BIG = 1.0e30
SCALE = 64 ** -0.5
RMS_EPS, SUBLN_EPS, LN_EPS = 1e-6, 1e-5, 1e-5
LAMBDA_INIT = 0.8 - 0.6 * math.exp(-0.3 * 0)
ALPHA = 4 ** 0.25
SLOPES = [2.0 ** (-8.0 * (h + 1) / 8) for h in range(8)]

U_IN1, U_WO = 0, 12
U_FFN1 = U_WO + 4
U_MIX = [U_FFN1 + 33, U_FFN1 + 33 + 27 + 33]
U_FFN2 = U_MIX[0] + 27
U_MOE = U_MIX[1] + 27
U_END = U_MOE + 3 * 44
Q_FFN1 = 16
Q_MIX = [Q_FFN1 + 22, Q_FFN1 + 22 + 27 + 22]
Q_FFN2 = Q_MIX[0] + 27
Q_MOE = Q_MIX[1] + 27
H_FFN1, H_FFN2, H_MOE = 0, 22, 44

IN1 = [("q", 0), ("k", 512), ("q", 256), ("k", 768), ("v", 1024), ("v", 1280),
       ("dq", 1536), ("dq", 1792), ("dk", 2048), ("dk", 2304), ("dv", 2560), ("dv", 2816)]
ORDER1 = [("unit", 0), ("unit", 1), ("sb_z", 0), ("unit", 2), ("unit", 3), ("unit", 4), ("sb_cum", 0),
          ("unit", 5), ("unit", 6), ("sb_pv", 0), ("sb_z", 1), ("unit", 7), ("rot", 0), ("sb_cum", 1),
          ("unit", 8), ("unit", 9), ("sb_pv", 1), ("rot", 1), ("unit", 10), ("unit", 11),
          ("d_t", 0), ("d_s", 0), ("d_x", 0), ("d_s", 1), ("d_pv", 0), ("d_x", 1),
          ("d_pv", 1), ("d_norm", 0), ("wo", 0), ("wo", 1), ("wo", 2), ("wo", 3)]
ORDER2 = [("unit", 0), ("unit", 1), ("unit", 2), ("gqa_s", 0), ("unit", 3), ("unit", 4),
          ("gqa_t", 0), ("unit", 5), ("unit", 6), ("gqa_s", 1), ("gqa_pv", 0), ("unit", 7), ("unit", 8),
          ("gqa_t", 1), ("unit", 9), ("unit", 10), ("gqa_pv", 1), ("gqa_out", 0), ("decay", 0)]
for _h in range(8):
    ORDER2 += [("ret_s", _h), ("unit", 11 + _h)]
    if _h:
        ORDER2 += [("ret_pv", _h - 1)]
ORDER2 += [("ret_pv", 7), ("ya", 0), ("ya", 1), ("ret_norm", 0), ("yr", 0), ("yr", 1), ("merge", 0),
           ("out", 0), ("out", 1), ("out", 2), ("out", 3)]

CONSTS = {}


def constants():
    p = np.arange(P, dtype=np.float32)[:, None]
    c = np.arange(P, dtype=np.float32)[None, :]
    i = np.arange(T, dtype=np.float32)[None, :]
    parts = {
        "ident": (p == c),
        "later": (p > c),
        "ones": np.ones((P, P)),
        "past": (p < c),
        "causal": np.where(c <= p, 0.0, -BIG),
    }
    inv = (np.float32(10000.0) ** (-np.arange(32, dtype=np.float32) / np.float32(32))).astype(np.float32)
    ang = (np.arange(T, dtype=np.float32)[:, None] * inv[None, :]).astype(np.float32)
    cos, sin = np.cos(ang), np.sin(ang)
    rows = lambda a: a.reshape(TT, P, 64).transpose(1, 0, 2).reshape(P, TT * 64)
    parts["cos"] = rows(np.concatenate([cos, cos], 1))
    parts["sin"] = rows(np.concatenate([-sin, sin], 1))
    dist = [np.where(np.abs(t * P + p - i) <= 128, np.abs(t * P + p - i), BIG) for t in range(TT)]
    parts["dist"] = np.concatenate(dist, 1)
    parts["ahead"] = np.concatenate([np.maximum(i - p, 0), np.maximum(P + p - i, 0)], 1)
    parts["ahead_on"] = np.concatenate([i >= p, i < P + p], 1)
    parts["expert"] = np.broadcast_to(np.arange(8, dtype=np.float32)[None, :], (P, 8))
    at = 0
    for name, a in parts.items():
        CONSTS[name] = (at, a.shape[1])
        at += a.shape[1]
    return np.ascontiguousarray(np.concatenate([np.asarray(a, np.float32) for a in parts.values()], 1))


CONST_TABLE = constants()


def two_blocks(nc, A, const_dram, out):
    with ExitStack() as ctx:
        def sb(name, shape, dt=F32):
            return ctx.enter_context(nc.sbuf_tensor(name, shape, dt))

        def sem(name):
            return ctx.enter_context(nc.semaphore(name))

        raw = sb("raw", [P, RING, UNIT])
        w_hi = sb("w_hi", [P, RING, UNIT], F32R)
        w_lo = sb("w_lo", [P, RING, UNIT], F32R)
        xt_hi = sb("xt_hi", [P, KT, T], F32R)
        xt_lo = sb("xt_lo", [P, KT, T], F32R)
        mt_hi = sb("mt_hi", [P, KT, T], F32R)
        mt_lo = sb("mt_lo", [P, KT, T], F32R)
        h_hi_t = sb("h_hi_t", [P, 2, T], F32R)
        h_lo_t = sb("h_lo_t", [P, 2, T], F32R)
        zeros = sb("zeros", [P, 512], F32R)
        x = sb("x", [P, TT, D])
        gb = sb("gb", [P, 2, D])
        const = sb("const", list(CONST_TABLE.shape))
        small = sb("small", [P, 768])
        scr = sb("scr", [P, 16896])
        ps = ctx.enter_context(nc.psum_tensor("ps", [P, 8, 512], F32))

        def table(name):
            at, n = CONSTS[name]
            return const[:, at:at + n]

        ident, later, ones, past, causal = (table(n) for n in ("ident", "later", "ones", "past", "causal"))

        def area(at, *dims):
            n = int(np.prod(dims))
            v = scr[:, at:at + n]
            if len(dims) == 1:
                return v
            names = "abcd"[:len(dims)]
            return v.rearrange(f"p ({' '.join(names)}) -> p {' '.join(names)}",
                               **{names[i]: d for i, d in enumerate(dims)})

        def tiny(at, n):
            return small[:, at:at + n]

        qT, kT, v_sb = area(0, 4, T), area(1024, 4, T), area(2048, TT, 512)
        dqk = [area(3072, TT, 8, 64), area(4096, TT, 8, 64)]
        dv = area(5120, TT, 512)
        dqkT = [area(6144, 4, T), area(7168, 4, T)]
        s_a, s_b, s_c = area(8192, 4, 384), area(9728, 4, 384), area(11264, 4, 384)
        rt = area(12800, TT, 8, 64)
        d_out = area(13824, TT, 4, P)
        normed = area(14848, TT, D)
        silu_t, hid = area(4096, 2, T), area(4608, 2, T)
        gate_all = area(0, EXPERTS, T)
        gate_cols = area(2048, TT * EXPERTS, P)
        qaT, kaT, va = area(0, 4, T), area(1024, 2, T), area(1536, TT, P)
        qrT, krT, vr = area(1792, 2, T), area(2304, 2, T), area(2816, TT, 512)
        sg = area(3840, 2, TT, 512)
        gates = area(5888, TT, 2048)
        decay = area(9984, 8, 2, T)
        b_rows = area(14080, 2, T)
        g_s, g_t = area(14592, 4, TT, T), area(9984, 4, TT, T)
        r_w = area(14592, 2, 2, 384)
        y_sq = area(14592, TT, 8, 64)
        y_n = area(15616, TT, 8, 64)
        attn = area(12032, TT, 512)
        y_mix = area(9984, 2, TT, D)
        merged = area(0, TT, D)

        stats = tiny(0, 24).rearrange("p (t c s) -> p t c s", t=TT, c=2)
        mv = tiny(24, 4).rearrange("p (t s) -> p t s", t=TT)
        ms = tiny(28, 2)
        rstd = tiny(30, 2)
        ss = tiny(32, 32)
        rs = tiny(64, 32)
        lam4 = tiny(96, 256).rearrange("p (v e) -> p v e", v=4)
        lam2 = tiny(352, 2)
        lam = tiny(354, 1)
        mx, nm, sums, rec = tiny(356, 8), tiny(364, 8), tiny(372, 8), tiny(380, 8)
        rec_all = tiny(388, 16)
        sink = tiny(404, 8)
        lg = tiny(412, 16)
        lg_t = tiny(428, 48).rearrange("p (a n) -> p a n", a=3)
        gq = tiny(476, 128).rearrange("p (a n) -> p a n", a=2)
        gsub = tiny(604, 128)
        top8 = tiny(96, 16).rearrange("p (t n) -> p t n", t=TT)
        logit = tiny(112, 16).rearrange("p (t n) -> p t n", t=TT)
        tw = tiny(128, 8).rearrange("p (t n) -> p t n", t=TT)
        idx_f = tiny(136, 16).rearrange("p (t n) -> p t n", t=TT)
        gate8 = tiny(152, 32).rearrange("p (a t n) -> p a t n", a=2, t=TT)
        idx_u = sb("idx_u", [P, TT, 8], U32)
        rw_hi = sb("rw_hi", [P, KT * 8], F32R)
        rw_lo = sb("rw_lo", [P, KT * 8], F32R)
        rw_raw = sb("rw_raw", [P, KT * 8])
        rb = tiny(184, 8)

        raw_landed = [sem(f"raw_landed{i}") for i in range(RING)]
        hi_ready, lo_ready, unit_used = sem("hi_ready"), sem("lo_ready"), sem("unit_used")
        evacuated = [sem("evacuated0"), sem("evacuated1")]
        silu_ready, hid_ready, hid_hi, hid_scaled = sem("silu_ready"), sem("hid_ready"), sem("hid_hi"), sem("hid_scaled")
        acc_done, acc_taken = sem("acc_done"), sem("acc_taken")
        act_step, dve_step, pool_step = sem("act_step"), sem("dve_step"), sem("pool_step")
        x_landed, consts_landed, small1_landed = sem("x_landed"), sem("consts_landed"), sem("small1_landed")
        gb_landed, gb_used = sem("gb_landed"), sem("gb_used")
        var_ready, rstd_ready = sem("var_ready"), sem("rstd_ready")
        rows_ready, rows_turned, xt_hi_ready, xt_ready = sem("rows_ready"), sem("rows_turned"), sem("xt_hi_ready"), sem("xt_ready")
        zeroed = sem("zeroed")
        stored = sem("stored")
        S = {}

        def ev(name):
            if name not in S:
                S[name] = sem(name)
            return S[name]

        block = ctx.enter_context(nc.Block())

        class Chain:
            def __init__(self, engine, step):
                self.engine, self.step, self.n = engine, step, 0

            def __call__(self, ins):
                self.n += 1
                ins.then_inc(self.step, 1)
                self.engine.wait_ge(self.step, self.n)

        def wait_evacuated(eng, q):
            eng.wait_ge(evacuated[q % 2], q // 2 + 1)

        def k_major(w):
            return w.rearrange("(k p) n -> p k n", p=P)

        @block.sync
        def _(sp):
            sp.dma_start(x[:, :, :], A["x"][0].rearrange("(t p) d -> p t d", p=P)).then_inc(x_landed, 16)

            def load(u, slot, first, second):
                if not (isinstance(u, int) and u < RING):
                    sp.wait_ge(lo_ready, u - RING + 1)
                for half, src in ((0, first), (1, second)):
                    dst = raw[:, slot, half * 1024:(half + 1) * 1024]
                    if len(src.shape) == 3:
                        dst = dst.rearrange("p (k n) -> p k n", k=src.shape[1])
                    elif len(src.shape) == 4:
                        dst = dst.rearrange("p (e k n) -> p e k n", e=src.shape[1], k=src.shape[2])
                    sp.dma_start(dst, src).then_inc(raw_landed[slot], 16)

            def load_square(u, w, c):
                v = k_major(w)
                load(u, u % RING, v[:, 0:4, c:c + 256], v[:, 4:8, c:c + 256])

            def load_short(u, w, c):
                v = k_major(w)
                load(u, u % RING, v[:, 0:2, c:c + 512], v[:, 2:4, c:c + 512])

            def load_ffn(u0, wg, wu, wd):
                gv, uv = k_major(wg), k_major(wu)
                with sp.Fori(0, FT_DENSE // 2) as i:
                    for j in range(2):
                        c = bass.ds(i * 256 + j * P, P)
                        load(u0 + j + i * 3, (u0 + j) % RING, gv[:, :, c], uv[:, :, c])
                    load(u0 + 2 + i * 3, (u0 + 2) % RING, wd[bass.ds(i * 256, P), :], wd[bass.ds(i * 256 + P, P), :])

            for n, (_, c) in enumerate(IN1):
                load_square(U_IN1 + n, A["w_in"][0], c)
            for n in range(4):
                load_square(U_WO + n, A["w_o"][0], n * 256)
            load_ffn(U_FFN1, A["w_gate"][0], A["w_up"][0], A["w_down"][0])
            for l in range(2):
                for n in range(19):
                    load_square(U_MIX[l] + n, A["w_in_2"][l], n * 256)
                for n in range(2):
                    load_short(U_MIX[l] + 19 + n, A["w_o_attn_2"][l], n * 512)
                for n in range(2):
                    load_short(U_MIX[l] + 21 + n, A["w_o_ret_2"][l], n * 512)
                for n in range(4):
                    load_square(U_MIX[l] + 23 + n, A["w_out_2"][l], n * 256)
                if l == 0:
                    load_ffn(U_FFN2, A["ffn_w1_2"][0], A["ffn_w3_2"][0], A["ffn_w2_2"][0])
            w1 = A["moe_w1_2"][0].rearrange("e (k p) n -> p e k n", p=P)
            w3 = A["moe_w3_2"][0].rearrange("e (k p) n -> p e k n", p=P)
            w2 = A["moe_w2_2"][0].rearrange("e f d -> (e f) d")

            def load_moe_pair(u, i, tiles, row):
                for j, (e, c) in enumerate(tiles):
                    at = (slice(None), bass.ds(e, 1), slice(None), bass.ds(c, P))
                    load(u + j, (U_MOE + j) % RING, w1[at], w3[at])
                load(u + 2, (U_MOE + 2) % RING, w2[bass.ds(row, P), :], w2[bass.ds(row + P, P), :])

            with sp.Fori(0, EXPERTS // 2) as g:
                with sp.Fori(0, 5) as i:
                    load_moe_pair(U_MOE + g * 33 + i * 3, i, [(g * 2, i * 256), (g * 2, i * 256 + P)], g * 2816 + i * 256)
                load_moe_pair(U_MOE + 15 + g * 33, None, [(g * 2, 1280), (g * 2 + 1, 0)], g * 2816 + 1280)
                with sp.Fori(0, 5) as i:
                    load_moe_pair(U_MOE + 18 + g * 33 + i * 3, i, [(g * 2 + 1, i * 256 + P), (g * 2 + 1, i * 256 + 2 * P)],
                                  g * 2816 + 1536 + i * 256)
            for t in range(TT):
                sp.wait_ge(rows_ready, 2 * 6 + t + 1)
                sp.dma_start(out[0, t * P:(t + 1) * P, :], x[:, t, :]).then_inc(stored, 16)
            sp.wait_ge(stored, 16 * TT)

        @block.gpsimd
        def _(pool):
            def row(v, n):
                return v.rearrange("(a n) -> a n", a=1).partition_broadcast(P) if len(v.shape) == 1 else v.partition_broadcast(P)

            pool.dma_start(const[:, :], const_dram).then_inc(consts_landed, 16)
            norms = [(A["attn_norm_g"][0], None), (A["ffn_norm_g"][0], None),
                     (A["ln_emb_g_2"], A["ln_emb_b_2"]),
                     (A["ln1_g_2"][0], A["ln1_b_2"][0]), (A["ln2_g_2"][0], A["ln2_b_2"][0]),
                     (A["ln1_g_2"][1], A["ln1_b_2"][1]), (A["ln2_g_2"][1], A["ln2_b_2"][1])]

            def load_norm(n):
                if n:
                    pool.wait_ge(gb_used, n)
                for i, v in enumerate(norms[n]):
                    pool.dma_start(gb[:, i, :], row(v if v is not None else norms[n][0], D)).then_inc(gb_landed, 16)

            pool.memset(zeros[:, :].bitcast(F32), 0.0).then_inc(zeroed, 1)
            load_norm(0)
            for i, name in enumerate(("lambda_q1", "lambda_k1", "lambda_q2", "lambda_k2")):
                pool.dma_start(lam4[:, i, :], row(A[name][0], 64)).then_inc(small1_landed, 16)
            pool.dma_start(gq[:, 0, :], row(A["diff_q_norm_g"][0], 64)).then_inc(small1_landed, 16)
            pool.dma_start(gq[:, 1, :], row(A["diff_k_norm_g"][0], 64)).then_inc(small1_landed, 16)
            pool.dma_start(gsub, row(A["diff_subln_g"][0], P)).then_inc(small1_landed, 16)
            load_norm(1)
            load_norm(2)
            for l in range(2):
                pool.wait_ge(rows_ready, 2 * (2 + 2 * l) + 2)
                pool.dma_start(sink, row(A["sink_logits_2"][l], 8)).then_inc(ev("mix_small"), 16)
                pool.dma_start(lg_t[:, 0, 0:8], row(A["decay_fwd_2"][l], 8)).then_inc(ev("mix_small"), 16)
                pool.dma_start(lg_t[:, 0, 8:16], row(A["decay_bwd_2"][l], 8)).then_inc(ev("mix_small"), 16)
                load_norm(3 + 2 * l)
                for n in range(8):
                    if n >= 2:
                        wait_evacuated(pool, Q_MIX[l] + 11 + n - 2)
                    pool.dma_start(b_rows[:, n % 2, :], row(A["b_gate_2"][l, n * 256:(n + 1) * 256], 256)).then_inc(ev(f"b_row{n % 2}"), 16)
                load_norm(4 + 2 * l)
                if l == 1:
                    pool.dma_start(rw_raw[:, :].rearrange("p (k n) -> p k n", n=8), k_major(A["router_w_2"][0])).then_inc(ev("router_landed"), 16)
                    pool.dma_start(rb, row(A["router_b_2"][0], 8)).then_inc(ev("router_landed"), 16)

        @block.scalar
        def _(act):
            link = Chain(act, act_step)
            A_ = nc.scalar.activation

            def split_hi(u, slot, count):
                act.wait_ge(raw_landed[slot], count * 32)
                if not (isinstance(u, int) and u < RING):
                    act.wait_ge(unit_used, u - RING + 1)
                A_(w_hi[:, slot, :], raw[:, slot, :], ACT.Copy).then_inc(hi_ready, 1)

            def split_next(u):
                if u + RING < U_END:
                    split_hi(u + RING, u % RING, (u + RING) // RING + 1)

            def evac(u, q, dst, src, func=ACT.Copy):
                act.wait_ge(unit_used, u + 1)
                A_(dst, src, func).then_inc(evacuated[q % 2], 1)

            def turn(n, banks, dst, count, name_in, name_out):
                for b in range(banks):
                    act.wait_ge(name_in, count + b + 1)
                    A_(dst[:, 2 * b:2 * b + 2, :], ps[:, 2 + b, :].rearrange("p (k t) -> p k t", k=2), ACT.Copy).then_inc(name_out, 1)

            def norm(n, turned=True):
                act.wait_ge(var_ready, n + 1)
                link(A_(rstd, ms, ACT.Ln))
                A_(rstd, rstd, ACT.Exp, scale=-0.5).then_inc(rstd_ready, 1)
                if turned:
                    turn(n, 4, xt_hi, 4 * n, rows_turned, xt_hi_ready)

            def inv_sqrt(n, src, dst):
                act.wait_ge(ev("group_var"), n + 1)
                link(A_(dst, src, ACT.Ln))
                A_(dst, dst, ACT.Exp, scale=-0.5).then_inc(ev("group_rstd"), 1)

            for u in range(RING):
                split_hi(u, u, 1)
            act.wait_ge(consts_landed, 16)
            norm(0)

            def unit1(n):
                q, kind = n, IN1[n][0]
                src = ps[:, q % 2, :]
                two = src.rearrange("p (t c) -> p t c", t=2)
                second = IN1[n][1] % 512 // 256
                dst = {"q": qT[:, 2 * second:2 * second + 2, :], "k": kT[:, 2 * second:2 * second + 2, :],
                       "v": v_sb[:, :, 256 * second:256 * second + 256],
                       "dq": dqk[0].rearrange("p t h e -> p t (h e)")[:, :, 256 * second:256 * second + 256],
                       "dk": dqk[1].rearrange("p t h e -> p t (h e)")[:, :, 256 * second:256 * second + 256],
                       "dv": dv[:, :, 256 * second:256 * second + 256]}[kind]
                evac(U_IN1 + n, q, dst, two)
                split_next(U_IN1 + n)

            def sb_z(g):
                act.wait_ge(ev("sb_z"), g + 1)
                if g:
                    act.wait_ge(ev("sb_pv"), g)
                link(A_(s_c, ps[:, 2:6, 0:384], ACT.Abs, scale=SCALE))
                link(A_(s_c, s_c, ACT.Exp, scale=-1.0))
                A_(s_c, s_c, ACT.Ln, bias=1.0).then_inc(ev("sb_ln"), 1)

            def sb_cum(g):
                act.wait_ge(ev("sb_sum"), g + 1)
                A_(s_c, s_a, ACT.Exp).then_inc(ev("sb_exp"), 1)

            def sb_pv(g):
                act.wait_ge(ev("sb_pv"), g + 1)
                A_(mt_hi[:, 2 * g:2 * g + 2, :], ps[:, 6 + g, :].rearrange("p (k t) -> p k t", k=2), ACT.Copy).then_inc(ev("sb_mt_hi"), 1)

            def rot(i):
                inv_sqrt(i, ss[:, 0:16], rs[:, 0:16])

            def d_t(_):
                for i in range(2):
                    act.wait_ge(ev("d_turned"), i + 1)
                    A_(dqkT[i], ps[:, 2 + 2 * i:4 + 2 * i, :].rearrange("p b (k t) -> p (b k) t", k=2), ACT.Copy).then_inc(ev("d_copied"), 1)

            def d_s(g):
                act.wait_ge(ev("d_max"), g + 1)
                for c in range(4):
                    A_(s_b[:, c, 0:P], s_a[:, c, 0:P], ACT.Exp, bias=nm[:, 2 * c:2 * c + 1], scale=SCALE,
                       accum_out=sums[:, 2 * c:2 * c + 1])
                    last = A_(s_b[:, c, P:384], s_a[:, c, P:384], ACT.Exp, bias=nm[:, 2 * c + 1:2 * c + 2], scale=SCALE,
                              accum_out=sums[:, 2 * c + 1:2 * c + 2])
                last.then_inc(ev("d_exp"), 1)

            def d_x(g):
                act.wait_ge(ev("d_probs_turned"), g + 1)
                A_(s_c[:, 2:4, :], ps[:, 6:8, 0:384], ACT.Copy).then_inc(ev("d_probsT"), 1)

            def d_norm(_):
                inv_sqrt(2, ss[:, 0:8], rs[:, 0:8])
                for b in range(2):
                    act.wait_ge(ev("d_out_turned"), b + 1)
                    A_(mt_hi[:, 4 + 2 * b:6 + 2 * b, :], ps[:, 2 + b, :].rearrange("p (k t) -> p k t", k=2), ACT.Copy).then_inc(ev("d_mt_hi"), 1)

            def wo(n):
                act.wait_ge(unit_used, U_WO + n + 1)
                split_next(U_WO + n)

            act.wait_ge(small1_landed, 16 * 7)
            act.wait_ge(ev("lam_sums"), 1)
            A_(lam2, lam2, ACT.Exp).then_inc(ev("lam_exp"), 1)
            tasks = {"unit": unit1, "sb_z": sb_z, "sb_cum": sb_cum, "sb_pv": sb_pv, "rot": rot, "d_t": d_t, "d_s": d_s,
                     "d_x": d_x, "d_pv": lambda g: None, "d_norm": d_norm, "wo": wo}
            for name, n in ORDER1:
                tasks[name](n)

            def ffn_pair(u, s0, h, count, split_after=True):
                for j in range(2):
                    act.wait_ge(unit_used, u + j + 1)
                    A_(silu_t[:, j, :], ps[:, (s0[1] + j) % 2, 0:T], ACT.Silu).then_inc(silu_ready, 1)
                    act.wait_ge(hid_ready, h + j + 1)
                    A_(h_hi_t[:, j, :], hid[:, j, :], ACT.Copy).then_inc(hid_hi, 1)
                    if split_after:
                        split_hi(u + j + RING, (s0[0] + j) % RING, count[j])
                if split_after:
                    split_hi(u + 2 + RING, (s0[0] + 2) % RING, count[2])

            def counts(u0, extra):
                return [(u0 + j + RING) // RING + 1 + extra for j in range(3)]

            def ffn(u0, q0, h0):
                with act.Fori(0, FT_DENSE // 2) as i:
                    ffn_pair(u0 + i * 3, (u0, q0), h0 + i * 2, [i + c for c in counts(u0, 0)])

            norm(1)
            ffn(U_FFN1, Q_FFN1, H_FFN1)
            norm(2)

            def mixer(l):
                U, Q = U_MIX[l], Q_MIX[l]

                def unit(n):
                    src = ps[:, (Q + n) % 2, :]
                    two = src.rearrange("p (t c) -> p t c", t=2)
                    act.wait_ge(unit_used, U + n + 1)
                    done = evacuated[(Q + n) % 2]
                    if n < 2:
                        A_(qaT[:, 2 * n:2 * n + 2, :], two, ACT.Copy).then_inc(done, 1)
                    elif n == 2:
                        for half in range(2):
                            for head in range(2):
                                A_(kaT[64 * half:64 * half + 64, head, :], src[64 * head:64 * head + 64, 0:T], ACT.Copy)
                        A_(va, src[:, T:2 * T].rearrange("p (t c) -> p t c", t=2), ACT.Copy).then_inc(done, 1)
                    elif n == 3:
                        A_(qrT, two, ACT.Copy).then_inc(done, 1)
                    elif n == 4:
                        A_(krT, two, ACT.Copy, scale=32 ** -0.5).then_inc(done, 1)
                    elif n < 7:
                        c = (n - 5) * 256
                        A_(vr[:, :, c:c + 256], two, ACT.Copy).then_inc(done, 1)
                    elif n < 11:
                        c = (n - 7) % 2 * 256
                        A_(sg[:, (n - 7) // 2, :, c:c + 256], two, ACT.Silu).then_inc(done, 1)
                    else:
                        c = (n - 11) * 256
                        act.wait_ge(ev("gate_logit"), 8 * l + n - 11 + 1)
                        A_(gates[:, :, c:c + 256], gates[:, :, c:c + 256], ACT.Sigmoid).then_inc(ev("gate_ready"), 1)
                    split_next(U + n)

                def decays(_):
                    act.wait_ge(ev("mix_small"), 16 * 3 * (l + 1))
                    link(A_(lg_t[:, 1, :], lg_t[:, 0, :], ACT.Abs))
                    A_(lg_t[:, 1, :], lg_t[:, 1, :], ACT.Exp, scale=-1.0).then_inc(ev("lg_exp"), 1)
                    act.wait_ge(ev("lg_one"), l + 1)
                    A_(lg, lg_t[:, 2, :], ACT.Ln).then_inc(ev("lg_ln"), 1)
                    act.wait_ge(ev("lg_ready"), l + 1)
                    ahead = table("ahead").rearrange("p (d i) -> p d i", d=2)
                    for h in range(8):
                        for way in range(2):
                            last = A_(decay[:, h, way, :], ahead[:, way, :], ACT.Exp, scale=lg[:, way * 8 + h:way * 8 + h + 1])
                    last.then_inc(ev("decay_exp"), 1)

                def gqa_s(g):
                    act.wait_ge(ev("g_max"), 2 * l + g + 1)
                    for c in range(8):
                        A_(g_s[:, c // 2, c % 2, :], g_s[:, c // 2, c % 2, :], ACT.Exp, bias=nm[:, c:c + 1],
                           scale=SCALE, accum_out=sums[:, c:c + 1])
                    A_(rec, rec, ACT.Exp).then_inc(ev("g_exp"), 1)

                def gqa_t(g):
                    act.wait_ge(ev("g_turned"), 2 * l + g + 1)
                    A_(g_t, ps[:, 2:6, :].rearrange("p h (k t) -> p h k t", k=2), ACT.Copy).then_inc(ev("g_probsT"), 1)

                def gqa_out(_):
                    for b in range(2):
                        act.wait_ge(ev("attn_turned"), 2 * l + b + 1)
                        A_(mt_hi[:, 2 * b:2 * b + 2, :], ps[:, 2 + b, :].rearrange("p (k t) -> p k t", k=2), ACT.Copy).then_inc(ev("attn_hi"), 1)

                def ret_norm(_):
                    for way in range(2):
                        inv_sqrt(3 + 2 * l + way, ss[:, 0:16], rs[:, 0:16])
                    for b in range(2):
                        act.wait_ge(ev("ret_turned"), 2 * l + b + 1)
                        A_(mt_hi[:, 4 + 2 * b:6 + 2 * b, :], ps[:, 2 + b, :].rearrange("p (k t) -> p k t", k=2), ACT.Copy).then_inc(ev("ret_hi"), 1)

                def half_product(n):
                    q = Q + 19 + n
                    act.wait_ge(unit_used, U + 19 + n + 1)
                    c = n % 2 * 512
                    A_(y_mix[:, n // 2, :, c:c + 512], ps[:, 0:2, :], ACT.Copy).then_inc(evacuated[q % 2], 1)
                    split_next(U + 19 + n)

                def merge(_):
                    for b in range(4):
                        act.wait_ge(ev("merged_turned"), 4 * l + b + 1)
                        A_(xt_hi[:, 2 * b:2 * b + 2, :], ps[:, 2 + b, :].rearrange("p (k t) -> p k t", k=2), ACT.Copy).then_inc(ev("merged_hi"), 1)

                def out_unit(n):
                    act.wait_ge(unit_used, U + 23 + n + 1)
                    split_next(U + 23 + n)

                tasks = {"unit": unit, "decay": decays, "gqa_s": gqa_s, "gqa_t": gqa_t, "gqa_pv": lambda n: None,
                         "gqa_out": gqa_out, "ret_s": lambda n: None, "ret_pv": lambda n: None, "ret_norm": ret_norm,
                         "ya": half_product, "yr": lambda n: half_product(2 + n), "merge": merge, "out": out_unit}
                for name, n in ORDER2:
                    tasks[name](n)

            mixer(0)
            norm(3)
            ffn(U_FFN2, Q_FFN2, H_FFN2)
            norm(4)
            mixer(1)
            norm(5)
            act.wait_ge(ev("router_landed"), 32)
            A_(rw_hi[:, :], rw_raw[:, :], ACT.Copy).then_inc(ev("router_hi"), 1)
            act.wait_ge(ev("top_diff"), 1)
            A_(tw[:, :, 0:1], tw[:, :, 0:1], ACT.Exp).then_inc(ev("top_exp"), 1)
            act.wait_ge(ev("gates_spread"), 1)
            A_(gate_all, ps[:, 2:6, :].rearrange("p b (e t) -> p (b e) t", e=2), ACT.Copy).then_inc(ev("gates_ready"), 1)

            base = counts(U_MOE, 0)

            def moe_pair(off, g, i, count_i, last=False):
                u = U_MOE + off + g * 33 + (i * 3 if i is not None else 0)
                h = H_MOE + off * 2 // 3 + g * 22 + (i * 2 if i is not None else 0)
                k = off // 3 + g * 11 + (i if i is not None else 0)
                ffn_pair(u, (U_MOE, Q_MOE), h, [k + c for c in base], split_after=not last)

            def moe_group(g, last=False):
                with act.Fori(0, 5) as i:
                    moe_pair(0, g, i, None)
                moe_pair(15, g, None, None)
                with act.Fori(0, 4 if last else 5) as i:
                    moe_pair(18, g, i, None)
                if last:
                    moe_pair(18, g, 4, None, last=True)

            with act.Fori(0, EXPERTS // 2 - 1) as g:
                moe_group(g)
            moe_group(EXPERTS // 2 - 1, last=True)
            norm(6, turned=False)

        @block.vector
        def _(dve):
            link = Chain(dve, dve_step)
            TTo, TS, STT, CP = nc.vector.tensor_tensor, nc.vector.tensor_scalar, nc.vector.scalar_tensor_tensor, nc.vector.tensor_copy

            def split_lo(u, slot):
                dve.wait_ge(hi_ready, u + 1)
                TTo(w_lo[:, slot, :], raw[:, slot, :], w_hi[:, slot, :].bitcast(F32), ALU.subtract).then_inc(lo_ready, 1)

            def split_next(u):
                if u + RING < U_END:
                    split_lo(u + RING, u % RING)

            def low_of(dst_lo, dst_hi, bank, wait_for, count, done):
                dve.wait_ge(wait_for, count)
                TTo(dst_lo, ps[:, bank, :].rearrange("p (k t) -> p k t", k=2), dst_hi.bitcast(F32), ALU.subtract).then_inc(done, 1)

            def norm(n, rms=False, turned=True):
                for t in range(TT):
                    for c in range(2):
                        last = nc.vector.bn_stats(stats[:, t, c, :], x[:, t, c * 512:(c + 1) * 512])
                    link(last)
                for t in range(TT):
                    last = nc.vector.bn_aggr(mv[:, t, :], stats[:, t, :, :])
                link(last)
                if rms:
                    link(TTo(ms, mv[:, :, 0], mv[:, :, 0], ALU.mult))
                    link(TTo(ms, ms, mv[:, :, 1], ALU.add))
                    TS(ms, ms, RMS_EPS, None, ALU.add).then_inc(var_ready, 1)
                else:
                    TS(ms, mv[:, :, 1], LN_EPS, None, ALU.add).then_inc(var_ready, 1)
                dve.wait_ge(rstd_ready, n + 1)
                dve.wait_ge(gb_landed, 32 * (n + 1))
                for t in range(TT):
                    if rms:
                        STT(normed[:, t, :], x[:, t, :], rstd[:, t:t + 1], gb[:, 0, :], ALU.mult, ALU.mult).then_inc(rows_ready, 1)
                    else:
                        link(STT(x[:, t, :], x[:, t, :], mv[:, t, 0:1], gb[:, 0, :], ALU.subtract, ALU.mult))
                        STT(x[:, t, :], x[:, t, :], rstd[:, t:t + 1], gb[:, 1, :], ALU.mult, ALU.add).then_inc(rows_ready, 1)
                dve.wait_ge(rows_ready, 2 * (n + 1))
                CP(ms[:, 0:1], rstd[:, 0:1]).then_inc(gb_used, 1)
                if turned:
                    for b in range(4):
                        low_of(xt_lo[:, 2 * b:2 * b + 2, :], xt_hi[:, 2 * b:2 * b + 2, :], 2 + b, xt_hi_ready, 4 * n + b + 1, xt_ready)

            def group_rstd(n, eps, width, groups):
                TS(ss[:, 0:groups], ss[:, 0:groups], 1.0 / width, eps, ALU.mult, ALU.add).then_inc(ev("group_var"), 1)
                dve.wait_ge(ev("group_rstd"), n + 1)

            for u in range(RING):
                split_lo(u, u)
            dve.wait_ge(x_landed, 16)
            norm(0, rms=True)
            dve.wait_ge(small1_landed, 16 * 7)
            dve.wait_ge(consts_landed, 16)
            link(TTo(lam4[:, 0:3:2, :], lam4[:, 0:3:2, :], lam4[:, 1:4:2, :], ALU.mult))
            nc.vector.tensor_reduce(lam2, lam4[:, 0:3:2, :], AX.X, ALU.add).then_inc(ev("lam_sums"), 1)
            dve.wait_ge(ev("lam_exp"), 1)
            link(TTo(lam, lam2[:, 0:1], lam2[:, 1:2], ALU.subtract))
            link(TS(lam, lam, -1.0, -LAMBDA_INIT, ALU.mult, ALU.add))
            link(TS(gsub, gsub, 1.0 - LAMBDA_INIT, None, ALU.mult))

            def blocks(v):
                return v.rearrange("p h (b n) -> p h b n", n=P)[:, :, 0:3:2, :]

            mask4 = past.unsqueeze(1).unsqueeze(1).to_broadcast([P, 4, 2, P])
            causal4 = causal.unsqueeze(1).unsqueeze(1).to_broadcast([P, 4, 2, P])

            def unit1(n):
                split_next(U_IN1 + n)

            def sb_z(g):
                dve.wait_ge(ev("sb_ln"), g + 1)
                if g:
                    dve.wait_ge(ev("sb_acc"), g)
                link(TS(s_a, ps[:, 2:6, 0:384], SCALE, 0.0, ALU.mult, ALU.min))
                link(TTo(s_a, s_a, s_c, ALU.subtract))
                link(STT(s_b, ps[:, 2:6, 0:384], -SCALE, s_a, ALU.mult, ALU.add))
                TTo(blocks(s_b), blocks(s_b), mask4, ALU.mult).then_inc(ev("sb_logs"), 1)

            def sb_cum(g):
                dve.wait_ge(ev("sb_acc"), g + 1)
                TTo(s_a, ps[:, 2:6, 0:384], s_a, ALU.add).then_inc(ev("sb_sum"), 1)
                dve.wait_ge(ev("sb_exp"), g + 1)
                TTo(blocks(s_c), blocks(s_c), mask4, ALU.mult).then_inc(ev("sb_weights"), 1)

            def sb_pv(g):
                low_of(mt_lo[:, 2 * g:2 * g + 2, :], mt_hi[:, 2 * g:2 * g + 2, :], 6 + g, ev("sb_mt_hi"), g + 1, ev("sb_mt"))

            def rot(i):
                v = dqk[i]
                for q in (6 + 2 * i, 7 + 2 * i):
                    wait_evacuated(dve, q)
                link(TTo(rt, v, v, ALU.mult))
                link(nc.vector.tensor_reduce(ss[:, 0:16].rearrange("p (t h) -> p t h", t=TT), rt, AX.X, ALU.add))
                group_rstd(i, RMS_EPS, 64, 16)
                link(TTo(v, v, rs[:, 0:16].rearrange("p (t h) -> p t h", t=TT).unsqueeze(3).to_broadcast([P, TT, 8, 64]), ALU.mult))
                g8 = gq[:, i, :].unsqueeze(1).unsqueeze(1).to_broadcast([P, TT, 8, 64])
                link(TTo(v, v, g8, ALU.mult))
                cos = table("cos").rearrange("p (t e) -> p t e", t=TT).unsqueeze(2).to_broadcast([P, TT, 8, 64])
                sin = table("sin").rearrange("p (t e) -> p t e", t=TT).unsqueeze(2).to_broadcast([P, TT, 8, 64])
                TTo(rt[:, :, :, 0:32], v[:, :, :, 32:64], sin[:, :, :, 0:32], ALU.mult)
                link(TTo(rt[:, :, :, 32:64], v[:, :, :, 0:32], sin[:, :, :, 32:64], ALU.mult))
                link(TTo(v, v, cos, ALU.mult))
                TTo(v, v, rt, ALU.add).then_inc(ev("rotated"), 1)

            def d_s(g):
                dve.wait_ge(ev("d_scores"), g + 1)
                if g:
                    dve.wait_ge(ev("d_exp"), g)
                TTo(blocks(s_a), blocks(ps[:, 2:6, 0:384]), causal4, ALU.add)
                link(CP(s_a[:, :, P:2 * P], ps[:, 2:6, P:2 * P]))
                m = mx.rearrange("p (c t) -> p c t", t=2)
                nc.vector.reduce_max(m[:, :, 0], s_a[:, :, 0:P], AX.X)
                link(nc.vector.reduce_max(m[:, :, 1], s_a[:, :, P:384], AX.X))
                TS(nm, mx, -SCALE, None, ALU.mult).then_inc(ev("d_max"), 1)
                dve.wait_ge(ev("d_exp"), g + 1)
                if g:
                    dve.wait_ge(ev("d_probs_turned"), g)
                link(nc.vector.reciprocal(rec, sums))
                r = rec.rearrange("p (h c t) -> p h c t", c=2, t=2)
                link(TS(r[:, :, 1, :], r[:, :, 1, :], lam, None, ALU.mult))
                span = ((0, P), (P, 384))
                for hh in range(2):
                    for t, (a, b) in enumerate(span):
                        k = 4 * hh + 2 + t
                        last = TS(s_c[:, hh, a:b], s_b[:, 2 * hh + 1, a:b], rec[:, k:k + 1], None, ALU.mult)
                link(last)
                for hh in range(2):
                    for t, (a, b) in enumerate(span):
                        k = 4 * hh + t
                        last = STT(s_c[:, hh, a:b], s_b[:, 2 * hh, a:b], rec[:, k:k + 1], s_c[:, hh, a:b], ALU.mult, ALU.add)
                last.then_inc(ev("d_probs"), 1)

            def d_pv(g):
                dve.wait_ge(ev("d_product"), g + 1)
                src = ps[:, 6, :].rearrange("p (t h e) -> p t h e", t=TT, h=2)
                CP(d_out[:, :, 2 * g:2 * g + 2, :], src).then_inc(ev("d_out_copied"), 1)

            def d_norm(_):
                dve.wait_ge(ev("d_out_copied"), 2)
                sq = rt.rearrange("p t h e -> p (t h e)").rearrange("p (t h e) -> p t h e", t=TT, h=4)
                link(TTo(sq, d_out, d_out, ALU.mult))
                link(nc.vector.tensor_reduce(ss[:, 0:8].rearrange("p (t h) -> p t h", t=TT), sq, AX.X, ALU.add))
                group_rstd(2, SUBLN_EPS, 128, 8)
                link(TTo(d_out, d_out, rs[:, 0:8].rearrange("p (t h) -> p t h", t=TT).unsqueeze(3).to_broadcast([P, TT, 4, P]), ALU.mult))
                TTo(d_out, d_out, gsub.unsqueeze(1).unsqueeze(1).to_broadcast([P, TT, 4, P]), ALU.mult).then_inc(ev("d_normed"), 1)
                for b in range(2):
                    low_of(mt_lo[:, 4 + 2 * b:6 + 2 * b, :], mt_hi[:, 4 + 2 * b:6 + 2 * b, :], 2 + b, ev("d_mt_hi"), b + 1, ev("d_mt"))

            def add_unit(u, q, n, alpha):
                dve.wait_ge(unit_used, u + 1)
                v = x[:, :, n * 256:(n + 1) * 256]
                STT(v, v, alpha, ps[:, q % 2, :].rearrange("p (t c) -> p t c", t=2), ALU.mult, ALU.add).then_inc(evacuated[q % 2], 1)
                split_next(u)

            tasks = {"unit": unit1, "sb_z": sb_z, "sb_cum": sb_cum, "sb_pv": sb_pv, "rot": rot, "d_t": lambda n: None,
                     "d_s": d_s, "d_x": lambda n: None, "d_pv": d_pv, "d_norm": d_norm,
                     "wo": lambda n: add_unit(U_WO + n, 12 + n, n, 1.0)}
            for name, n in ORDER1:
                tasks[name](n)
            def residual_whole(q):
                wait_evacuated(dve, q - 1)
                wait_evacuated(dve, q - 2)

            residual_whole(Q_FFN1)

            def ffn_pair(u, s0, h, gate=None, split_after=True):
                for j in range(2):
                    bank = (s0[1] + j) % 2
                    dve.wait_ge(silu_ready, h + j + 1)
                    up = ps[:, bank, T:2 * T]
                    if gate is not None:
                        TTo(hid[:, j, :], up, gate[j], ALU.mult).then_inc(hid_scaled, 1)
                        dve.wait_ge(hid_scaled, h + j + 1 - H_MOE)
                        TTo(hid[:, j, :], hid[:, j, :], silu_t[:, j, :], ALU.mult).then_inc(hid_ready, 1)
                    else:
                        TTo(hid[:, j, :], up, silu_t[:, j, :], ALU.mult).then_inc(hid_ready, 1)
                    dve.wait_ge(hid_hi, h + j + 1)
                    TTo(h_lo_t[:, j, :], hid[:, j, :], h_hi_t[:, j, :].bitcast(F32), ALU.subtract).then_inc(evacuated[bank], 1)
                    if split_after:
                        split_lo(u + j + RING, (s0[0] + j) % RING)
                if split_after:
                    split_lo(u + 2 + RING, (s0[0] + 2) % RING)

            def add_acc(n, alpha):
                dve.wait_ge(acc_done, n + 1)
                for t in range(TT):
                    for c in range(2):
                        v = x[:, t, c * 512:(c + 1) * 512]
                        last = STT(v, v, alpha, ps[:, 2 + 2 * t + c, :], ALU.mult, ALU.add)
                link(last)

            def ffn(n, u0, q0, h0, alpha):
                with dve.Fori(0, FT_DENSE // 2) as i:
                    ffn_pair(u0 + i * 3, (u0, q0), h0 + i * 2)
                add_acc(n, alpha)

            norm(1, rms=True)
            ffn(0, U_FFN1, Q_FFN1, H_FFN1, 1.0)
            norm(2)

            def mixer(l):
                U, Q = U_MIX[l], Q_MIX[l]

                def unit(n):
                    if n >= 11:
                        k = n - 11
                        dve.wait_ge(unit_used, U + n + 1)
                        dve.wait_ge(ev(f"b_row{k % 2}"), 16 * (4 * l + k // 2 + 1))
                        row = b_rows[:, k % 2, :].unsqueeze(1).to_broadcast([P, TT, 256])
                        TTo(gates[:, :, k * 256:(k + 1) * 256], ps[:, (Q + n) % 2, :].rearrange("p (t c) -> p t c", t=2),
                            row, ALU.add).then_inc(evacuated[(Q + n) % 2], 1)
                        wait_evacuated(dve, Q + n)
                        CP(ms[:, 0:1], ms[:, 1:2]).then_inc(ev("gate_logit"), 1)
                    split_next(U + n)

                def decays(_):
                    dve.wait_ge(ev("lg_exp"), l + 1)
                    TS(lg_t[:, 2, :], lg_t[:, 1, :], 1.0, None, ALU.add).then_inc(ev("lg_one"), 1)
                    dve.wait_ge(ev("lg_ln"), l + 1)
                    link(TS(ss[:, 0:16], lg_t[:, 2, :], -1.0, -1.0, ALU.add, ALU.mult))
                    link(TTo(ss[:, 0:16], lg_t[:, 1, :], ss[:, 0:16], ALU.add))
                    link(nc.vector.reciprocal(rs[:, 0:16], lg_t[:, 2, :]))
                    link(TTo(ss[:, 0:16], ss[:, 0:16], rs[:, 0:16], ALU.mult))
                    link(TTo(lg, lg, ss[:, 0:16], ALU.add))
                    link(TS(lg_t[:, 0, :], lg_t[:, 0, :], 0.0, None, ALU.min))
                    TTo(lg, lg_t[:, 0, :], lg, ALU.subtract).then_inc(ev("lg_ready"), 1)
                    dve.wait_ge(ev("decay_exp"), l + 1)
                    on = table("ahead_on").rearrange("p (d i) -> p d i", d=2)
                    TTo(decay, decay, on.unsqueeze(1).to_broadcast([P, 8, 2, T]), ALU.mult).then_inc(ev("decay_ready"), 1)

                def gqa_s(g):
                    dve.wait_ge(ev("g_scores"), 2 * l + g + 1)
                    if g:
                        dve.wait_ge(ev("g_turned"), 2 * l + g)
                    dist = table("dist").rearrange("p (t k) -> p t k", t=TT)
                    for h in range(4):
                        last = STT(g_s[:, h, :, :], dist, -SLOPES[4 * g + h] / SCALE,
                                   ps[:, 2 + h, :].rearrange("p (t k) -> p t k", t=TT), ALU.mult, ALU.add)
                    link(last)
                    link(nc.vector.reduce_max(mx.rearrange("p (h t) -> p h t", t=TT), g_s, AX.X))
                    link(TS(mx, mx, SCALE, None, ALU.mult))
                    dve.wait_ge(ev("mix_small"), 16 * 3 * (l + 1))
                    sk = sink[:, 4 * g:4 * g + 4].unsqueeze(2).to_broadcast([P, 4, TT])
                    mh = mx.rearrange("p (h t) -> p h t", t=TT)
                    link(TTo(mh, mh, sk, ALU.max))
                    TS(nm, mx, -1.0, None, ALU.mult)
                    TTo(rec.rearrange("p (h t) -> p h t", t=TT), sk, mh, ALU.subtract).then_inc(ev("g_max"), 1)
                    dve.wait_ge(ev("g_exp"), 2 * l + g + 1)
                    link(TTo(rec, rec, sums, ALU.add))
                    link(nc.vector.reciprocal(rec_all[:, 8 * g:8 * g + 8], rec))

                def gqa_out(_):
                    dve.wait_ge(ev("g_product"), 2 * l + 2)
                    r = rec_all.rearrange("p (h t) -> p h t", t=TT)
                    for t in range(TT):
                        last = TTo(attn[:, t, :].rearrange("p (h e) -> p h e", e=64), ps[:, 6 + t, :].rearrange("p (h e) -> p h e", e=64),
                                   r[:, :, t].unsqueeze(2).to_broadcast([P, 8, 64]), ALU.mult)
                    last.then_inc(ev("attn_rows"), 1)
                    for b in range(2):
                        low_of(mt_lo[:, 2 * b:2 * b + 2, :], mt_hi[:, 2 * b:2 * b + 2, :], 2 + b, ev("attn_hi"), 2 * l + b + 1, ev("attn_mt"))

                def ret_s(h):
                    n = 8 * l + h
                    dve.wait_ge(ev("r_scores"), n + 1)
                    if h >= 2:
                        dve.wait_ge(ev("r_product"), n - 1)
                    s = ps[:, 2 + h % 2, :]
                    w = r_w[:, h % 2, :, :]
                    TTo(w[:, 0, 0:T], s[:, 0:T], decay[:, h, 0, :], ALU.mult)
                    TTo(w[:, 0, T:384], s[:, T + P:2 * T], decay[:, h, 0, 0:P], ALU.mult)
                    TTo(w[:, 1, 0:T], s[:, T:2 * T], decay[:, h, 1, :], ALU.mult)
                    TTo(w[:, 1, T:384], s[:, 0:P], decay[:, h, 1, P:T], ALU.mult).then_inc(ev("r_weights"), 1)

                def ret_norm(_):
                    dve.wait_ge(ev("r_product"), 8 * l + 8)
                    for way in range(2):
                        src = ps[:, 4 + 2 * way:6 + 2 * way, :].rearrange("p t (h e) -> p t h e", e=64)
                        mean = ss[:, 16:32].rearrange("p (t h) -> p t h", t=TT)
                        link(nc.vector.tensor_reduce(mean, src, AX.X, ALU.add))
                        link(TS(ss[:, 16:32], ss[:, 16:32], 1.0 / 64, None, ALU.mult))
                        link(TTo(y_n, src, mean.unsqueeze(3).to_broadcast([P, TT, 8, 64]), ALU.subtract))
                        link(TTo(y_sq, y_n, y_n, ALU.mult))
                        link(nc.vector.tensor_reduce(ss[:, 0:16].rearrange("p (t h) -> p t h", t=TT), y_sq, AX.X, ALU.add))
                        group_rstd(3 + 2 * l + way, LN_EPS, 64, 16)
                        link(TTo(y_n, y_n, rs[:, 0:16].rearrange("p (t h) -> p t h", t=TT).unsqueeze(3).to_broadcast([P, TT, 8, 64]), ALU.mult))
                        g = sg[:, way, :, :].rearrange("p t (h e) -> p t h e", e=64)
                        link(TTo(g, g, y_n, ALU.mult))
                    TTo(sg[:, 0, :, :], sg[:, 0, :, :], sg[:, 1, :, :], ALU.add).then_inc(ev("ret_rows"), 1)
                    for b in range(2):
                        low_of(mt_lo[:, 4 + 2 * b:6 + 2 * b, :], mt_hi[:, 4 + 2 * b:6 + 2 * b, :], 2 + b, ev("ret_hi"), 2 * l + b + 1, ev("ret_mt"))

                def merge(_):
                    for q in range(19, 23):
                        wait_evacuated(dve, Q + q)
                    dve.wait_ge(ev("gate_ready"), 8 * (l + 1))
                    for t in range(TT):
                        TTo(y_mix[:, 0, t, :], y_mix[:, 0, t, :], gates[:, t, 0:D], ALU.mult)
                        link(TTo(y_mix[:, 1, t, :], y_mix[:, 1, t, :], gates[:, t, D:2 * D], ALU.mult))
                        TTo(merged[:, t, :], y_mix[:, 0, t, :], y_mix[:, 1, t, :], ALU.add).then_inc(ev("merged_rows"), 1)
                    for b in range(4):
                        low_of(xt_lo[:, 2 * b:2 * b + 2, :], xt_hi[:, 2 * b:2 * b + 2, :], 2 + b, ev("merged_hi"), 4 * l + b + 1, ev("merged_xt"))

                tasks = {"unit": unit, "decay": decays, "gqa_s": gqa_s, "gqa_t": lambda n: None, "gqa_pv": lambda n: None,
                         "gqa_out": gqa_out, "ret_s": ret_s, "ret_pv": lambda n: None, "ret_norm": ret_norm,
                         "ya": lambda n: split_next(U + 19 + n), "yr": lambda n: split_next(U + 21 + n), "merge": merge,
                         "out": lambda n: add_unit(U + 23 + n, Q + 23 + n, n, ALPHA)}
                for name, n in ORDER2:
                    tasks[name](n)
                residual_whole(Q + 27)

            mixer(0)
            norm(3)
            ffn(1, U_FFN2, Q_FFN2, H_FFN2, ALPHA)
            norm(4)
            mixer(1)
            norm(5)
            dve.wait_ge(ev("router_hi"), 1)
            TTo(rw_lo[:, :], rw_raw[:, :], rw_hi[:, :].bitcast(F32), ALU.subtract).then_inc(ev("router_split"), 1)
            dve.wait_ge(ev("router_product"), 1)
            link(TTo(logit, ps[:, 2, 0:16].rearrange("p (t n) -> p t n", t=TT), rb.unsqueeze(1).to_broadcast([P, TT, 8]), ALU.add))
            for t in range(TT):
                last = nc.vector.max(top8[:, t, :], logit[:, t, :])
            link(last)
            for t in range(TT):
                last = nc.vector.max_index(idx_u[:, t, :], top8[:, t, :], logit[:, t, :])
            link(last)
            link(CP(idx_f, idx_u[:, :, :]))
            TTo(tw[:, :, 0:1], top8[:, :, 1:2], top8[:, :, 0:1], ALU.subtract).then_inc(ev("top_diff"), 1)
            dve.wait_ge(ev("top_exp"), 1)
            link(TS(tw[:, :, 1:2], tw[:, :, 0:1], 1.0, None, ALU.add))
            link(nc.vector.reciprocal(tw[:, :, 2:3], tw[:, :, 1:2]))
            link(TTo(tw[:, :, 3:4], tw[:, :, 0:1], tw[:, :, 2:3], ALU.mult))
            for t in range(TT):
                for a in range(2):
                    last = TS(gate8[:, a, t, :], table("expert"), idx_f[:, t, a:a + 1], tw[:, t, 2 + a:3 + a], ALU.is_equal, ALU.mult)
            link(last)
            link(TTo(gate8[:, 0, :, :], gate8[:, 0, :, :], gate8[:, 1, :, :], ALU.add))
            CP(gate_cols, gate8[:, 0, :, :].rearrange("p t n -> p (t n)").unsqueeze(2).to_broadcast([P, 16, P])).then_inc(ev("gate_cols"), 1)
            dve.wait_ge(ev("gates_ready"), 1)

            def moe_pair(off, g, i, experts, last=False):
                u = U_MOE + off + g * 33 + (i * 3 if i is not None else 0)
                h = H_MOE + off * 2 // 3 + g * 22 + (i * 2 if i is not None else 0)
                flat = gate_all.rearrange("p e t -> p (e t)")
                gate = [flat[:, bass.ds(e * T, T)] for e in experts]
                ffn_pair(u, (U_MOE, Q_MOE), h, gate, split_after=not last)

            def moe_group(g, last=False):
                first, second = g * 2, g * 2 + 1
                with dve.Fori(0, 5) as i:
                    moe_pair(0, g, i, (first, first))
                moe_pair(15, g, None, (first, second))
                with dve.Fori(0, 4 if last else 5) as i:
                    moe_pair(18, g, i, (second, second))
                if last:
                    moe_pair(18, g, 4, (second, second), last=True)

            with dve.Fori(0, EXPERTS // 2 - 1) as g:
                moe_group(g)
            moe_group(EXPERTS // 2 - 1, last=True)
            add_acc(2, ALPHA)
            norm(6, turned=False)

        @block.tensor
        def _(pe):
            MM, TR = nc.tensor.matmul, nc.tensor.transpose

            def product(dst, a_hi, a_lo, b_hi, b_lo, start, stop):
                MM(dst, a_hi, b_hi, start=start, stop=False)
                MM(dst, a_hi, b_lo, start=False, stop=False)
                return MM(dst, a_lo, b_hi, start=False, stop=stop)

            def weights_still(s, col, dst, xh=xt_hi, xl=xt_lo, step=256):
                for k in range(KT):
                    w = slice(k * step + col, k * step + col + P)
                    last = product(dst, w_hi[:, s, w], w_lo[:, s, w], xh[:, k, :], xl[:, k, :], k == 0, k == KT - 1)
                return last

            def tokens_still(s, t, dst, xh=xt_hi, xl=xt_lo, k0=0, nk=KT, step=256, col=0, width=256):
                for k in range(nk):
                    w = slice(k * step + col, k * step + col + width)
                    tok = slice(t * P, (t + 1) * P)
                    last = product(dst, xh[:, k0 + k, tok], xl[:, k0 + k, tok], w_hi[:, s, w], w_lo[:, s, w], k == 0, k == nk - 1)
                return last

            def begin(u, q):
                pe.wait_ge(lo_ready, u + 1)
                if q >= 2:
                    wait_evacuated(pe, q - 2)

            def turn_rows(n, rows):
                pe.wait_ge(rows_ready, 2 * n + 1)
                for k in range(KT):
                    TR(ps[:, 2 + k // 2, k % 2 * T:k % 2 * T + P], rows[:, 0, k * P:(k + 1) * P], ident)
                pe.wait_ge(rows_ready, 2 * n + 2)
                for k in range(KT):
                    last = TR(ps[:, 2 + k // 2, k % 2 * T + P:k % 2 * T + T], rows[:, 1, k * P:(k + 1) * P], ident)
                    if k % 2:
                        last.then_inc(rows_turned, 1)
                pe.wait_ge(xt_ready, 4 * (n + 1))

            def turn_four(src, done):
                for k in range(4):
                    for t in range(TT):
                        last = TR(ps[:, 2 + k // 2, k % 2 * T + t * P:k % 2 * T + (t + 1) * P], src[:, t, k * P:(k + 1) * P], ident)
                    if k % 2:
                        last.then_inc(done, 1)

            pe.wait_ge(consts_landed, 16)
            turn_rows(0, normed)

            def unit1(n):
                s = n % RING
                begin(n, n)
                for c in range(2):
                    dst = ps[:, n % 2, c * 256:(c + 1) * 256]
                    last = weights_still(s, c * P, dst) if IN1[n][0] in "qk" else tokens_still(s, c, dst)
                last.then_inc(unit_used, 1)

            def sb_z(g):
                for q in (2 * g, 2 * g + 1):
                    wait_evacuated(pe, q)
                if g:
                    pe.wait_ge(ev("sb_sum"), g)
                for i in range(4):
                    h = 4 * g + i
                    r = slice(h % 2 * 64, h % 2 * 64 + 64)
                    MM(ps[:, 2 + i, 0:T], kT[r, h // 2, 0:P], qT[r, h // 2, :], start=True, stop=True)
                    last = MM(ps[:, 2 + i, T:384], kT[r, h // 2, P:T], qT[r, h // 2, P:T], start=True, stop=True)
                last.then_inc(ev("sb_z"), 1)

            def sb_cum(g):
                pe.wait_ge(ev("sb_logs"), g + 1)
                for i in range(4):
                    MM(ps[:, 2 + i, 0:P], later, s_b[:, i, 0:P], start=True, stop=True)
                    MM(ps[:, 2 + i, P:T], later, s_b[:, i, P:T], start=True, stop=False)
                    MM(ps[:, 2 + i, P:T], ones, s_b[:, i, T:384], start=False, stop=True)
                    last = MM(ps[:, 2 + i, T:384], later, s_b[:, i, T:384], start=True, stop=True)
                last.then_inc(ev("sb_acc"), 1)

            def sb_pv(g):
                for q in (4, 5):
                    wait_evacuated(pe, q)
                pe.wait_ge(ev("sb_weights"), g + 1)
                for i in range(4):
                    h = 4 * g + i
                    r = slice(h % 2 * 64, h % 2 * 64 + 64)
                    c = i // 2 * 256
                    e = slice(h * 64, h * 64 + 64)
                    MM(ps[r, 6 + g, c:c + P], v_sb[:, 0, e], s_c[:, i, 0:P], start=True, stop=True)
                    MM(ps[r, 6 + g, c + P:c + T], v_sb[:, 0, e], s_c[:, i, P:T], start=True, stop=False)
                    last = MM(ps[r, 6 + g, c + P:c + T], v_sb[:, 1, e], s_c[:, i, T:384], start=False, stop=True)
                last.then_inc(ev("sb_pv"), 1)

            def d_t(_):
                pe.wait_ge(ev("sb_sum"), 2)
                for i in range(2):
                    pe.wait_ge(ev("rotated"), i + 1)
                    v = dqk[i].rearrange("p t h e -> p t (h e)")
                    for h in range(4):
                        for t in range(TT):
                            last = TR(ps[:, 2 + 2 * i + h // 2, h % 2 * T + t * P:h % 2 * T + (t + 1) * P], v[:, t, h * P:(h + 1) * P], ident)
                    last.then_inc(ev("d_turned"), 1)

            def d_s(g):
                pe.wait_ge(ev("d_copied"), 2)
                if g:
                    pe.wait_ge(ev("d_max"), g)
                for c in range(4):
                    h = 2 * g + c // 2
                    r = slice(c % 2 * 64, c % 2 * 64 + 64)
                    MM(ps[:, 2 + c, 0:P], dqkT[0][r, h, 0:P], dqkT[1][r, h, 0:P], start=True, stop=True)
                    last = MM(ps[:, 2 + c, P:384], dqkT[0][r, h, P:T], dqkT[1][r, h, :], start=True, stop=True)
                last.then_inc(ev("d_scores"), 1)

            def d_x(g):
                pe.wait_ge(ev("d_probs"), g + 1)
                if g:
                    pe.wait_ge(ev("d_out_copied"), g)
                else:
                    pe.wait_ge(ev("sb_mt"), 2)
                for i in range(2):
                    for b in range(3):
                        last = TR(ps[:, 6 + i, b * P:(b + 1) * P], s_c[:, i, b * P:(b + 1) * P], ident)
                last.then_inc(ev("d_probs_turned"), 1)

            def d_pv(g):
                for q in (10, 11):
                    wait_evacuated(pe, q)
                pe.wait_ge(ev("d_probsT"), g + 1)
                for i in range(2):
                    e = slice((2 * g + i) * P, (2 * g + i + 1) * P)
                    MM(ps[:, 6, i * P:(i + 1) * P], s_c[:, 2 + i, 0:P], dv[:, 0, e], start=True, stop=True)
                    MM(ps[:, 6, T + i * P:T + (i + 1) * P], s_c[:, 2 + i, P:T], dv[:, 0, e], start=True, stop=False)
                    last = MM(ps[:, 6, T + i * P:T + (i + 1) * P], s_c[:, 2 + i, T:384], dv[:, 1, e], start=False, stop=True)
                last.then_inc(ev("d_product"), 1)

            def d_norm(_):
                pe.wait_ge(ev("d_normed"), 1)
                turn_four(d_out.rearrange("p t h e -> p t (h e)"), ev("d_out_turned"))

            def wo(n):
                u = U_WO + n
                if n == 0:
                    pe.wait_ge(ev("sb_mt"), 2)
                    pe.wait_ge(ev("d_mt"), 2)
                begin(u, 12 + n)
                for t in range(TT):
                    last = tokens_still(u % RING, t, ps[:, (12 + n) % 2, t * 256:(t + 1) * 256], mt_hi, mt_lo)
                last.then_inc(unit_used, 1)

            tasks = {"unit": unit1, "sb_z": sb_z, "sb_cum": sb_cum, "sb_pv": sb_pv, "rot": lambda n: None, "d_t": d_t,
                     "d_s": d_s, "d_x": d_x, "d_pv": d_pv, "d_norm": d_norm, "wo": wo}
            for name, n in ORDER1:
                tasks[name](n)

            def ffn_pair(u, s0, half_q):
                for j in range(2):
                    s, bank = (s0[0] + j) % RING, (s0[1] + j) % 2
                    pe.wait_ge(lo_ready, u + j + 1)
                    pe.wait_ge(evacuated[bank], half_q[j])
                    weights_still(s, 0, ps[:, bank, 0:T], step=P)
                    for k in range(KT):
                        w = slice(1024 + k * P, 1024 + (k + 1) * P)
                        last = product(ps[:, bank, T:2 * T], w_hi[:, s, w], w_lo[:, s, w], xt_hi[:, k, :], xt_lo[:, k, :], k == 0, k == KT - 1)
                    last.then_inc(unit_used, 1)
                s = (s0[0] + 2) % RING
                pe.wait_ge(lo_ready, u + 3)
                for j in range(2):
                    pe.wait_ge(evacuated[(s0[1] + j) % 2], half_q[j] + 1)
                    for t in range(TT):
                        tok = slice(t * P, (t + 1) * P)
                        for c in range(2):
                            w = slice(j * 1024 + c * 512, j * 1024 + (c + 1) * 512)
                            dst = ps[:, 2 + 2 * t + c, :]
                            MM(dst, h_hi_t[:, j, tok], w_hi[:, s, w], start=False, stop=False)
                            MM(dst, h_hi_t[:, j, tok], w_lo[:, s, w], start=False, stop=False)
                            last = MM(dst, h_lo_t[:, j, tok], w_hi[:, s, w], start=False, stop=False)
                last.then_inc(unit_used, 1)

            def clear_acc():
                pe.wait_ge(zeroed, 1)
                for b in range(4):
                    MM(ps[:, 2 + b, :], zeros[:, 0:P], zeros[:, :], start=True, stop=False)

            def close_acc():
                for b in range(4):
                    last = MM(ps[:, 2 + b, :], zeros[:, 0:P], zeros[:, :], start=False, stop=True)
                last.then_inc(acc_done, 1)

            def ffn(u0, q0):
                clear_acc()
                with pe.Fori(0, FT_DENSE // 2) as i:
                    ffn_pair(u0 + i * 3, (u0, q0), [i + (q0 + j) // 2 for j in range(2)])
                close_acc()

            turn_rows(1, normed)
            ffn(U_FFN1, Q_FFN1)
            turn_rows(2, x)

            def mixer(l):
                U, Q = U_MIX[l], Q_MIX[l]

                def unit(n):
                    u, q = U + n, Q + n
                    s = u % RING
                    begin(u, q)
                    if n == 2:
                        weights_still(s, 0, ps[:, q % 2, 0:T])
                        for t in range(TT):
                            last = tokens_still(s, t, ps[:, q % 2, T + t * P:T + (t + 1) * P], col=P, width=P)
                    else:
                        for c in range(2):
                            dst = ps[:, q % 2, c * 256:(c + 1) * 256]
                            last = weights_still(s, c * P, dst) if n in (0, 1, 3, 4) else tokens_still(s, c, dst)
                    last.then_inc(unit_used, 1)

                def gqa_s(g):
                    for q in range(3):
                        wait_evacuated(pe, Q + q)
                    if g:
                        pe.wait_ge(ev("g_probsT"), 2 * l + g)
                    for i in range(4):
                        h = 4 * g + i
                        r = slice(h % 2 * 64, h % 2 * 64 + 64)
                        for t in range(TT):
                            last = MM(ps[:, 2 + i, t * T:(t + 1) * T], qaT[r, h // 2, t * P:(t + 1) * P], kaT[r, h // 4, :], start=True, stop=True)
                    last.then_inc(ev("g_scores"), 1)

                def gqa_t(g):
                    pe.wait_ge(ev("g_exp"), 2 * l + g + 1)
                    for i in range(4):
                        for k in range(2):
                            for t in range(TT):
                                last = TR(ps[:, 2 + i, k * T + t * P:k * T + (t + 1) * P], g_s[:, i, t, k * P:(k + 1) * P], ident)
                    last.then_inc(ev("g_turned"), 1)

                def gqa_pv(g):
                    pe.wait_ge(ev("g_probsT"), 2 * l + g + 1)
                    for i in range(4):
                        h = 4 * g + i
                        for t in range(TT):
                            for k in range(2):
                                last = MM(ps[:, 6 + t, h * 64:(h + 1) * 64], g_t[:, i, k, t * P:(t + 1) * P], va[:, k, g * 64:(g + 1) * 64],
                                          start=k == 0, stop=k == 1)
                    last.then_inc(ev("g_product"), 1)

                def gqa_out(_):
                    pe.wait_ge(ev("attn_rows"), l + 1)
                    turn_four(attn, ev("attn_turned"))

                def ret_s(h):
                    n = 8 * l + h
                    for q in (3, 4):
                        wait_evacuated(pe, Q + q)
                    if h < 2:
                        pe.wait_ge(ev("attn_mt"), 2 * l + 2)
                        pe.wait_ge(ev("decay_ready"), l + 1)
                    else:
                        pe.wait_ge(ev("r_weights"), n - 1)
                    r = slice(h % 4 * 32, h % 4 * 32 + 32)
                    for k in range(2):
                        last = MM(ps[:, 2 + h % 2, k * T:(k + 1) * T], krT[r, h // 4, k * P:(k + 1) * P], qrT[r, h // 4, :], start=True, stop=True)
                    last.then_inc(ev("r_scores"), 1)

                def ret_pv(h):
                    n = 8 * l + h
                    for q in (5, 6):
                        wait_evacuated(pe, Q + q)
                    pe.wait_ge(ev("r_weights"), n + 1)
                    e = slice(h * 64, h * 64 + 64)
                    w = r_w[:, h % 2, :, :]
                    for way in range(2):
                        near, far = way, 1 - way
                        own = slice(near * P, near * P + P)
                        both = slice(far * P, far * P + P)
                        MM(ps[:, 4 + 2 * way + near, e], w[:, way, own], vr[:, near, e], start=True, stop=True)
                        MM(ps[:, 4 + 2 * way + far, e], w[:, way, both], vr[:, near, e], start=True, stop=False)
                        last = MM(ps[:, 4 + 2 * way + far, e], w[:, way, T:384], vr[:, far, e], start=False, stop=True)
                    last.then_inc(ev("r_product"), 1)

                def ret_norm(_):
                    pe.wait_ge(ev("ret_rows"), l + 1)
                    turn_four(sg[:, 0, :, :], ev("ret_turned"))

                def half_product(n):
                    u, q = U + 19 + n, Q + 19 + n
                    if n == 0:
                        pe.wait_ge(ev("attn_mt"), 2 * l + 2)
                    if n == 2:
                        pe.wait_ge(ev("ret_mt"), 2 * l + 2)
                    begin(u, q)
                    wait_evacuated(pe, q - 1)
                    for t in range(TT):
                        last = tokens_still(u % RING, t, ps[:, t, :], mt_hi, mt_lo, k0=n // 2 * 4, nk=4, step=512, width=512)
                    last.then_inc(unit_used, 1)

                def merge(_):
                    for t in range(TT):
                        pe.wait_ge(ev("merged_rows"), 2 * l + t + 1)
                        for k in range(KT):
                            last = TR(ps[:, 2 + k // 2, k % 2 * T + t * P:k % 2 * T + (t + 1) * P], merged[:, t, k * P:(k + 1) * P], ident)
                            if t and k % 2:
                                last.then_inc(ev("merged_turned"), 1)

                def out_unit(n):
                    u, q = U + 23 + n, Q + 23 + n
                    if n == 0:
                        pe.wait_ge(ev("merged_xt"), 4 * l + 4)
                    begin(u, q)
                    for t in range(TT):
                        last = tokens_still(u % RING, t, ps[:, q % 2, t * 256:(t + 1) * 256])
                    last.then_inc(unit_used, 1)

                tasks = {"unit": unit, "decay": lambda n: None, "gqa_s": gqa_s, "gqa_t": gqa_t, "gqa_pv": gqa_pv,
                         "gqa_out": gqa_out, "ret_s": ret_s, "ret_pv": ret_pv, "ret_norm": ret_norm,
                         "ya": half_product, "yr": lambda n: half_product(2 + n), "merge": merge, "out": out_unit}
                for name, n in ORDER2:
                    tasks[name](n)

            mixer(0)
            turn_rows(3, x)
            ffn(U_FFN2, Q_FFN2)
            turn_rows(4, x)
            mixer(1)
            turn_rows(5, x)
            pe.wait_ge(ev("router_split"), 1)
            for t in range(TT):
                tok = slice(t * P, (t + 1) * P)
                for k in range(KT):
                    w = slice(k * 8, k * 8 + 8)
                    last = product(ps[:, 2, t * 8:t * 8 + 8], xt_hi[:, k, tok], xt_lo[:, k, tok], rw_hi[:, w], rw_lo[:, w], k == 0, k == KT - 1)
            last.then_inc(ev("router_product"), 1)
            pe.wait_ge(ev("gate_cols"), 1)
            for e in range(EXPERTS):
                for t in range(TT):
                    last = MM(ps[:, 2 + e // 2, e % 2 * T + t * P:e % 2 * T + (t + 1) * P], gate_cols[:, t * 8 + e, :], ident, start=True, stop=True)
            last.then_inc(ev("gates_spread"), 1)
            pe.wait_ge(ev("gates_ready"), 1)
            clear_acc()

            def moe_pair(off, g, i):
                k = off // 3 + g * 11 + (i if i is not None else 0)
                u = U_MOE + off + g * 33 + (i * 3 if i is not None else 0)
                ffn_pair(u, (U_MOE, Q_MOE), [k + (Q_MOE + j) // 2 for j in range(2)])

            with pe.Fori(0, EXPERTS // 2) as g:
                with pe.Fori(0, 5) as i:
                    moe_pair(0, g, i)
                moe_pair(15, g, None)
                with pe.Fori(0, 5) as i:
                    moe_pair(18, g, i)
            close_acc()


_INS = ["x", "attn_norm_g", "w_in", "diff_q_norm_g", "diff_k_norm_g", "lambda_q1", "lambda_k1", "lambda_q2",
        "lambda_k2", "diff_subln_g", "w_o", "ffn_norm_g", "w_gate", "w_up", "w_down", "ln_emb_g_2", "ln_emb_b_2",
        "w_in_2", "b_gate_2", "sink_logits_2", "decay_fwd_2", "decay_bwd_2", "w_o_attn_2", "w_o_ret_2", "w_out_2",
        "ln1_g_2", "ln1_b_2", "ffn_w1_2", "ffn_w3_2", "ffn_w2_2", "router_w_2", "router_b_2", "moe_w1_2", "moe_w3_2",
        "moe_w2_2", "ln2_g_2", "ln2_b_2"]


def kernel(**inputs):
    import numpy as _np
    import concourse.bacc as _bacc
    from concourse.bass_utils import run_bass_kernel_spmd as _run

    nc = _bacc.Bacc("TRN2", target_bir_lowering=False, num_devices=1)
    arrays, aps = {}, {}
    for name in _INS:
        a = _np.ascontiguousarray(inputs[name])
        arrays[f"in_{name}_dram"] = a
        aps[name] = nc.dram_tensor(f"in_{name}_dram", a.shape, mybir.dt.from_np(a.dtype), kind="ExternalInput").ap()
    arrays["const_dram"] = CONST_TABLE
    const = nc.dram_tensor("const_dram", CONST_TABLE.shape, F32, kind="ExternalInput").ap()
    out = nc.dram_tensor("out_dram", (1, T, D), F32, kind="ExternalOutput").ap()
    two_blocks(nc, aps, const, out)
    r = _run(nc, [arrays], core_ids=[0])
    return r.results[0]["out_dram"]
```

```python
import math
from contextlib import ExitStack

import numpy as np

import concourse.bass as bass
from concourse import mybir

F32 = mybir.dt.float32
F32R = mybir.dt.float32r
U32 = mybir.dt.uint32
ALU = mybir.AluOpType
ACT = mybir.ActivationFunctionType
AX = mybir.AxisListType

P = 128
T = 256
TT = T // P
D = 1024
KT = D // P
F_DENSE = 2816
F_EXPERT = 1408
EXPERTS = 8
SLOTS = P
FT_DENSE = F_DENSE // P
FT_EXPERT = F_EXPERT // P
RING = 3
UNIT = 2048
BIG = 1.0e30
SCALE = 64 ** -0.5
RMS_EPS, SUBLN_EPS, LN_EPS = 1e-6, 1e-5, 1e-5
LAMBDA_INIT = 0.8 - 0.6 * math.exp(-0.3 * 0)
ALPHA = 4 ** 0.25
SLOPES = [2.0 ** (-8.0 * (h + 1) / 8) for h in range(8)]

U_IN1, U_WO = 0, 12
U_FFN1 = U_WO + 4
U_MIX = [U_FFN1 + 33, U_FFN1 + 33 + 27 + 33]
U_FFN2 = U_MIX[0] + 27
U_MOE = U_MIX[1] + 27
EXPERT_UNITS = [("G", 0), ("U", 0)] + [x for i in range(1, 5) for x in (("G", i), ("D", i - 1), ("U", i))] + \
    [("M", 5), ("D", 4), ("A", 5), ("B", 5)]
PER_EXPERT = len(EXPERT_UNITS)
RAW_MOE = 2 * RING
PAIRS = 6
U_END = U_MOE + PER_EXPERT * EXPERTS
Q_FFN1 = 16
Q_MIX = [Q_FFN1 + 22, Q_FFN1 + 22 + 27 + 22]
Q_FFN2 = Q_MIX[0] + 27
Q_MOE = Q_MIX[1] + 27
H_FFN1, H_FFN2, H_MOE = 0, 22, 44

IN1 = [("q", 0), ("k", 512), ("q", 256), ("k", 768), ("v", 1024), ("v", 1280),
       ("dq", 1536), ("dq", 1792), ("dk", 2048), ("dk", 2304), ("dv", 2560), ("dv", 2816)]
ORDER1 = [("unit", 0), ("unit", 1), ("sb_z", 0), ("unit", 2), ("unit", 3), ("unit", 4), ("sb_cum", 0),
          ("unit", 5), ("unit", 6), ("sb_pv", 0), ("sb_z", 1), ("unit", 7), ("rot", 0), ("sb_cum", 1),
          ("unit", 8), ("unit", 9), ("sb_pv", 1), ("rot", 1), ("unit", 10), ("unit", 11),
          ("d_t", 0), ("d_s", 0), ("d_x", 0), ("d_s", 1), ("d_pv", 0), ("d_x", 1),
          ("d_pv", 1), ("d_norm", 0), ("wo", 0), ("wo", 1), ("wo", 2), ("wo", 3)]
ORDER2 = [("unit", 0), ("unit", 1), ("unit", 2), ("gqa_s", 0), ("unit", 3), ("unit", 4),
          ("gqa_t", 0), ("unit", 5), ("unit", 6), ("gqa_s", 1), ("gqa_pv", 0), ("unit", 7), ("unit", 8),
          ("gqa_t", 1), ("unit", 9), ("unit", 10), ("gqa_pv", 1), ("gqa_out", 0), ("decay", 0)]
for _h in range(8):
    ORDER2 += [("ret_s", _h), ("unit", 11 + _h)]
    if _h:
        ORDER2 += [("ret_pv", _h - 1)]
ORDER2 += [("ret_pv", 7), ("ya", 0), ("ya", 1), ("ret_norm", 0), ("yr", 0), ("yr", 1), ("merge", 0),
           ("out", 0), ("out", 1), ("out", 2), ("out", 3)]

CONSTS = {}


def constants():
    p = np.arange(P, dtype=np.float32)[:, None]
    c = np.arange(P, dtype=np.float32)[None, :]
    i = np.arange(T, dtype=np.float32)[None, :]
    parts = {
        "ident": (p == c),
        "later": (p > c),
        "ones": np.ones((P, P)),
        "past": (p < c),
        "causal": np.where(c <= p, 0.0, -BIG),
    }
    inv = (np.float32(10000.0) ** (-np.arange(32, dtype=np.float32) / np.float32(32))).astype(np.float32)
    ang = (np.arange(T, dtype=np.float32)[:, None] * inv[None, :]).astype(np.float32)
    cos, sin = np.cos(ang), np.sin(ang)
    rows = lambda a: a.reshape(TT, P, 64).transpose(1, 0, 2).reshape(P, TT * 64)
    parts["cos"] = rows(np.concatenate([cos, cos], 1))
    parts["sin"] = rows(np.concatenate([-sin, sin], 1))
    dist = [np.where(np.abs(t * P + p - i) <= 128, np.abs(t * P + p - i), BIG) for t in range(TT)]
    parts["dist"] = np.concatenate(dist, 1)
    parts["ahead"] = np.concatenate([np.maximum(i - p, 0), np.maximum(P + p - i, 0)], 1)
    parts["ahead_on"] = np.concatenate([i >= p, i < P + p], 1)
    parts["slot"] = np.broadcast_to(c, (P, P))
    at = 0
    for name, a in parts.items():
        CONSTS[name] = (at, a.shape[1])
        at += a.shape[1]
    return np.ascontiguousarray(np.concatenate([np.asarray(a, np.float32) for a in parts.values()], 1))


CONST_TABLE = constants()


def two_blocks(nc, A, const_dram, out):
    with ExitStack() as ctx:
        def sb(name, shape, dt=F32):
            return ctx.enter_context(nc.sbuf_tensor(name, shape, dt))

        def sem(name):
            return ctx.enter_context(nc.semaphore(name))

        raw = sb("raw", [P, RING, UNIT])
        w_hi = sb("w_hi", [P, RING, UNIT], F32R)
        w_lo = sb("w_lo", [P, RING, UNIT], F32R)
        xt_hi = sb("xt_hi", [P, KT, T], F32R)
        xt_lo = sb("xt_lo", [P, KT, T], F32R)
        mt_hi = sb("mt_hi", [P, KT, T], F32R)
        mt_lo = sb("mt_lo", [P, KT, T], F32R)
        h_hi_t = sb("h_hi_t", [P, 2, T], F32R)
        h_lo_t = sb("h_lo_t", [P, 2, T], F32R)
        zeros = sb("zeros", [P, 512], F32R)
        x = sb("x", [P, TT, D])
        gb = sb("gb", [P, 2, D])
        const = sb("const", list(CONST_TABLE.shape))
        small = sb("small", [P, 768])
        scr_at = nc.sbuf_base + (-nc.sbuf_base) % 32
        scr = sb("scr", [P, 16896])
        ps = ctx.enter_context(nc.psum_tensor("ps", [P, 8, 512], F32))

        def table(name):
            at, n = CONSTS[name]
            return const[:, at:at + n]

        ident, later, ones, past, causal = (table(n) for n in ("ident", "later", "ones", "past", "causal"))

        def area(at, *dims):
            n = int(np.prod(dims))
            v = scr[:, at:at + n]
            if len(dims) == 1:
                return v
            names = "abcd"[:len(dims)]
            return v.rearrange(f"p ({' '.join(names)}) -> p {' '.join(names)}",
                               **{names[i]: d for i, d in enumerate(dims)})

        def tiny(at, n):
            return small[:, at:at + n]

        xs_hi = mt_hi[:, :, :].rearrange("p k t -> p (k t)").rearrange("p (t d) -> p t d", t=TT)
        xs_lo = mt_lo[:, :, :].rearrange("p k t -> p (k t)").rearrange("p (t d) -> p t d", t=TT)
        qT, kT, v_sb = area(0, 4, T), area(1024, 4, T), area(2048, TT, 512)
        dqk = [area(3072, TT, 8, 64), area(4096, TT, 8, 64)]
        dv = area(5120, TT, 512)
        dqkT = [area(6144, 4, T), area(7168, 4, T)]
        s_a, s_b, s_c = area(8192, 4, 384), area(9728, 4, 384), area(11264, 4, 384)
        rt = area(12800, TT, 8, 64)
        d_out = area(13824, TT, 4, P)
        normed = area(14848, TT, D)
        silu_t, hid = area(4096, 2, T), area(4608, 2, T)
        pick = area(0, TT, EXPERTS, P)
        pick_t = area(2048, EXPERTS, T)

        def over_scr(name, at, n):
            return nc.alloc_sbuf_tensor_at(name, [P, n], F32R, offset=scr_at + 4 * at)

        raw_moe = [raw[:, (U_MOE + k) % RING, :] for k in range(RING)] + [area(at, UNIT) for at in (11520, 13568, 0)]
        pick_r = over_scr("pick_r", 5120, 2048)
        xg_hi = over_scr("xg_hi", 7168, 1024)
        xg_lo = over_scr("xg_lo", 8192, 1024)
        pick_now = over_scr("pick_now", 9216, 256)
        y_hi = over_scr("y_hi", 9472, 1024)
        y_lo = over_scr("y_lo", 10496, 1024)
        qaT, kaT, va = area(0, 4, T), area(1024, 2, T), area(1536, TT, P)
        qrT, krT, vr = area(1792, 2, T), area(2304, 2, T), area(2816, TT, 512)
        sg = area(3840, 2, TT, 512)
        gates = area(5888, TT, 2048)
        decay = area(9984, 8, 2, T)
        b_rows = area(14080, 2, T)
        g_s, g_t = area(14592, 4, TT, T), area(9984, 4, TT, T)
        r_w = area(14592, 2, 2, 384)
        y_sq = area(14592, TT, 8, 64)
        y_n = area(15616, TT, 8, 64)
        attn = area(12032, TT, 512)
        y_mix = area(9984, 2, TT, D)
        merged = area(0, TT, D)

        stats = tiny(0, 24).rearrange("p (t c s) -> p t c s", t=TT, c=2)
        mv = tiny(24, 4).rearrange("p (t s) -> p t s", t=TT)
        ms = tiny(28, 2)
        rstd = tiny(30, 2)
        ss = tiny(32, 32)
        rs = tiny(64, 32)
        lam4 = tiny(96, 256).rearrange("p (v e) -> p v e", v=4)
        lam2 = tiny(352, 2)
        lam = tiny(354, 1)
        mx, nm, sums, rec = tiny(356, 8), tiny(364, 8), tiny(372, 8), tiny(380, 8)
        rec_all = tiny(388, 16)
        sink = tiny(404, 8)
        lg = tiny(412, 16)
        lg_t = tiny(428, 48).rearrange("p (a n) -> p a n", a=3)
        gq = tiny(476, 128).rearrange("p (a n) -> p a n", a=2)
        gsub = tiny(604, 128)
        top8 = tiny(96, 16).rearrange("p (t n) -> p t n", t=TT)
        logit = tiny(112, 16).rearrange("p (t n) -> p t n", t=TT)
        tw = tiny(128, 8).rearrange("p (t n) -> p t n", t=TT)
        idx_f = tiny(136, 16).rearrange("p (t n) -> p t n", t=TT)
        gate8 = tiny(152, 32).rearrange("p (a t n) -> p a t n", a=2, t=TT)
        sel8 = tiny(192, 32).rearrange("p (a t n) -> p a t n", a=2, t=TT)
        rank8 = tiny(224, 16).rearrange("p (t n) -> p t n", t=TT)
        counts8 = sb("counts8", [P, EXPERTS], mybir.dt.int32)
        idx_u = sb("idx_u", [P, TT, 8], U32)
        rw_hi = sb("rw_hi", [P, KT * 8], F32R)
        rw_lo = sb("rw_lo", [P, KT * 8], F32R)
        rw_raw = sb("rw_raw", [P, KT * 8])
        rb = tiny(184, 8)

        raw_landed = [sem(f"raw_landed{i}") for i in range(RING)]
        raw_moe_landed = [raw_landed[(U_MOE + k) % RING] for k in range(RING)] + [sem(f"raw_moe_landed{i}") for i in range(RING)]
        hi_ready, lo_ready, unit_used = sem("hi_ready"), sem("lo_ready"), sem("unit_used")
        evacuated = [sem("evacuated0"), sem("evacuated1")]
        silu_ready, hid_ready, hid_hi = sem("silu_ready"), sem("hid_ready"), sem("hid_hi")
        acc_done = sem("acc_done")
        silued, hid_rows, hid_turned = sem("silued"), sem("hid_rows"), sem("hid_turned")
        hid_hi_m, hid_pair = sem("hid_hi_m"), sem("hid_pair")
        act_step, dve_step, pool_step = sem("act_step"), sem("dve_step"), sem("pool_step")
        x_landed, consts_landed, small1_landed = sem("x_landed"), sem("consts_landed"), sem("small1_landed")
        gb_landed, gb_used = sem("gb_landed"), sem("gb_used")
        var_ready, rstd_ready = sem("var_ready"), sem("rstd_ready")
        rows_ready, rows_turned, xt_hi_ready, xt_ready = sem("rows_ready"), sem("rows_turned"), sem("xt_hi_ready"), sem("xt_ready")
        zeroed = sem("zeroed")
        stored = sem("stored")
        S = {}

        def ev(name):
            if name not in S:
                S[name] = sem(name)
            return S[name]

        block = ctx.enter_context(nc.Block())

        class Chain:
            def __init__(self, engine, step):
                self.engine, self.step, self.n = engine, step, 0

            def __call__(self, ins):
                self.n += 1
                ins.then_inc(self.step, 1)
                self.engine.wait_ge(self.step, self.n)

        def wait_evacuated(eng, q):
            eng.wait_ge(evacuated[q % 2], q // 2 + 1)

        def k_major(w):
            return w.rearrange("(k p) n -> p k n", p=P)

        @block.sync
        def _(sp):
            sp.dma_start(x[:, :, :], A["x"][0].rearrange("(t p) d -> p t d", p=P)).then_inc(x_landed, 16)

            def load(u, slot, first, second, width=1024):
                if not (isinstance(u, int) and u < RING):
                    sp.wait_ge(lo_ready, u - RING + 1)
                fill(raw[:, slot, :], raw_landed[slot], first, second, width)

            def fill(place, landed, first, second, width):
                for half, src in ((0, first), (1, second)):
                    dst = place[:, half * width:(half + 1) * width]
                    if len(src.shape) == 3:
                        dst = dst.rearrange("p (k n) -> p k n", k=src.shape[1])
                    elif len(src.shape) == 4:
                        dst = dst.rearrange("p (e k n) -> p e k n", e=src.shape[1], k=src.shape[2])
                    sp.dma_start(dst, src).then_inc(landed, 16)

            def load_square(u, w, c):
                v = k_major(w)
                load(u, u % RING, v[:, 0:4, c:c + 256], v[:, 4:8, c:c + 256])

            def load_short(u, w, c):
                v = k_major(w)
                load(u, u % RING, v[:, 0:2, c:c + 512], v[:, 2:4, c:c + 512])

            def load_ffn(u0, wg, wu, wd):
                gv, uv = k_major(wg), k_major(wu)
                with sp.Fori(0, FT_DENSE // 2) as i:
                    for j in range(2):
                        c = bass.ds(i * 256 + j * P, P)
                        load(u0 + j + i * 3, (u0 + j) % RING, gv[:, :, c], uv[:, :, c])
                    load(u0 + 2 + i * 3, (u0 + 2) % RING, wd[bass.ds(i * 256, P), :], wd[bass.ds(i * 256 + P, P), :])

            for n, (_, c) in enumerate(IN1):
                load_square(U_IN1 + n, A["w_in"][0], c)
            for n in range(4):
                load_square(U_WO + n, A["w_o"][0], n * 256)
            load_ffn(U_FFN1, A["w_gate"][0], A["w_up"][0], A["w_down"][0])
            for l in range(2):
                for n in range(19):
                    load_square(U_MIX[l] + n, A["w_in_2"][l], n * 256)
                for n in range(2):
                    load_short(U_MIX[l] + 19 + n, A["w_o_attn_2"][l], n * 512)
                for n in range(2):
                    load_short(U_MIX[l] + 21 + n, A["w_o_ret_2"][l], n * 512)
                for n in range(4):
                    load_square(U_MIX[l] + 23 + n, A["w_out_2"][l], n * 256)
                if l == 0:
                    load_ffn(U_FFN2, A["ffn_w1_2"][0], A["ffn_w3_2"][0], A["ffn_w2_2"][0])
            w1 = A["moe_w1_2"][0].rearrange("e (k p) n -> p e k n", p=P)
            w3 = A["moe_w3_2"][0].rearrange("e (k p) n -> p e k n", p=P)
            w2 = A["moe_w2_2"][0].rearrange("e f d -> (e f) d")

            def load_expert(e, first=False):
                own = (slice(None), bass.ds(e, 1))
                for p, (kind, i) in enumerate(EXPERT_UNITS):
                    slot = p % RAW_MOE
                    if not (first and p < RAW_MOE):
                        sp.wait_ge(lo_ready, U_MOE + e * PER_EXPERT + p - RAW_MOE + 1)
                    elif p < RING:
                        sp.wait_ge(lo_ready, U_MOE + p - RING + 1)
                    elif p == RING:
                        sp.wait_ge(ev("router_landed"), 32)
                        sp.wait_ge(ev("routing"), 1)
                    elif p == RAW_MOE - 1:
                        sp.wait_ge(ev("pick_r"), 1)
                        sp.wait_ge(ev("pick_t"), 1)
                    width = 1024
                    if kind in "GU":
                        w, c = (w1, w3)[kind == "U"], slice(i * 256, (i + 1) * 256)
                        halves = w[own + (slice(0, 4), c)], w[own + (slice(4, 8), c)]
                    elif kind == "M":
                        c = slice(1280, F_EXPERT)
                        halves = w1[own + (slice(None), c)], w3[own + (slice(None), c)]
                    elif kind == "D":
                        row = e * F_EXPERT + i * 256
                        halves = w2[bass.ds(row, P), :], w2[bass.ds(row + P, P), :]
                    else:
                        row, c, width = w2[bass.ds(e * F_EXPERT + 1280, P), :], 512 * (kind == "B"), 256
                        halves = row[:, c:c + 256], row[:, c + 256:c + 512]
                    fill(raw_moe[slot], raw_moe_landed[slot], *halves, width)

            load_expert(0, first=True)
            with sp.Fori(1, EXPERTS) as e:
                load_expert(e)
            for t in range(TT):
                sp.wait_ge(rows_ready, 2 * 6 + t + 1)
                sp.dma_start(out[0, t * P:(t + 1) * P, :], x[:, t, :]).then_inc(stored, 16)
            sp.wait_ge(stored, 16 * TT)

        @block.gpsimd
        def _(pool):
            def row(v, n):
                return v.rearrange("(a n) -> a n", a=1).partition_broadcast(P) if len(v.shape) == 1 else v.partition_broadcast(P)

            pool.dma_start(const[:, :], const_dram).then_inc(consts_landed, 16)
            norms = [(A["attn_norm_g"][0], None), (A["ffn_norm_g"][0], None),
                     (A["ln_emb_g_2"], A["ln_emb_b_2"]),
                     (A["ln1_g_2"][0], A["ln1_b_2"][0]), (A["ln2_g_2"][0], A["ln2_b_2"][0]),
                     (A["ln1_g_2"][1], A["ln1_b_2"][1]), (A["ln2_g_2"][1], A["ln2_b_2"][1])]

            def load_norm(n):
                if n:
                    pool.wait_ge(gb_used, n)
                for i, v in enumerate(norms[n]):
                    pool.dma_start(gb[:, i, :], row(v if v is not None else norms[n][0], D)).then_inc(gb_landed, 16)

            pool.memset(zeros[:, :].bitcast(F32), 0.0).then_inc(zeroed, 1)
            load_norm(0)
            for i, name in enumerate(("lambda_q1", "lambda_k1", "lambda_q2", "lambda_k2")):
                pool.dma_start(lam4[:, i, :], row(A[name][0], 64)).then_inc(small1_landed, 16)
            pool.dma_start(gq[:, 0, :], row(A["diff_q_norm_g"][0], 64)).then_inc(small1_landed, 16)
            pool.dma_start(gq[:, 1, :], row(A["diff_k_norm_g"][0], 64)).then_inc(small1_landed, 16)
            pool.dma_start(gsub, row(A["diff_subln_g"][0], P)).then_inc(small1_landed, 16)
            load_norm(1)
            load_norm(2)
            for l in range(2):
                pool.wait_ge(rows_ready, 2 * (2 + 2 * l) + 2)
                pool.dma_start(sink, row(A["sink_logits_2"][l], 8)).then_inc(ev("mix_small"), 16)
                pool.dma_start(lg_t[:, 0, 0:8], row(A["decay_fwd_2"][l], 8)).then_inc(ev("mix_small"), 16)
                pool.dma_start(lg_t[:, 0, 8:16], row(A["decay_bwd_2"][l], 8)).then_inc(ev("mix_small"), 16)
                load_norm(3 + 2 * l)
                for n in range(8):
                    if n >= 2:
                        wait_evacuated(pool, Q_MIX[l] + 11 + n - 2)
                    pool.dma_start(b_rows[:, n % 2, :], row(A["b_gate_2"][l, n * 256:(n + 1) * 256], 256)).then_inc(ev(f"b_row{n % 2}"), 16)
                load_norm(4 + 2 * l)
                if l == 1:
                    pool.dma_start(rw_raw[:, :].rearrange("p (k n) -> p k n", n=8), k_major(A["router_w_2"][0])).then_inc(ev("router_landed"), 16)
                    pool.dma_start(rb, row(A["router_b_2"][0], 8)).then_inc(ev("router_landed"), 16)

        @block.scalar
        def _(act):
            link = Chain(act, act_step)
            A_ = nc.scalar.activation

            def split_hi(u, slot, count):
                act.wait_ge(raw_landed[slot], count * 32)
                if not (isinstance(u, int) and u < RING):
                    act.wait_ge(unit_used, u - RING + 1)
                A_(w_hi[:, slot, :], raw[:, slot, :], ACT.Copy).then_inc(hi_ready, 1)

            def split_next(u):
                if u + RING < U_END:
                    split_hi(u + RING, u % RING, (u + RING) // RING + 1)

            def evac(u, q, dst, src, func=ACT.Copy):
                act.wait_ge(unit_used, u + 1)
                A_(dst, src, func).then_inc(evacuated[q % 2], 1)

            def turn(n, banks, dst, count, name_in, name_out):
                for b in range(banks):
                    act.wait_ge(name_in, count + b + 1)
                    A_(dst[:, 2 * b:2 * b + 2, :], ps[:, 2 + b, :].rearrange("p (k t) -> p k t", k=2), ACT.Copy).then_inc(name_out, 1)

            def norm(n, turned=True):
                act.wait_ge(var_ready, n + 1)
                link(A_(rstd, ms, ACT.Ln))
                A_(rstd, rstd, ACT.Exp, scale=-0.5).then_inc(rstd_ready, 1)
                if turned:
                    turn(n, 4, xt_hi, 4 * n, rows_turned, xt_hi_ready)

            def inv_sqrt(n, src, dst):
                act.wait_ge(ev("group_var"), n + 1)
                link(A_(dst, src, ACT.Ln))
                A_(dst, dst, ACT.Exp, scale=-0.5).then_inc(ev("group_rstd"), 1)

            for u in range(RING):
                split_hi(u, u, 1)
            act.wait_ge(consts_landed, 16)
            norm(0)

            def unit1(n):
                q, kind = n, IN1[n][0]
                src = ps[:, q % 2, :]
                two = src.rearrange("p (t c) -> p t c", t=2)
                second = IN1[n][1] % 512 // 256
                dst = {"q": qT[:, 2 * second:2 * second + 2, :], "k": kT[:, 2 * second:2 * second + 2, :],
                       "v": v_sb[:, :, 256 * second:256 * second + 256],
                       "dq": dqk[0].rearrange("p t h e -> p t (h e)")[:, :, 256 * second:256 * second + 256],
                       "dk": dqk[1].rearrange("p t h e -> p t (h e)")[:, :, 256 * second:256 * second + 256],
                       "dv": dv[:, :, 256 * second:256 * second + 256]}[kind]
                evac(U_IN1 + n, q, dst, two)
                split_next(U_IN1 + n)

            def sb_z(g):
                act.wait_ge(ev("sb_z"), g + 1)
                if g:
                    act.wait_ge(ev("sb_pv"), g)
                link(A_(s_c, ps[:, 2:6, 0:384], ACT.Abs, scale=SCALE))
                link(A_(s_c, s_c, ACT.Exp, scale=-1.0))
                A_(s_c, s_c, ACT.Ln, bias=1.0).then_inc(ev("sb_ln"), 1)

            def sb_cum(g):
                act.wait_ge(ev("sb_sum"), g + 1)
                A_(s_c, s_a, ACT.Exp).then_inc(ev("sb_exp"), 1)

            def sb_pv(g):
                act.wait_ge(ev("sb_pv"), g + 1)
                A_(mt_hi[:, 2 * g:2 * g + 2, :], ps[:, 6 + g, :].rearrange("p (k t) -> p k t", k=2), ACT.Copy).then_inc(ev("sb_mt_hi"), 1)

            def rot(i):
                inv_sqrt(i, ss[:, 0:16], rs[:, 0:16])

            def d_t(_):
                for i in range(2):
                    act.wait_ge(ev("d_turned"), i + 1)
                    A_(dqkT[i], ps[:, 2 + 2 * i:4 + 2 * i, :].rearrange("p b (k t) -> p (b k) t", k=2), ACT.Copy).then_inc(ev("d_copied"), 1)

            def d_s(g):
                act.wait_ge(ev("d_max"), g + 1)
                for c in range(4):
                    A_(s_b[:, c, 0:P], s_a[:, c, 0:P], ACT.Exp, bias=nm[:, 2 * c:2 * c + 1], scale=SCALE,
                       accum_out=sums[:, 2 * c:2 * c + 1])
                    last = A_(s_b[:, c, P:384], s_a[:, c, P:384], ACT.Exp, bias=nm[:, 2 * c + 1:2 * c + 2], scale=SCALE,
                              accum_out=sums[:, 2 * c + 1:2 * c + 2])
                last.then_inc(ev("d_exp"), 1)

            def d_x(g):
                act.wait_ge(ev("d_probs_turned"), g + 1)
                A_(s_c[:, 2:4, :], ps[:, 6:8, 0:384], ACT.Copy).then_inc(ev("d_probsT"), 1)

            def d_norm(_):
                inv_sqrt(2, ss[:, 0:8], rs[:, 0:8])
                for b in range(2):
                    act.wait_ge(ev("d_out_turned"), b + 1)
                    A_(mt_hi[:, 4 + 2 * b:6 + 2 * b, :], ps[:, 2 + b, :].rearrange("p (k t) -> p k t", k=2), ACT.Copy).then_inc(ev("d_mt_hi"), 1)

            def wo(n):
                act.wait_ge(unit_used, U_WO + n + 1)
                split_next(U_WO + n)

            act.wait_ge(small1_landed, 16 * 7)
            act.wait_ge(ev("lam_sums"), 1)
            A_(lam2, lam2, ACT.Exp).then_inc(ev("lam_exp"), 1)
            tasks = {"unit": unit1, "sb_z": sb_z, "sb_cum": sb_cum, "sb_pv": sb_pv, "rot": rot, "d_t": d_t, "d_s": d_s,
                     "d_x": d_x, "d_pv": lambda g: None, "d_norm": d_norm, "wo": wo}
            for name, n in ORDER1:
                tasks[name](n)

            def ffn_pair(u, s0, h, count):
                for j in range(2):
                    act.wait_ge(unit_used, u + j + 1)
                    A_(silu_t[:, j, :], ps[:, (s0[1] + j) % 2, 0:T], ACT.Silu).then_inc(silu_ready, 1)
                    act.wait_ge(hid_ready, h + j + 1)
                    A_(h_hi_t[:, j, :], hid[:, j, :], ACT.Copy).then_inc(hid_hi, 1)
                    split_hi(u + j + RING, (s0[0] + j) % RING, count[j])
                split_hi(u + 2 + RING, (s0[0] + 2) % RING, count[2])

            def counts(u0, extra):
                return [(u0 + j + RING) // RING + 1 + extra for j in range(3)]

            def ffn(u0, q0, h0):
                with act.Fori(0, FT_DENSE // 2) as i:
                    ffn_pair(u0 + i * 3, (u0, q0), h0 + i * 2, [i + c for c in counts(u0, 0)])

            norm(1)
            ffn(U_FFN1, Q_FFN1, H_FFN1)
            norm(2)

            def mixer(l):
                U, Q = U_MIX[l], Q_MIX[l]

                def unit(n):
                    src = ps[:, (Q + n) % 2, :]
                    two = src.rearrange("p (t c) -> p t c", t=2)
                    act.wait_ge(unit_used, U + n + 1)
                    done = evacuated[(Q + n) % 2]
                    if n < 2:
                        A_(qaT[:, 2 * n:2 * n + 2, :], two, ACT.Copy).then_inc(done, 1)
                    elif n == 2:
                        for half in range(2):
                            for head in range(2):
                                A_(kaT[64 * half:64 * half + 64, head, :], src[64 * head:64 * head + 64, 0:T], ACT.Copy)
                        A_(va, src[:, T:2 * T].rearrange("p (t c) -> p t c", t=2), ACT.Copy).then_inc(done, 1)
                    elif n == 3:
                        A_(qrT, two, ACT.Copy).then_inc(done, 1)
                    elif n == 4:
                        A_(krT, two, ACT.Copy, scale=32 ** -0.5).then_inc(done, 1)
                    elif n < 7:
                        c = (n - 5) * 256
                        A_(vr[:, :, c:c + 256], two, ACT.Copy).then_inc(done, 1)
                    elif n < 11:
                        c = (n - 7) % 2 * 256
                        A_(sg[:, (n - 7) // 2, :, c:c + 256], two, ACT.Silu).then_inc(done, 1)
                    else:
                        c = (n - 11) * 256
                        act.wait_ge(ev("gate_logit"), 8 * l + n - 11 + 1)
                        A_(gates[:, :, c:c + 256], gates[:, :, c:c + 256], ACT.Sigmoid).then_inc(ev("gate_ready"), 1)
                    split_next(U + n)

                def decays(_):
                    act.wait_ge(ev("mix_small"), 16 * 3 * (l + 1))
                    link(A_(lg_t[:, 1, :], lg_t[:, 0, :], ACT.Abs))
                    A_(lg_t[:, 1, :], lg_t[:, 1, :], ACT.Exp, scale=-1.0).then_inc(ev("lg_exp"), 1)
                    act.wait_ge(ev("lg_one"), l + 1)
                    A_(lg, lg_t[:, 2, :], ACT.Ln).then_inc(ev("lg_ln"), 1)
                    act.wait_ge(ev("lg_ready"), l + 1)
                    ahead = table("ahead").rearrange("p (d i) -> p d i", d=2)
                    for h in range(8):
                        for way in range(2):
                            last = A_(decay[:, h, way, :], ahead[:, way, :], ACT.Exp, scale=lg[:, way * 8 + h:way * 8 + h + 1])
                    last.then_inc(ev("decay_exp"), 1)

                def gqa_s(g):
                    act.wait_ge(ev("g_max"), 2 * l + g + 1)
                    for c in range(8):
                        A_(g_s[:, c // 2, c % 2, :], g_s[:, c // 2, c % 2, :], ACT.Exp, bias=nm[:, c:c + 1],
                           scale=SCALE, accum_out=sums[:, c:c + 1])
                    A_(rec, rec, ACT.Exp).then_inc(ev("g_exp"), 1)

                def gqa_t(g):
                    act.wait_ge(ev("g_turned"), 2 * l + g + 1)
                    A_(g_t, ps[:, 2:6, :].rearrange("p h (k t) -> p h k t", k=2), ACT.Copy).then_inc(ev("g_probsT"), 1)

                def gqa_out(_):
                    for b in range(2):
                        act.wait_ge(ev("attn_turned"), 2 * l + b + 1)
                        A_(mt_hi[:, 2 * b:2 * b + 2, :], ps[:, 2 + b, :].rearrange("p (k t) -> p k t", k=2), ACT.Copy).then_inc(ev("attn_hi"), 1)

                def ret_norm(_):
                    for way in range(2):
                        inv_sqrt(3 + 2 * l + way, ss[:, 0:16], rs[:, 0:16])
                    for b in range(2):
                        act.wait_ge(ev("ret_turned"), 2 * l + b + 1)
                        A_(mt_hi[:, 4 + 2 * b:6 + 2 * b, :], ps[:, 2 + b, :].rearrange("p (k t) -> p k t", k=2), ACT.Copy).then_inc(ev("ret_hi"), 1)

                def half_product(n):
                    q = Q + 19 + n
                    act.wait_ge(unit_used, U + 19 + n + 1)
                    c = n % 2 * 512
                    A_(y_mix[:, n // 2, :, c:c + 512], ps[:, 0:2, :], ACT.Copy).then_inc(evacuated[q % 2], 1)
                    split_next(U + 19 + n)

                def merge(_):
                    for b in range(4):
                        act.wait_ge(ev("merged_turned"), 4 * l + b + 1)
                        A_(xt_hi[:, 2 * b:2 * b + 2, :], ps[:, 2 + b, :].rearrange("p (k t) -> p k t", k=2), ACT.Copy).then_inc(ev("merged_hi"), 1)

                def out_unit(n):
                    act.wait_ge(unit_used, U + 23 + n + 1)
                    split_next(U + 23 + n)

                tasks = {"unit": unit, "decay": decays, "gqa_s": gqa_s, "gqa_t": gqa_t, "gqa_pv": lambda n: None,
                         "gqa_out": gqa_out, "ret_s": lambda n: None, "ret_pv": lambda n: None, "ret_norm": ret_norm,
                         "ya": half_product, "yr": lambda n: half_product(2 + n), "merge": merge, "out": out_unit}
                for name, n in ORDER2:
                    tasks[name](n)

            mixer(0)
            norm(3)
            ffn(U_FFN2, Q_FFN2, H_FFN2)
            norm(4)
            mixer(1)
            norm(5)
            act.wait_ge(ev("router_landed"), 32)
            A_(rw_hi[:, :], rw_raw[:, :], ACT.Copy).then_inc(ev("router_hi"), 1)
            act.wait_ge(ev("top_diff"), 1)
            A_(tw[:, :, 0:1], tw[:, :, 0:1], ACT.Exp).then_inc(ev("top_exp"), 1)
            A_(xs_hi, x[:, :, :], ACT.Copy).then_inc(ev("xs_hi"), 1)
            act.wait_ge(ev("pick_turned"), 1)
            A_(pick_t, ps[:, 2:6, :].rearrange("p b (e t) -> p (b e) t", e=2), ACT.Copy).then_inc(ev("pick_t"), 1)

            def take_gathered(n):
                act.wait_ge(ev("gathered"), n + 1)
                A_(xg_hi[:, :], ps[:, 2:4, :], ACT.Copy).then_inc(ev("xg_hi"), 1)

            take_gathered(0)
            def expert(e, dense, last):
                tiles = TT if dense else 1
                u, n = U_MOE + e * PER_EXPERT, e * PAIRS

                def silu(i, p):
                    act.wait_ge(unit_used, u + p + 1)
                    width = P if i == 5 else T
                    src = ps[:, 0, :].rearrange("p (t c) -> p t c", t=TT)[:, 0:tiles, 0:width]
                    A_(silu_t[:, 0:tiles, 0:width], src, ACT.Silu).then_inc(silued, 1)

                def take_hidden(i):
                    act.wait_ge(hid_turned, n + i + 1)
                    js = 1 if i == 5 else 2
                    src = ps[:, 1, :].rearrange("p (j t) -> p j t", j=2)[:, 0:js, 0:tiles * P]
                    A_(h_hi_t[:, 0:js, 0:tiles * P], src, ACT.Copy).then_inc(hid_hi_m, 1)

                def ahead(p):
                    q = p + RING
                    if q < PER_EXPERT or not last:
                        width = 512 if q < PER_EXPERT and EXPERT_UNITS[q][0] in "AB" else UNIT
                        k, slot = q % RAW_MOE, (U_MOE + q) % RING
                        before = (U_MOE + k) // RING if k < RING else 0
                        act.wait_ge(raw_moe_landed[k], 32 * (before + 1 + q // RAW_MOE + e * (PER_EXPERT // RAW_MOE)))
                        act.wait_ge(unit_used, u + p + 1)
                        A_(w_hi[:, slot, 0:width], raw_moe[k][:, 0:width], ACT.Copy).then_inc(hi_ready, 1)

                silu(0, 0)
                ahead(0)
                ahead(1)
                for i in range(1, 5):
                    p = 3 * i - 1
                    take_hidden(i - 1)
                    silu(i, p)
                    for q in range(p, p + 3):
                        ahead(q)
                take_hidden(4)
                silu(5, 14)
                ahead(14)
                take_hidden(5)
                if not dense and not last:
                    take_gathered(e + 1)
                ahead(15)
                act.wait_ge(ev("y_done"), e + 1)
                if dense:
                    A_(ms[:, 0:1], ms[:, 1:2], ACT.Copy).then_inc(ev("y_hi"), 1)
                else:
                    A_(y_hi[:, :], ps[:, 6:8, :], ACT.Copy).then_inc(ev("y_hi"), 1)
                ahead(16)
                ahead(17)
                if dense and not last:
                    take_gathered(e + 1)

            def either(e, last=False):
                n = act.value_load(counts8[0:1, bass.ds(e, 1)], min_val=0, max_val=T)
                with act.If(n > SLOTS):
                    expert(e, True, last)
                with act.Else():
                    expert(e, False, last)

            act.wait_ge(ev("counts_ready"), 1)
            with act.Fori(0, EXPERTS - 1) as e:
                either(e)
            either(EXPERTS - 1, last=True)
            norm(6, turned=False)

        @block.vector
        def _(dve):
            link = Chain(dve, dve_step)
            TTo, TS, STT, CP = nc.vector.tensor_tensor, nc.vector.tensor_scalar, nc.vector.scalar_tensor_tensor, nc.vector.tensor_copy

            def split_lo(u, slot):
                dve.wait_ge(hi_ready, u + 1)
                TTo(w_lo[:, slot, :], raw[:, slot, :], w_hi[:, slot, :].bitcast(F32), ALU.subtract).then_inc(lo_ready, 1)

            def split_next(u):
                if u + RING < U_END:
                    split_lo(u + RING, u % RING)

            def low_of(dst_lo, dst_hi, bank, wait_for, count, done):
                dve.wait_ge(wait_for, count)
                TTo(dst_lo, ps[:, bank, :].rearrange("p (k t) -> p k t", k=2), dst_hi.bitcast(F32), ALU.subtract).then_inc(done, 1)

            def norm(n, rms=False, turned=True):
                for t in range(TT):
                    for c in range(2):
                        last = nc.vector.bn_stats(stats[:, t, c, :], x[:, t, c * 512:(c + 1) * 512])
                    link(last)
                for t in range(TT):
                    last = nc.vector.bn_aggr(mv[:, t, :], stats[:, t, :, :])
                link(last)
                if rms:
                    link(TTo(ms, mv[:, :, 0], mv[:, :, 0], ALU.mult))
                    link(TTo(ms, ms, mv[:, :, 1], ALU.add))
                    TS(ms, ms, RMS_EPS, None, ALU.add).then_inc(var_ready, 1)
                else:
                    TS(ms, mv[:, :, 1], LN_EPS, None, ALU.add).then_inc(var_ready, 1)
                dve.wait_ge(rstd_ready, n + 1)
                dve.wait_ge(gb_landed, 32 * (n + 1))
                for t in range(TT):
                    if rms:
                        STT(normed[:, t, :], x[:, t, :], rstd[:, t:t + 1], gb[:, 0, :], ALU.mult, ALU.mult).then_inc(rows_ready, 1)
                    else:
                        link(STT(x[:, t, :], x[:, t, :], mv[:, t, 0:1], gb[:, 0, :], ALU.subtract, ALU.mult))
                        STT(x[:, t, :], x[:, t, :], rstd[:, t:t + 1], gb[:, 1, :], ALU.mult, ALU.add).then_inc(rows_ready, 1)
                dve.wait_ge(rows_ready, 2 * (n + 1))
                CP(ms[:, 0:1], rstd[:, 0:1]).then_inc(gb_used, 1)
                if turned:
                    for b in range(4):
                        low_of(xt_lo[:, 2 * b:2 * b + 2, :], xt_hi[:, 2 * b:2 * b + 2, :], 2 + b, xt_hi_ready, 4 * n + b + 1, xt_ready)

            def group_rstd(n, eps, width, groups):
                TS(ss[:, 0:groups], ss[:, 0:groups], 1.0 / width, eps, ALU.mult, ALU.add).then_inc(ev("group_var"), 1)
                dve.wait_ge(ev("group_rstd"), n + 1)

            for u in range(RING):
                split_lo(u, u)
            dve.wait_ge(x_landed, 16)
            norm(0, rms=True)
            dve.wait_ge(small1_landed, 16 * 7)
            dve.wait_ge(consts_landed, 16)
            link(TTo(lam4[:, 0:3:2, :], lam4[:, 0:3:2, :], lam4[:, 1:4:2, :], ALU.mult))
            nc.vector.tensor_reduce(lam2, lam4[:, 0:3:2, :], AX.X, ALU.add).then_inc(ev("lam_sums"), 1)
            dve.wait_ge(ev("lam_exp"), 1)
            link(TTo(lam, lam2[:, 0:1], lam2[:, 1:2], ALU.subtract))
            link(TS(lam, lam, -1.0, -LAMBDA_INIT, ALU.mult, ALU.add))
            link(TS(gsub, gsub, 1.0 - LAMBDA_INIT, None, ALU.mult))

            def blocks(v):
                return v.rearrange("p h (b n) -> p h b n", n=P)[:, :, 0:3:2, :]

            mask4 = past.unsqueeze(1).unsqueeze(1).to_broadcast([P, 4, 2, P])
            causal4 = causal.unsqueeze(1).unsqueeze(1).to_broadcast([P, 4, 2, P])

            def unit1(n):
                split_next(U_IN1 + n)

            def sb_z(g):
                dve.wait_ge(ev("sb_ln"), g + 1)
                if g:
                    dve.wait_ge(ev("sb_acc"), g)
                link(TS(s_a, ps[:, 2:6, 0:384], SCALE, 0.0, ALU.mult, ALU.min))
                link(TTo(s_a, s_a, s_c, ALU.subtract))
                link(STT(s_b, ps[:, 2:6, 0:384], -SCALE, s_a, ALU.mult, ALU.add))
                TTo(blocks(s_b), blocks(s_b), mask4, ALU.mult).then_inc(ev("sb_logs"), 1)

            def sb_cum(g):
                dve.wait_ge(ev("sb_acc"), g + 1)
                TTo(s_a, ps[:, 2:6, 0:384], s_a, ALU.add).then_inc(ev("sb_sum"), 1)
                dve.wait_ge(ev("sb_exp"), g + 1)
                TTo(blocks(s_c), blocks(s_c), mask4, ALU.mult).then_inc(ev("sb_weights"), 1)

            def sb_pv(g):
                low_of(mt_lo[:, 2 * g:2 * g + 2, :], mt_hi[:, 2 * g:2 * g + 2, :], 6 + g, ev("sb_mt_hi"), g + 1, ev("sb_mt"))

            def rot(i):
                v = dqk[i]
                for q in (6 + 2 * i, 7 + 2 * i):
                    wait_evacuated(dve, q)
                link(TTo(rt, v, v, ALU.mult))
                link(nc.vector.tensor_reduce(ss[:, 0:16].rearrange("p (t h) -> p t h", t=TT), rt, AX.X, ALU.add))
                group_rstd(i, RMS_EPS, 64, 16)
                link(TTo(v, v, rs[:, 0:16].rearrange("p (t h) -> p t h", t=TT).unsqueeze(3).to_broadcast([P, TT, 8, 64]), ALU.mult))
                g8 = gq[:, i, :].unsqueeze(1).unsqueeze(1).to_broadcast([P, TT, 8, 64])
                link(TTo(v, v, g8, ALU.mult))
                cos = table("cos").rearrange("p (t e) -> p t e", t=TT).unsqueeze(2).to_broadcast([P, TT, 8, 64])
                sin = table("sin").rearrange("p (t e) -> p t e", t=TT).unsqueeze(2).to_broadcast([P, TT, 8, 64])
                TTo(rt[:, :, :, 0:32], v[:, :, :, 32:64], sin[:, :, :, 0:32], ALU.mult)
                link(TTo(rt[:, :, :, 32:64], v[:, :, :, 0:32], sin[:, :, :, 32:64], ALU.mult))
                link(TTo(v, v, cos, ALU.mult))
                TTo(v, v, rt, ALU.add).then_inc(ev("rotated"), 1)

            def d_s(g):
                dve.wait_ge(ev("d_scores"), g + 1)
                if g:
                    dve.wait_ge(ev("d_exp"), g)
                TTo(blocks(s_a), blocks(ps[:, 2:6, 0:384]), causal4, ALU.add)
                link(CP(s_a[:, :, P:2 * P], ps[:, 2:6, P:2 * P]))
                m = mx.rearrange("p (c t) -> p c t", t=2)
                nc.vector.reduce_max(m[:, :, 0], s_a[:, :, 0:P], AX.X)
                link(nc.vector.reduce_max(m[:, :, 1], s_a[:, :, P:384], AX.X))
                TS(nm, mx, -SCALE, None, ALU.mult).then_inc(ev("d_max"), 1)
                dve.wait_ge(ev("d_exp"), g + 1)
                if g:
                    dve.wait_ge(ev("d_probs_turned"), g)
                link(nc.vector.reciprocal(rec, sums))
                r = rec.rearrange("p (h c t) -> p h c t", c=2, t=2)
                link(TS(r[:, :, 1, :], r[:, :, 1, :], lam, None, ALU.mult))
                span = ((0, P), (P, 384))
                for hh in range(2):
                    for t, (a, b) in enumerate(span):
                        k = 4 * hh + 2 + t
                        last = TS(s_c[:, hh, a:b], s_b[:, 2 * hh + 1, a:b], rec[:, k:k + 1], None, ALU.mult)
                link(last)
                for hh in range(2):
                    for t, (a, b) in enumerate(span):
                        k = 4 * hh + t
                        last = STT(s_c[:, hh, a:b], s_b[:, 2 * hh, a:b], rec[:, k:k + 1], s_c[:, hh, a:b], ALU.mult, ALU.add)
                last.then_inc(ev("d_probs"), 1)

            def d_pv(g):
                dve.wait_ge(ev("d_product"), g + 1)
                src = ps[:, 6, :].rearrange("p (t h e) -> p t h e", t=TT, h=2)
                CP(d_out[:, :, 2 * g:2 * g + 2, :], src).then_inc(ev("d_out_copied"), 1)

            def d_norm(_):
                dve.wait_ge(ev("d_out_copied"), 2)
                sq = rt.rearrange("p t h e -> p (t h e)").rearrange("p (t h e) -> p t h e", t=TT, h=4)
                link(TTo(sq, d_out, d_out, ALU.mult))
                link(nc.vector.tensor_reduce(ss[:, 0:8].rearrange("p (t h) -> p t h", t=TT), sq, AX.X, ALU.add))
                group_rstd(2, SUBLN_EPS, 128, 8)
                link(TTo(d_out, d_out, rs[:, 0:8].rearrange("p (t h) -> p t h", t=TT).unsqueeze(3).to_broadcast([P, TT, 4, P]), ALU.mult))
                TTo(d_out, d_out, gsub.unsqueeze(1).unsqueeze(1).to_broadcast([P, TT, 4, P]), ALU.mult).then_inc(ev("d_normed"), 1)
                for b in range(2):
                    low_of(mt_lo[:, 4 + 2 * b:6 + 2 * b, :], mt_hi[:, 4 + 2 * b:6 + 2 * b, :], 2 + b, ev("d_mt_hi"), b + 1, ev("d_mt"))

            def add_unit(u, q, n, alpha):
                dve.wait_ge(unit_used, u + 1)
                v = x[:, :, n * 256:(n + 1) * 256]
                STT(v, v, alpha, ps[:, q % 2, :].rearrange("p (t c) -> p t c", t=2), ALU.mult, ALU.add).then_inc(evacuated[q % 2], 1)
                split_next(u)

            tasks = {"unit": unit1, "sb_z": sb_z, "sb_cum": sb_cum, "sb_pv": sb_pv, "rot": rot, "d_t": lambda n: None,
                     "d_s": d_s, "d_x": lambda n: None, "d_pv": d_pv, "d_norm": d_norm,
                     "wo": lambda n: add_unit(U_WO + n, 12 + n, n, 1.0)}
            for name, n in ORDER1:
                tasks[name](n)
            def residual_whole(q):
                wait_evacuated(dve, q - 1)
                wait_evacuated(dve, q - 2)

            residual_whole(Q_FFN1)

            def ffn_pair(u, s0, h):
                for j in range(2):
                    bank = (s0[1] + j) % 2
                    dve.wait_ge(silu_ready, h + j + 1)
                    up = ps[:, bank, T:2 * T]
                    TTo(hid[:, j, :], up, silu_t[:, j, :], ALU.mult).then_inc(hid_ready, 1)
                    dve.wait_ge(hid_hi, h + j + 1)
                    TTo(h_lo_t[:, j, :], hid[:, j, :], h_hi_t[:, j, :].bitcast(F32), ALU.subtract).then_inc(evacuated[bank], 1)
                    split_lo(u + j + RING, (s0[0] + j) % RING)
                split_lo(u + 2 + RING, (s0[0] + 2) % RING)

            def add_acc(n, alpha):
                dve.wait_ge(acc_done, n + 1)
                for t in range(TT):
                    for c in range(2):
                        v = x[:, t, c * 512:(c + 1) * 512]
                        last = STT(v, v, alpha, ps[:, 2 + 2 * t + c, :], ALU.mult, ALU.add)
                link(last)

            def ffn(n, u0, q0, h0, alpha):
                with dve.Fori(0, FT_DENSE // 2) as i:
                    ffn_pair(u0 + i * 3, (u0, q0), h0 + i * 2)
                add_acc(n, alpha)

            norm(1, rms=True)
            ffn(0, U_FFN1, Q_FFN1, H_FFN1, 1.0)
            norm(2)

            def mixer(l):
                U, Q = U_MIX[l], Q_MIX[l]

                def unit(n):
                    if n >= 11:
                        k = n - 11
                        dve.wait_ge(unit_used, U + n + 1)
                        dve.wait_ge(ev(f"b_row{k % 2}"), 16 * (4 * l + k // 2 + 1))
                        row = b_rows[:, k % 2, :].unsqueeze(1).to_broadcast([P, TT, 256])
                        TTo(gates[:, :, k * 256:(k + 1) * 256], ps[:, (Q + n) % 2, :].rearrange("p (t c) -> p t c", t=2),
                            row, ALU.add).then_inc(evacuated[(Q + n) % 2], 1)
                        wait_evacuated(dve, Q + n)
                        CP(ms[:, 0:1], ms[:, 1:2]).then_inc(ev("gate_logit"), 1)
                    split_next(U + n)

                def decays(_):
                    dve.wait_ge(ev("lg_exp"), l + 1)
                    TS(lg_t[:, 2, :], lg_t[:, 1, :], 1.0, None, ALU.add).then_inc(ev("lg_one"), 1)
                    dve.wait_ge(ev("lg_ln"), l + 1)
                    link(TS(ss[:, 0:16], lg_t[:, 2, :], -1.0, -1.0, ALU.add, ALU.mult))
                    link(TTo(ss[:, 0:16], lg_t[:, 1, :], ss[:, 0:16], ALU.add))
                    link(nc.vector.reciprocal(rs[:, 0:16], lg_t[:, 2, :]))
                    link(TTo(ss[:, 0:16], ss[:, 0:16], rs[:, 0:16], ALU.mult))
                    link(TTo(lg, lg, ss[:, 0:16], ALU.add))
                    link(TS(lg_t[:, 0, :], lg_t[:, 0, :], 0.0, None, ALU.min))
                    TTo(lg, lg_t[:, 0, :], lg, ALU.subtract).then_inc(ev("lg_ready"), 1)
                    dve.wait_ge(ev("decay_exp"), l + 1)
                    on = table("ahead_on").rearrange("p (d i) -> p d i", d=2)
                    TTo(decay, decay, on.unsqueeze(1).to_broadcast([P, 8, 2, T]), ALU.mult).then_inc(ev("decay_ready"), 1)

                def gqa_s(g):
                    dve.wait_ge(ev("g_scores"), 2 * l + g + 1)
                    if g:
                        dve.wait_ge(ev("g_turned"), 2 * l + g)
                    dist = table("dist").rearrange("p (t k) -> p t k", t=TT)
                    for h in range(4):
                        last = STT(g_s[:, h, :, :], dist, -SLOPES[4 * g + h] / SCALE,
                                   ps[:, 2 + h, :].rearrange("p (t k) -> p t k", t=TT), ALU.mult, ALU.add)
                    link(last)
                    link(nc.vector.reduce_max(mx.rearrange("p (h t) -> p h t", t=TT), g_s, AX.X))
                    link(TS(mx, mx, SCALE, None, ALU.mult))
                    dve.wait_ge(ev("mix_small"), 16 * 3 * (l + 1))
                    sk = sink[:, 4 * g:4 * g + 4].unsqueeze(2).to_broadcast([P, 4, TT])
                    mh = mx.rearrange("p (h t) -> p h t", t=TT)
                    link(TTo(mh, mh, sk, ALU.max))
                    TS(nm, mx, -1.0, None, ALU.mult)
                    TTo(rec.rearrange("p (h t) -> p h t", t=TT), sk, mh, ALU.subtract).then_inc(ev("g_max"), 1)
                    dve.wait_ge(ev("g_exp"), 2 * l + g + 1)
                    link(TTo(rec, rec, sums, ALU.add))
                    link(nc.vector.reciprocal(rec_all[:, 8 * g:8 * g + 8], rec))

                def gqa_out(_):
                    dve.wait_ge(ev("g_product"), 2 * l + 2)
                    r = rec_all.rearrange("p (h t) -> p h t", t=TT)
                    for t in range(TT):
                        last = TTo(attn[:, t, :].rearrange("p (h e) -> p h e", e=64), ps[:, 6 + t, :].rearrange("p (h e) -> p h e", e=64),
                                   r[:, :, t].unsqueeze(2).to_broadcast([P, 8, 64]), ALU.mult)
                    last.then_inc(ev("attn_rows"), 1)
                    for b in range(2):
                        low_of(mt_lo[:, 2 * b:2 * b + 2, :], mt_hi[:, 2 * b:2 * b + 2, :], 2 + b, ev("attn_hi"), 2 * l + b + 1, ev("attn_mt"))

                def ret_s(h):
                    n = 8 * l + h
                    dve.wait_ge(ev("r_scores"), n + 1)
                    if h >= 2:
                        dve.wait_ge(ev("r_product"), n - 1)
                    s = ps[:, 2 + h % 2, :]
                    w = r_w[:, h % 2, :, :]
                    TTo(w[:, 0, 0:T], s[:, 0:T], decay[:, h, 0, :], ALU.mult)
                    TTo(w[:, 0, T:384], s[:, T + P:2 * T], decay[:, h, 0, 0:P], ALU.mult)
                    TTo(w[:, 1, 0:T], s[:, T:2 * T], decay[:, h, 1, :], ALU.mult)
                    TTo(w[:, 1, T:384], s[:, 0:P], decay[:, h, 1, P:T], ALU.mult).then_inc(ev("r_weights"), 1)

                def ret_norm(_):
                    dve.wait_ge(ev("r_product"), 8 * l + 8)
                    for way in range(2):
                        src = ps[:, 4 + 2 * way:6 + 2 * way, :].rearrange("p t (h e) -> p t h e", e=64)
                        mean = ss[:, 16:32].rearrange("p (t h) -> p t h", t=TT)
                        link(nc.vector.tensor_reduce(mean, src, AX.X, ALU.add))
                        link(TS(ss[:, 16:32], ss[:, 16:32], 1.0 / 64, None, ALU.mult))
                        link(TTo(y_n, src, mean.unsqueeze(3).to_broadcast([P, TT, 8, 64]), ALU.subtract))
                        link(TTo(y_sq, y_n, y_n, ALU.mult))
                        link(nc.vector.tensor_reduce(ss[:, 0:16].rearrange("p (t h) -> p t h", t=TT), y_sq, AX.X, ALU.add))
                        group_rstd(3 + 2 * l + way, LN_EPS, 64, 16)
                        link(TTo(y_n, y_n, rs[:, 0:16].rearrange("p (t h) -> p t h", t=TT).unsqueeze(3).to_broadcast([P, TT, 8, 64]), ALU.mult))
                        g = sg[:, way, :, :].rearrange("p t (h e) -> p t h e", e=64)
                        link(TTo(g, g, y_n, ALU.mult))
                    TTo(sg[:, 0, :, :], sg[:, 0, :, :], sg[:, 1, :, :], ALU.add).then_inc(ev("ret_rows"), 1)
                    for b in range(2):
                        low_of(mt_lo[:, 4 + 2 * b:6 + 2 * b, :], mt_hi[:, 4 + 2 * b:6 + 2 * b, :], 2 + b, ev("ret_hi"), 2 * l + b + 1, ev("ret_mt"))

                def merge(_):
                    for q in range(19, 23):
                        wait_evacuated(dve, Q + q)
                    dve.wait_ge(ev("gate_ready"), 8 * (l + 1))
                    for t in range(TT):
                        TTo(y_mix[:, 0, t, :], y_mix[:, 0, t, :], gates[:, t, 0:D], ALU.mult)
                        link(TTo(y_mix[:, 1, t, :], y_mix[:, 1, t, :], gates[:, t, D:2 * D], ALU.mult))
                        TTo(merged[:, t, :], y_mix[:, 0, t, :], y_mix[:, 1, t, :], ALU.add).then_inc(ev("merged_rows"), 1)
                    for b in range(4):
                        low_of(xt_lo[:, 2 * b:2 * b + 2, :], xt_hi[:, 2 * b:2 * b + 2, :], 2 + b, ev("merged_hi"), 4 * l + b + 1, ev("merged_xt"))

                tasks = {"unit": unit, "decay": decays, "gqa_s": gqa_s, "gqa_t": lambda n: None, "gqa_pv": lambda n: None,
                         "gqa_out": gqa_out, "ret_s": ret_s, "ret_pv": lambda n: None, "ret_norm": ret_norm,
                         "ya": lambda n: split_next(U + 19 + n), "yr": lambda n: split_next(U + 21 + n), "merge": merge,
                         "out": lambda n: add_unit(U + 23 + n, Q + 23 + n, n, ALPHA)}
                for name, n in ORDER2:
                    tasks[name](n)
                residual_whole(Q + 27)

            mixer(0)
            norm(3)
            ffn(1, U_FFN2, Q_FFN2, H_FFN2, ALPHA)
            norm(4)
            mixer(1)
            norm(5)
            dve.wait_ge(xt_ready, 4 * 6)
            CP(ms[:, 0:1], ms[:, 1:2]).then_inc(ev("routing"), 1)
            dve.wait_ge(ev("router_hi"), 1)
            TTo(rw_lo[:, :], rw_raw[:, :], rw_hi[:, :].bitcast(F32), ALU.subtract).then_inc(ev("router_split"), 1)
            dve.wait_ge(ev("router_product"), 1)
            link(TTo(logit, ps[:, 2, 0:16].rearrange("p (t n) -> p t n", t=TT), rb.unsqueeze(1).to_broadcast([P, TT, 8]), ALU.add))
            for t in range(TT):
                last = nc.vector.max(top8[:, t, :], logit[:, t, :])
            link(last)
            for t in range(TT):
                last = nc.vector.max_index(idx_u[:, t, :], top8[:, t, :], logit[:, t, :])
            link(last)
            link(CP(idx_f, idx_u[:, :, :]))
            TTo(tw[:, :, 0:1], top8[:, :, 1:2], top8[:, :, 0:1], ALU.subtract).then_inc(ev("top_diff"), 1)
            dve.wait_ge(ev("top_exp"), 1)
            link(TS(tw[:, :, 1:2], tw[:, :, 0:1], 1.0, None, ALU.add))
            link(nc.vector.reciprocal(tw[:, :, 2:3], tw[:, :, 1:2]))
            link(TTo(tw[:, :, 3:4], tw[:, :, 0:1], tw[:, :, 2:3], ALU.mult))
            for t in range(TT):
                for a in range(2):
                    last = TS(gate8[:, a, t, :], table("slot")[:, 0:EXPERTS], idx_f[:, t, a:a + 1], tw[:, t, 2 + a:3 + a], ALU.is_equal, ALU.mult)
            for t in range(TT):
                for a in range(2):
                    last = TS(sel8[:, a, t, :], table("slot")[:, 0:EXPERTS], idx_f[:, t, a:a + 1], None, ALU.is_equal)
            link(last)
            TTo(gate8[:, 0, :, :], gate8[:, 0, :, :], gate8[:, 1, :, :], ALU.add)
            TTo(sel8[:, 0, :, :], sel8[:, 0, :, :], sel8[:, 1, :, :], ALU.add).then_inc(ev("selected"), 1)
            dve.wait_ge(ev("xs_hi"), 1)
            TTo(xs_lo, x[:, :, :], xs_hi.bitcast(F32), ALU.subtract).then_inc(ev("xs_ready"), 1)
            dve.wait_ge(ev("ranked"), 1)
            CP(counts8[:, :], ps[:, 3, 16:24]).then_inc(ev("counts_ready"), 1)
            link(CP(rank8, ps[:, 3, 0:16].rearrange("p (t n) -> p t n", t=TT)))
            for t in range(TT):
                for e in range(EXPERTS):
                    last = TS(pick[:, t, e, :], table("slot"), rank8[:, t, e:e + 1], sel8[:, 0, t, e:e + 1], ALU.is_equal, ALU.mult)
            last.then_inc(ev("picks"), 1)
            dve.wait_ge(ev("picks"), 1)
            CP(pick_r[:, :], pick.rearrange("p t e s -> p (t e s)")).then_inc(ev("pick_r"), 1)
            TS(x[:, :, :], x[:, :, :], ALPHA, None, ALU.mult).then_inc(ev("moe_added"), 1)

            def take_gathered(n):
                dve.wait_ge(ev("xg_hi"), n + 1)
                CP(xg_lo[:, :], ps[:, 4:6, :]).then_inc(ev("xg_ready"), 1)

            take_gathered(0)
            dve.wait_ge(ev("pick_t"), 1)
            pick_flat = pick_t.rearrange("p e t -> p (e t)")
            gates_flat = gate8[:, 0, :, :].rearrange("p t n -> p (t n)")

            def expert(e, dense, last):
                tiles = TT if dense else 1
                u, n = U_MOE + e * PER_EXPERT, e * PAIRS

                def gate_up(i, p):
                    dve.wait_ge(unit_used, u + p + 1)
                    dve.wait_ge(silued, n + i + 1)
                    width, bank, at = (P, 0, P) if i == 5 else (T, 1, 0)
                    src = ps[:, bank, :].rearrange("p (t c) -> p t c", t=TT)[:, 0:tiles, at:at + width]
                    TTo(hid[:, 0:tiles, 0:width], src, silu_t[:, 0:tiles, 0:width], ALU.mult).then_inc(hid_rows, 1)

                def take_hidden(i):
                    dve.wait_ge(hid_hi_m, n + i + 1)
                    js = 1 if i == 5 else 2
                    src = ps[:, 1, :].rearrange("p (j t) -> p j t", j=2)[:, 0:js, 0:tiles * P]
                    TTo(h_lo_t[:, 0:js, 0:tiles * P], src, h_hi_t[:, 0:js, 0:tiles * P].bitcast(F32), ALU.subtract).then_inc(hid_pair, 1)

                def ahead(p):
                    q = p + RING
                    if q < PER_EXPERT or not last:
                        slot = (U_MOE + q) % RING
                        width = 512 if q < PER_EXPERT and EXPERT_UNITS[q][0] in "AB" else UNIT
                        dve.wait_ge(hi_ready, u + q + 1)
                        TTo(w_lo[:, slot, 0:width], raw_moe[q % RAW_MOE][:, 0:width], w_hi[:, slot, 0:width].bitcast(F32),
                            ALU.subtract).then_inc(lo_ready, 1)

                def add():
                    dve.wait_ge(ev("sum_ready"), e + 1)
                    for t in range(TT):
                        v = x[:, t, :].rearrange("p (c n) -> p c n", c=2)
                        last_add = STT(v, ps[:, 2 + 2 * t:4 + 2 * t, :], gates_flat[:, bass.ds(e + t * EXPERTS, 1)], v, ALU.mult, ALU.add)
                    last_add.then_inc(ev("moe_added"), 1)

                if not dense:
                    CP(pick_now[:, :], pick_flat[:, bass.ds(e * T, T)])
                ahead(0)
                gate_up(0, 1)
                take_hidden(0)
                ahead(1)
                for i in range(1, 5):
                    p = 3 * i - 1
                    ahead(p)
                    gate_up(i, p + 2)
                    ahead(p + 1)
                    take_hidden(i)
                    ahead(p + 2)
                gate_up(5, 14)
                ahead(14)
                take_hidden(5)
                if not dense and not last:
                    take_gathered(e + 1)
                ahead(15)
                dve.wait_ge(ev("y_hi"), e + 1)
                if dense:
                    CP(ms[:, 0:1], ms[:, 1:2]).then_inc(ev("y_ready"), 1)
                    add()
                    if not last:
                        take_gathered(e + 1)
                    ahead(16)
                else:
                    TTo(y_lo[:, :], ps[:, 6:8, :].rearrange("p b n -> p (b n)"), y_hi[:, :].bitcast(F32), ALU.subtract).then_inc(ev("y_ready"), 1)
                    ahead(16)
                    add()
                ahead(17)

            def either(e, last=False):
                n = dve.value_load(counts8[0:1, bass.ds(e, 1)], min_val=0, max_val=T)
                with dve.If(n > SLOTS):
                    expert(e, True, last)
                with dve.Else():
                    expert(e, False, last)

            with dve.Fori(0, EXPERTS - 1) as e:
                either(e)
            either(EXPERTS - 1, last=True)
            dve.wait_ge(ev("moe_added"), EXPERTS + 1)
            norm(6, turned=False)

        @block.tensor
        def _(pe):
            MM, TR = nc.tensor.matmul, nc.tensor.transpose

            def product(dst, a_hi, a_lo, b_hi, b_lo, start, stop):
                MM(dst, a_hi, b_hi, start=start, stop=False)
                MM(dst, a_hi, b_lo, start=False, stop=False)
                return MM(dst, a_lo, b_hi, start=False, stop=stop)

            def weights_still(s, col, dst, xh=xt_hi, xl=xt_lo, step=256):
                for k in range(KT):
                    w = slice(k * step + col, k * step + col + P)
                    last = product(dst, w_hi[:, s, w], w_lo[:, s, w], xh[:, k, :], xl[:, k, :], k == 0, k == KT - 1)
                return last

            def tokens_still(s, t, dst, xh=xt_hi, xl=xt_lo, k0=0, nk=KT, step=256, col=0, width=256):
                for k in range(nk):
                    w = slice(k * step + col, k * step + col + width)
                    tok = slice(t * P, (t + 1) * P)
                    last = product(dst, xh[:, k0 + k, tok], xl[:, k0 + k, tok], w_hi[:, s, w], w_lo[:, s, w], k == 0, k == nk - 1)
                return last

            def begin(u, q):
                pe.wait_ge(lo_ready, u + 1)
                if q >= 2:
                    wait_evacuated(pe, q - 2)

            def turn_rows(n, rows):
                pe.wait_ge(rows_ready, 2 * n + 1)
                for k in range(KT):
                    TR(ps[:, 2 + k // 2, k % 2 * T:k % 2 * T + P], rows[:, 0, k * P:(k + 1) * P], ident)
                pe.wait_ge(rows_ready, 2 * n + 2)
                for k in range(KT):
                    last = TR(ps[:, 2 + k // 2, k % 2 * T + P:k % 2 * T + T], rows[:, 1, k * P:(k + 1) * P], ident)
                    if k % 2:
                        last.then_inc(rows_turned, 1)
                pe.wait_ge(xt_ready, 4 * (n + 1))

            def turn_four(src, done):
                for k in range(4):
                    for t in range(TT):
                        last = TR(ps[:, 2 + k // 2, k % 2 * T + t * P:k % 2 * T + (t + 1) * P], src[:, t, k * P:(k + 1) * P], ident)
                    if k % 2:
                        last.then_inc(done, 1)

            pe.wait_ge(consts_landed, 16)
            turn_rows(0, normed)

            def unit1(n):
                s = n % RING
                begin(n, n)
                for c in range(2):
                    dst = ps[:, n % 2, c * 256:(c + 1) * 256]
                    last = weights_still(s, c * P, dst) if IN1[n][0] in "qk" else tokens_still(s, c, dst)
                last.then_inc(unit_used, 1)

            def sb_z(g):
                for q in (2 * g, 2 * g + 1):
                    wait_evacuated(pe, q)
                if g:
                    pe.wait_ge(ev("sb_sum"), g)
                for i in range(4):
                    h = 4 * g + i
                    r = slice(h % 2 * 64, h % 2 * 64 + 64)
                    MM(ps[:, 2 + i, 0:T], kT[r, h // 2, 0:P], qT[r, h // 2, :], start=True, stop=True)
                    last = MM(ps[:, 2 + i, T:384], kT[r, h // 2, P:T], qT[r, h // 2, P:T], start=True, stop=True)
                last.then_inc(ev("sb_z"), 1)

            def sb_cum(g):
                pe.wait_ge(ev("sb_logs"), g + 1)
                for i in range(4):
                    MM(ps[:, 2 + i, 0:P], later, s_b[:, i, 0:P], start=True, stop=True)
                    MM(ps[:, 2 + i, P:T], later, s_b[:, i, P:T], start=True, stop=False)
                    MM(ps[:, 2 + i, P:T], ones, s_b[:, i, T:384], start=False, stop=True)
                    last = MM(ps[:, 2 + i, T:384], later, s_b[:, i, T:384], start=True, stop=True)
                last.then_inc(ev("sb_acc"), 1)

            def sb_pv(g):
                for q in (4, 5):
                    wait_evacuated(pe, q)
                pe.wait_ge(ev("sb_weights"), g + 1)
                for i in range(4):
                    h = 4 * g + i
                    r = slice(h % 2 * 64, h % 2 * 64 + 64)
                    c = i // 2 * 256
                    e = slice(h * 64, h * 64 + 64)
                    MM(ps[r, 6 + g, c:c + P], v_sb[:, 0, e], s_c[:, i, 0:P], start=True, stop=True)
                    MM(ps[r, 6 + g, c + P:c + T], v_sb[:, 0, e], s_c[:, i, P:T], start=True, stop=False)
                    last = MM(ps[r, 6 + g, c + P:c + T], v_sb[:, 1, e], s_c[:, i, T:384], start=False, stop=True)
                last.then_inc(ev("sb_pv"), 1)

            def d_t(_):
                pe.wait_ge(ev("sb_sum"), 2)
                for i in range(2):
                    pe.wait_ge(ev("rotated"), i + 1)
                    v = dqk[i].rearrange("p t h e -> p t (h e)")
                    for h in range(4):
                        for t in range(TT):
                            last = TR(ps[:, 2 + 2 * i + h // 2, h % 2 * T + t * P:h % 2 * T + (t + 1) * P], v[:, t, h * P:(h + 1) * P], ident)
                    last.then_inc(ev("d_turned"), 1)

            def d_s(g):
                pe.wait_ge(ev("d_copied"), 2)
                if g:
                    pe.wait_ge(ev("d_max"), g)
                for c in range(4):
                    h = 2 * g + c // 2
                    r = slice(c % 2 * 64, c % 2 * 64 + 64)
                    MM(ps[:, 2 + c, 0:P], dqkT[0][r, h, 0:P], dqkT[1][r, h, 0:P], start=True, stop=True)
                    last = MM(ps[:, 2 + c, P:384], dqkT[0][r, h, P:T], dqkT[1][r, h, :], start=True, stop=True)
                last.then_inc(ev("d_scores"), 1)

            def d_x(g):
                pe.wait_ge(ev("d_probs"), g + 1)
                if g:
                    pe.wait_ge(ev("d_out_copied"), g)
                else:
                    pe.wait_ge(ev("sb_mt"), 2)
                for i in range(2):
                    for b in range(3):
                        last = TR(ps[:, 6 + i, b * P:(b + 1) * P], s_c[:, i, b * P:(b + 1) * P], ident)
                last.then_inc(ev("d_probs_turned"), 1)

            def d_pv(g):
                for q in (10, 11):
                    wait_evacuated(pe, q)
                pe.wait_ge(ev("d_probsT"), g + 1)
                for i in range(2):
                    e = slice((2 * g + i) * P, (2 * g + i + 1) * P)
                    MM(ps[:, 6, i * P:(i + 1) * P], s_c[:, 2 + i, 0:P], dv[:, 0, e], start=True, stop=True)
                    MM(ps[:, 6, T + i * P:T + (i + 1) * P], s_c[:, 2 + i, P:T], dv[:, 0, e], start=True, stop=False)
                    last = MM(ps[:, 6, T + i * P:T + (i + 1) * P], s_c[:, 2 + i, T:384], dv[:, 1, e], start=False, stop=True)
                last.then_inc(ev("d_product"), 1)

            def d_norm(_):
                pe.wait_ge(ev("d_normed"), 1)
                turn_four(d_out.rearrange("p t h e -> p t (h e)"), ev("d_out_turned"))

            def wo(n):
                u = U_WO + n
                if n == 0:
                    pe.wait_ge(ev("sb_mt"), 2)
                    pe.wait_ge(ev("d_mt"), 2)
                begin(u, 12 + n)
                for t in range(TT):
                    last = tokens_still(u % RING, t, ps[:, (12 + n) % 2, t * 256:(t + 1) * 256], mt_hi, mt_lo)
                last.then_inc(unit_used, 1)

            tasks = {"unit": unit1, "sb_z": sb_z, "sb_cum": sb_cum, "sb_pv": sb_pv, "rot": lambda n: None, "d_t": d_t,
                     "d_s": d_s, "d_x": d_x, "d_pv": d_pv, "d_norm": d_norm, "wo": wo}
            for name, n in ORDER1:
                tasks[name](n)

            def ffn_pair(u, s0, half_q):
                for j in range(2):
                    s, bank = (s0[0] + j) % RING, (s0[1] + j) % 2
                    pe.wait_ge(lo_ready, u + j + 1)
                    pe.wait_ge(evacuated[bank], half_q[j])
                    weights_still(s, 0, ps[:, bank, 0:T], step=P)
                    for k in range(KT):
                        w = slice(1024 + k * P, 1024 + (k + 1) * P)
                        last = product(ps[:, bank, T:2 * T], w_hi[:, s, w], w_lo[:, s, w], xt_hi[:, k, :], xt_lo[:, k, :], k == 0, k == KT - 1)
                    last.then_inc(unit_used, 1)
                s = (s0[0] + 2) % RING
                pe.wait_ge(lo_ready, u + 3)
                for j in range(2):
                    pe.wait_ge(evacuated[(s0[1] + j) % 2], half_q[j] + 1)
                    for t in range(TT):
                        tok = slice(t * P, (t + 1) * P)
                        for c in range(2):
                            w = slice(j * 1024 + c * 512, j * 1024 + (c + 1) * 512)
                            dst = ps[:, 2 + 2 * t + c, :]
                            MM(dst, h_hi_t[:, j, tok], w_hi[:, s, w], start=False, stop=False)
                            MM(dst, h_hi_t[:, j, tok], w_lo[:, s, w], start=False, stop=False)
                            last = MM(dst, h_lo_t[:, j, tok], w_hi[:, s, w], start=False, stop=False)
                last.then_inc(unit_used, 1)

            def clear_acc():
                pe.wait_ge(zeroed, 1)
                for b in range(4):
                    MM(ps[:, 2 + b, :], zeros[:, 0:P], zeros[:, :], start=True, stop=False)

            def close_acc():
                for b in range(4):
                    last = MM(ps[:, 2 + b, :], zeros[:, 0:P], zeros[:, :], start=False, stop=True)
                last.then_inc(acc_done, 1)

            def ffn(u0, q0):
                clear_acc()
                with pe.Fori(0, FT_DENSE // 2) as i:
                    ffn_pair(u0 + i * 3, (u0, q0), [i + (q0 + j) // 2 for j in range(2)])
                close_acc()

            turn_rows(1, normed)
            ffn(U_FFN1, Q_FFN1)
            turn_rows(2, x)

            def mixer(l):
                U, Q = U_MIX[l], Q_MIX[l]

                def unit(n):
                    u, q = U + n, Q + n
                    s = u % RING
                    begin(u, q)
                    if n == 2:
                        weights_still(s, 0, ps[:, q % 2, 0:T])
                        for t in range(TT):
                            last = tokens_still(s, t, ps[:, q % 2, T + t * P:T + (t + 1) * P], col=P, width=P)
                    else:
                        for c in range(2):
                            dst = ps[:, q % 2, c * 256:(c + 1) * 256]
                            last = weights_still(s, c * P, dst) if n in (0, 1, 3, 4) else tokens_still(s, c, dst)
                    last.then_inc(unit_used, 1)

                def gqa_s(g):
                    for q in range(3):
                        wait_evacuated(pe, Q + q)
                    if g:
                        pe.wait_ge(ev("g_probsT"), 2 * l + g)
                    for i in range(4):
                        h = 4 * g + i
                        r = slice(h % 2 * 64, h % 2 * 64 + 64)
                        for t in range(TT):
                            last = MM(ps[:, 2 + i, t * T:(t + 1) * T], qaT[r, h // 2, t * P:(t + 1) * P], kaT[r, h // 4, :], start=True, stop=True)
                    last.then_inc(ev("g_scores"), 1)

                def gqa_t(g):
                    pe.wait_ge(ev("g_exp"), 2 * l + g + 1)
                    for i in range(4):
                        for k in range(2):
                            for t in range(TT):
                                last = TR(ps[:, 2 + i, k * T + t * P:k * T + (t + 1) * P], g_s[:, i, t, k * P:(k + 1) * P], ident)
                    last.then_inc(ev("g_turned"), 1)

                def gqa_pv(g):
                    pe.wait_ge(ev("g_probsT"), 2 * l + g + 1)
                    for i in range(4):
                        h = 4 * g + i
                        for t in range(TT):
                            for k in range(2):
                                last = MM(ps[:, 6 + t, h * 64:(h + 1) * 64], g_t[:, i, k, t * P:(t + 1) * P], va[:, k, g * 64:(g + 1) * 64],
                                          start=k == 0, stop=k == 1)
                    last.then_inc(ev("g_product"), 1)

                def gqa_out(_):
                    pe.wait_ge(ev("attn_rows"), l + 1)
                    turn_four(attn, ev("attn_turned"))

                def ret_s(h):
                    n = 8 * l + h
                    for q in (3, 4):
                        wait_evacuated(pe, Q + q)
                    if h < 2:
                        pe.wait_ge(ev("attn_mt"), 2 * l + 2)
                        pe.wait_ge(ev("decay_ready"), l + 1)
                    else:
                        pe.wait_ge(ev("r_weights"), n - 1)
                    r = slice(h % 4 * 32, h % 4 * 32 + 32)
                    for k in range(2):
                        last = MM(ps[:, 2 + h % 2, k * T:(k + 1) * T], krT[r, h // 4, k * P:(k + 1) * P], qrT[r, h // 4, :], start=True, stop=True)
                    last.then_inc(ev("r_scores"), 1)

                def ret_pv(h):
                    n = 8 * l + h
                    for q in (5, 6):
                        wait_evacuated(pe, Q + q)
                    pe.wait_ge(ev("r_weights"), n + 1)
                    e = slice(h * 64, h * 64 + 64)
                    w = r_w[:, h % 2, :, :]
                    for way in range(2):
                        near, far = way, 1 - way
                        own = slice(near * P, near * P + P)
                        both = slice(far * P, far * P + P)
                        MM(ps[:, 4 + 2 * way + near, e], w[:, way, own], vr[:, near, e], start=True, stop=True)
                        MM(ps[:, 4 + 2 * way + far, e], w[:, way, both], vr[:, near, e], start=True, stop=False)
                        last = MM(ps[:, 4 + 2 * way + far, e], w[:, way, T:384], vr[:, far, e], start=False, stop=True)
                    last.then_inc(ev("r_product"), 1)

                def ret_norm(_):
                    pe.wait_ge(ev("ret_rows"), l + 1)
                    turn_four(sg[:, 0, :, :], ev("ret_turned"))

                def half_product(n):
                    u, q = U + 19 + n, Q + 19 + n
                    if n == 0:
                        pe.wait_ge(ev("attn_mt"), 2 * l + 2)
                    if n == 2:
                        pe.wait_ge(ev("ret_mt"), 2 * l + 2)
                    begin(u, q)
                    wait_evacuated(pe, q - 1)
                    for t in range(TT):
                        last = tokens_still(u % RING, t, ps[:, t, :], mt_hi, mt_lo, k0=n // 2 * 4, nk=4, step=512, width=512)
                    last.then_inc(unit_used, 1)

                def merge(_):
                    for t in range(TT):
                        pe.wait_ge(ev("merged_rows"), 2 * l + t + 1)
                        for k in range(KT):
                            last = TR(ps[:, 2 + k // 2, k % 2 * T + t * P:k % 2 * T + (t + 1) * P], merged[:, t, k * P:(k + 1) * P], ident)
                            if t and k % 2:
                                last.then_inc(ev("merged_turned"), 1)

                def out_unit(n):
                    u, q = U + 23 + n, Q + 23 + n
                    if n == 0:
                        pe.wait_ge(ev("merged_xt"), 4 * l + 4)
                    begin(u, q)
                    for t in range(TT):
                        last = tokens_still(u % RING, t, ps[:, q % 2, t * 256:(t + 1) * 256])
                    last.then_inc(unit_used, 1)

                tasks = {"unit": unit, "decay": lambda n: None, "gqa_s": gqa_s, "gqa_t": gqa_t, "gqa_pv": gqa_pv,
                         "gqa_out": gqa_out, "ret_s": ret_s, "ret_pv": ret_pv, "ret_norm": ret_norm,
                         "ya": half_product, "yr": lambda n: half_product(2 + n), "merge": merge, "out": out_unit}
                for name, n in ORDER2:
                    tasks[name](n)

            mixer(0)
            turn_rows(3, x)
            ffn(U_FFN2, Q_FFN2)
            turn_rows(4, x)
            mixer(1)
            turn_rows(5, x)
            pe.wait_ge(ev("router_split"), 1)
            for t in range(TT):
                tok = slice(t * P, (t + 1) * P)
                for k in range(KT):
                    w = slice(k * 8, k * 8 + 8)
                    last = product(ps[:, 2, t * 8:t * 8 + 8], xt_hi[:, k, tok], xt_lo[:, k, tok], rw_hi[:, w], rw_lo[:, w], k == 0, k == KT - 1)
            last.then_inc(ev("router_product"), 1)
            pe.wait_ge(ev("selected"), 1)
            first, second = sel8[:, 0, 0, :], sel8[:, 0, 1, :]
            MM(ps[:, 3, 0:8], past, first, start=True, stop=True)
            MM(ps[:, 3, 8:16], past, second, start=True, stop=False)
            MM(ps[:, 3, 8:16], ones, first, start=False, stop=True)
            MM(ps[:, 3, 16:24], ones, first, start=True, stop=False)
            MM(ps[:, 3, 16:24], ones, second, start=False, stop=True).then_inc(ev("ranked"), 1)
            pe.wait_ge(ev("picks"), 1)
            for e in range(EXPERTS):
                for t in range(TT):
                    last = TR(ps[:, 2 + e // 2, e % 2 * T + t * P:e % 2 * T + (t + 1) * P], pick[:, t, e, :], ident)
            last.then_inc(ev("pick_turned"), 1)
            pick_cols = pick_r[:, :]

            def gather(e):
                for part, src in ((0, xs_hi), (1, xs_lo)):
                    for k in range(KT):
                        dst = ps[:, 2 + 2 * part + k // 4, k % 4 * P:k % 4 * P + P]
                        for t in range(TT):
                            last = MM(dst, src[:, t, k * P:(k + 1) * P], pick_cols[:, bass.ds(e * P + t * EXPERTS * P, P)],
                                      start=t == 0, stop=t == 1)
                last.then_inc(ev("gathered"), 1)

            pe.wait_ge(ev("pick_t"), 1)
            pe.wait_ge(ev("pick_r"), 1)
            pe.wait_ge(ev("xs_ready"), 1)
            gather(0)
            pe.wait_ge(ev("counts_ready"), 1)
            pe.wait_ge(ev("xg_ready"), 1)
            xg = [v[:, :].rearrange("p (k s) -> p k s", k=KT) for v in (xg_hi, xg_lo)]

            def expert(e, dense, last_one):
                xh, xl, tiles = (xt_hi, xt_lo, TT) if dense else (*xg, 1)
                u, n = U_MOE + e * PER_EXPERT, e * PAIRS
                sums = [(t, c, 2 + 2 * t + c) for t in range(TT) for c in range(2)] if dense else [(0, c, 6 + c) for c in range(2)]

                def rows(p, bank, halfway=None):
                    s = (U_MOE + p) % RING
                    kind = EXPERT_UNITS[p][0]
                    if kind == "M":
                        w = [v[:, s, :].rearrange("p (a k n) -> p k a n", a=2, k=KT) for v in (w_hi, w_lo)]
                    else:
                        w = [v[:, s, :].rearrange("p (k n) -> p k n", k=KT) for v in (w_hi, w_lo)]
                    pe.wait_ge(lo_ready, u + p + 1)
                    for t in range(tiles):
                        dst = ps[:, bank, t * T:(t + 1) * T]
                        if kind == "M":
                            dst = dst.rearrange("p (a n) -> p a n", a=2)
                        tok = slice(t * P, (t + 1) * P)
                        for k in range(KT):
                            last = product(dst, xh[:, k, tok], xl[:, k, tok], w[0][:, k], w[1][:, k], k == 0, k == KT - 1)
                            if t == 0 and k == 3 and halfway is not None:
                                halfway()
                    last.then_inc(unit_used, 1)

                def turn_hidden(i):
                    pe.wait_ge(hid_rows, n + i + 1)
                    for j in range(1 if i == 5 else 2):
                        for t in range(tiles):
                            last = TR(ps[:, 1, j * T + t * P:j * T + (t + 1) * P], hid[:, t, j * P:(j + 1) * P], ident)
                    last.then_inc(hid_turned, 1)

                def down(j, p, at, c_of=None):
                    s = (U_MOE + p) % RING
                    for t, c, bank in sums:
                        if c_of in (None, c):
                            tok = slice(t * P, (t + 1) * P)
                            w = slice(at, at + 512) if c_of is not None else slice(at + c * 512, at + (c + 1) * 512)
                            last = product(ps[:, bank, :], h_hi_t[:, j, tok], h_lo_t[:, j, tok], w_hi[:, s, w], w_lo[:, s, w], False, False)
                    return last

                def down_pair(i, p):
                    pe.wait_ge(lo_ready, u + p + 1)
                    pe.wait_ge(hid_pair, n + i + 1)
                    down(0, p, 0)
                    down(1, p, 1024).then_inc(unit_used, 1)

                if dense:
                    pe.wait_ge(ev("moe_added"), e + 1)
                for _, _, bank in sums:
                    MM(ps[:, bank, :], zeros[:, 0:P], zeros[:, :], start=True, stop=False)
                rows(0, 0)
                rows(1, 1)
                for i in range(1, 5):
                    p = 3 * i - 1
                    pe.wait_ge(silued, n + i)
                    rows(p, 0, lambda: turn_hidden(i - 1))
                    down_pair(i - 1, p + 1)
                    rows(p + 2, 1)
                pe.wait_ge(silued, n + 5)
                rows(14, 0, lambda: turn_hidden(4))
                down_pair(4, 15)
                turn_hidden(5)
                if not dense:
                    pe.wait_ge(ev("moe_added"), e + 1)
                    if not last_one:
                        gather(e + 1)
                pe.wait_ge(hid_pair, n + 6)
                for c in range(2):
                    pe.wait_ge(lo_ready, u + 17 + c)
                    down(0, 16 + c, 0, c).then_inc(unit_used, 1)
                for n, (_, _, bank) in enumerate(sums):
                    last = MM(ps[:, bank, :], zeros[:, 0:P], zeros[:, :], start=False, stop=True)
                    if n == (0 if dense else 1):
                        last.then_inc(ev("y_done"), 1)
                if dense:
                    last.then_inc(ev("sum_ready"), 1)
                if dense and not last_one:
                    pe.wait_ge(ev("moe_added"), e + 2)
                    gather(e + 1)
                    pe.wait_ge(ev("xg_ready"), e + 2)
                if not dense:
                    if not last_one:
                        pe.wait_ge(ev("xg_ready"), e + 2)
                    pe.wait_ge(ev("y_ready"), e + 1)
                    for t in range(TT):
                        for c in range(2):
                            tok, w = slice(t * P, (t + 1) * P), slice(c * 512, (c + 1) * 512)
                            MM(ps[:, 2 + 2 * t + c, :], pick_now[:, tok], y_hi[:, w], start=True, stop=False)
                            last = MM(ps[:, 2 + 2 * t + c, :], pick_now[:, tok], y_lo[:, w], start=False, stop=True)
                    last.then_inc(ev("sum_ready"), 1)

            def either(e, last=False):
                n = pe.value_load(counts8[0:1, bass.ds(e, 1)], min_val=0, max_val=T)
                with pe.If(n > SLOTS):
                    expert(e, True, last)
                with pe.Else():
                    expert(e, False, last)

            with pe.Fori(0, EXPERTS - 1) as e:
                either(e)
            either(EXPERTS - 1, last=True)


_INS = ["x", "attn_norm_g", "w_in", "diff_q_norm_g", "diff_k_norm_g", "lambda_q1", "lambda_k1", "lambda_q2",
        "lambda_k2", "diff_subln_g", "w_o", "ffn_norm_g", "w_gate", "w_up", "w_down", "ln_emb_g_2", "ln_emb_b_2",
        "w_in_2", "b_gate_2", "sink_logits_2", "decay_fwd_2", "decay_bwd_2", "w_o_attn_2", "w_o_ret_2", "w_out_2",
        "ln1_g_2", "ln1_b_2", "ffn_w1_2", "ffn_w3_2", "ffn_w2_2", "router_w_2", "router_b_2", "moe_w1_2", "moe_w3_2",
        "moe_w2_2", "ln2_g_2", "ln2_b_2"]


def kernel(**inputs):
    import numpy as _np
    import concourse.bacc as _bacc
    from concourse.bass_utils import run_bass_kernel_spmd as _run

    nc = _bacc.Bacc("TRN2", target_bir_lowering=False, num_devices=1)
    arrays, aps = {}, {}
    for name in _INS:
        a = _np.ascontiguousarray(inputs[name])
        arrays[f"in_{name}_dram"] = a
        aps[name] = nc.dram_tensor(f"in_{name}_dram", a.shape, mybir.dt.from_np(a.dtype), kind="ExternalInput").ap()
    arrays["const_dram"] = CONST_TABLE
    const = nc.dram_tensor("const_dram", CONST_TABLE.shape, F32, kind="ExternalInput").ap()
    out = nc.dram_tensor("out_dram", (1, T, D), F32, kind="ExternalOutput").ap()
    two_blocks(nc, aps, const, out)
    r = _run(nc, [arrays], core_ids=[0])
    return r.results[0]["out_dram"]
```

```python
import math
from contextlib import ExitStack

import numpy as np

import concourse.bass as bass
from concourse import mybir

F32 = mybir.dt.float32
F32R = mybir.dt.float32r
U32 = mybir.dt.uint32
ALU = mybir.AluOpType
ACT = mybir.ActivationFunctionType
AX = mybir.AxisListType

P = 128
T = 256
TT = T // P
D = 1024
KT = D // P
F_DENSE = 2816
F_EXPERT = 1408
EXPERTS = 8
SLOTS = P
FT_DENSE = F_DENSE // P
FT_EXPERT = F_EXPERT // P
RING = 3
UNIT = 2048
BIG = 1.0e30
SCALE = 64 ** -0.5
RMS_EPS, SUBLN_EPS, LN_EPS = 1e-6, 1e-5, 1e-5
LAMBDA_INIT = 0.8 - 0.6 * math.exp(-0.3 * 0)
ALPHA = 4 ** 0.25
SLOPES = [2.0 ** (-8.0 * (h + 1) / 8) for h in range(8)]

U_IN1, U_WO = 0, 12
U_FFN1 = U_WO + 4
U_MIX = [U_FFN1 + 33, U_FFN1 + 33 + 27 + 33]
U_FFN2 = U_MIX[0] + 27
U_MOE = U_MIX[1] + 27
EXPERT_UNITS = [("G", 0), ("U", 0)] + [x for i in range(1, 5) for x in (("G", i), ("D", i - 1), ("U", i))] + \
    [("M", 5), ("D", 4), ("A", 5), ("B", 5)]
PER_EXPERT = len(EXPERT_UNITS)
RAW_MOE = 2 * RING
PAIRS = 6
U_END = U_MOE + PER_EXPERT * EXPERTS
Q_FFN1 = 16
Q_MIX = [Q_FFN1 + 22, Q_FFN1 + 22 + 27 + 22]
Q_FFN2 = Q_MIX[0] + 27
Q_MOE = Q_MIX[1] + 27
H_FFN1, H_FFN2, H_MOE = 0, 22, 44

IN1 = [("q", 0), ("k", 512), ("q", 256), ("k", 768), ("v", 1024), ("v", 1280),
       ("dq", 1536), ("dq", 1792), ("dk", 2048), ("dk", 2304), ("dv", 2560), ("dv", 2816)]
HAS = {kind: [n for n, (k, _) in enumerate(IN1) if k == kind] for kind, _ in IN1}
ORDER1 = [("unit", 0), ("unit", 1), ("sb_z", 0), ("unit", 2), ("unit", 3), ("unit", 4), ("sb_cum", 0),
          ("unit", 5), ("unit", 6), ("sb_pv", 0), ("sb_z", 1), ("unit", 7), ("unit", 8),
          ("sb_cum", 1), ("rot", 0), ("unit", 9), ("sb_pv", 1), ("rot", 1), ("unit", 10), ("unit", 11), ("d_t", 0), ("d_s", 0),
          ("d_s", 1), ("wo_half", 0), ("d_p", 0), ("d_x", 0), ("d_p", 1), ("d_pv", 0), ("d_x", 1), ("d_pv", 1),
          ("d_rows", 0), ("wo_half", 1), ("d_norm", 0),
          ("wo", 0), ("wo", 1), ("wo", 2), ("wo", 3)]
ORDER2 = [("unit", 0), ("unit", 1), ("log_decay", 0), ("unit", 2), ("gqa_s", 0), ("unit", 3), ("unit", 4),
          ("gqa_t", 0), ("unit", 5), ("decay", 3), ("unit", 6), ("gqa_s", 1), ("gqa_pv", 0), ("unit", 7), ("unit", 8),
          ("gqa_t", 1), ("unit", 9), ("unit", 10), ("gqa_pv", 1), ("gqa_rows", 0), ("unit", 11), ("gqa_out", 0),
          ("decay", 0), ("unit", 12), ("ret_s", 0), ("decay", 1), ("ret_s", 1), ("unit", 13), ("ret_pv", 0), ("ret_s", 2),
          ("decay", 2), ("unit", 14), ("ret_pv", 1), ("ret_s", 3), ("unit", 15), ("ret_pv", 2), ("ret_s", 4),
          ("sigmoid", 0), ("ret_pv", 3), ("ret_mean", 0), ("unit", 16), ("ret_var", 0), ("ret_s", 5), ("ret_pv", 4),
          ("unit", 17), ("ret_norm", 0), ("ret_s", 6), ("ret_pv", 5), ("ret_s", 7), ("unit", 18), ("ret_pv", 6),
          ("sigmoid", 1), ("ret_pv", 7), ("ret_mean", 1), ("ret_t", 0), ("ret_var", 1), ("ret_norm", 1), ("ya", 0), ("ya", 1),
          ("ya_out", 0), ("ret_t", 1), ("next", 19), ("ya_out", 1), ("next", 20), ("yr", 0), ("next", 21), ("yr", 1),
          ("merge", 0), ("merge", 1), ("next", 22), ("out", 0), ("out", 1), ("out", 2), ("out", 3)]

CONSTS = {}


def constants():
    p = np.arange(P, dtype=np.float32)[:, None]
    c = np.arange(P, dtype=np.float32)[None, :]
    i = np.arange(T, dtype=np.float32)[None, :]
    parts = {
        "ident": (p == c),
        "later": (p > c),
        "ones": np.ones((P, P)),
        "past": (p < c),
        "causal": np.where(c <= p, 0.0, -BIG),
    }
    inv = (np.float32(10000.0) ** (-np.arange(32, dtype=np.float32) / np.float32(32))).astype(np.float32)
    ang = (np.arange(T, dtype=np.float32)[:, None] * inv[None, :]).astype(np.float32)
    cos, sin = np.cos(ang), np.sin(ang)
    rows = lambda a: a.reshape(TT, P, 64).transpose(1, 0, 2).reshape(P, TT * 64)
    parts["cos"] = rows(np.concatenate([cos, cos], 1))
    parts["sin"] = rows(np.concatenate([-sin, sin], 1))
    dist = [np.where(np.abs(t * P + p - i) <= 128, np.abs(t * P + p - i), BIG) for t in range(TT)]
    parts["dist"] = np.concatenate(dist, 1)
    parts["ahead"] = np.concatenate([np.maximum(i - p, 0), np.maximum(P + p - i, 0)], 1)
    parts["ahead_on"] = np.concatenate([i >= p, i < P + p], 1)
    parts["slot"] = np.broadcast_to(c, (P, P))
    at = 0
    for name, a in parts.items():
        CONSTS[name] = (at, a.shape[1])
        at += a.shape[1]
    return np.ascontiguousarray(np.concatenate([np.asarray(a, np.float32) for a in parts.values()], 1))


CONST_TABLE = constants()


def two_blocks(nc, A, const_dram, out):
    with ExitStack() as ctx:
        def sb(name, shape, dt=F32):
            return ctx.enter_context(nc.sbuf_tensor(name, shape, dt))

        def sem(name):
            return ctx.enter_context(nc.semaphore(name))

        raw = sb("raw", [P, RING, UNIT])
        w_hi = sb("w_hi", [P, RING, UNIT], F32R)
        w_lo = sb("w_lo", [P, RING, UNIT], F32R)
        xt_hi = sb("xt_hi", [P, KT, T], F32R)
        xt_lo = sb("xt_lo", [P, KT, T], F32R)
        mt_hi = sb("mt_hi", [P, KT, T], F32R)
        mt_lo = sb("mt_lo", [P, KT, T], F32R)
        h_hi_t = sb("h_hi_t", [P, 2, T], F32R)
        h_lo_t = sb("h_lo_t", [P, 2, T], F32R)
        zeros = sb("zeros", [P, 512], F32R)
        x = sb("x", [P, TT, D])
        gb = sb("gb", [P, 2, D])
        const = sb("const", list(CONST_TABLE.shape))
        small = sb("small", [P, 768])
        scr_at = nc.sbuf_base + (-nc.sbuf_base) % 32
        scr = sb("scr", [P, 16896])
        ps = ctx.enter_context(nc.psum_tensor("ps", [P, 8, 512], F32))

        def table(name):
            at, n = CONSTS[name]
            return const[:, at:at + n]

        ident, later, ones, past, causal = (table(n) for n in ("ident", "later", "ones", "past", "causal"))

        def area(at, *dims):
            n = int(np.prod(dims))
            v = scr[:, at:at + n]
            if len(dims) == 1:
                return v
            names = "abcd"[:len(dims)]
            return v.rearrange(f"p ({' '.join(names)}) -> p {' '.join(names)}",
                               **{names[i]: d for i, d in enumerate(dims)})

        def tiny(at, n):
            return small[:, at:at + n]

        xs_hi = mt_hi[:, :, :].rearrange("p k t -> p (k t)").rearrange("p (t d) -> p t d", t=TT)
        xs_lo = mt_lo[:, :, :].rearrange("p k t -> p (k t)").rearrange("p (t d) -> p t d", t=TT)
        qT, kT, v_sb = area(0, 4, T), area(1024, 4, T), area(2048, TT, 512)
        dqk = [area(3072, TT, 8, 64), area(4096, TT, 8, 64)]
        dv = area(5120, TT, 512)
        dqkT = [area(6144, 4, T), area(7168, 4, T)]
        s_a, s_b, s_c = area(8192, 4, 384), area(9728, 4, 384), area(11264, 4, 384)
        rt = area(12800, TT, 8, 64)
        d_out = area(13824, TT, 4, P)
        normed = area(14848, TT, D)
        d_a, d_e = [s_a, area(3072, 4, 384)], [s_b, area(14848, 4, 384)]
        silu_t, hid = area(4096, 2, T), area(4608, 2, T)
        pick_t = area(2048, EXPERTS, T)

        def over_scr(name, at, n):
            return nc.alloc_sbuf_tensor_at(name, [P, n], F32R, offset=scr_at + 4 * at)

        raw_moe = [raw[:, (U_MOE + k) % RING, :] for k in range(RING)] + [area(at, UNIT) for at in (11520, 13568, 0)]
        pick_r = over_scr("pick_r", 5120, 2048)
        pick = pick_r[:, :].rearrange("p (t e s) -> p t e s", t=TT, e=EXPERTS)
        xg_hi = over_scr("xg_hi", 7168, 1024)
        xg_lo = over_scr("xg_lo", 8192, 1024)
        pick_now = over_scr("pick_now", 9216, 256)
        y_hi = over_scr("y_hi", 9472, 1024)
        y_lo = over_scr("y_lo", 10496, 1024)
        qaT, kaT, va = area(0, 4, T), area(1024, 2, T), area(1536, TT, P)
        qrT, krT, vr = area(1792, 2, T), area(2304, 2, T), area(2816, TT, 512)
        sg = area(3840, 2, TT, 512)
        gates = area(5888, TT, 2048)
        decay = area(9984, 8, 2, T)
        b_rows = area(14080, 2, T)
        g_s, g_t = area(14592, 4, TT, T), area(9984, 4, TT, T)
        r_w = area(14592, 2, 2, 384)
        y_n = [area(9984, 2 * TT, 4, 64), area(14592, 2 * TT, 4, 64)]
        y_sq = [area(11008, 2 * TT, 4, 64), area(15616, 2 * TT, 4, 64)]
        attn = area(12032, TT, 512)
        y_mix = area(9984, 2, TT, D)
        merged = area(0, TT, D)

        stats = tiny(0, 24).rearrange("p (t c s) -> p t c s", t=TT, c=2)
        mv = tiny(24, 4).rearrange("p (t s) -> p t s", t=TT)
        ms = tiny(28, 2)
        rstd = tiny(30, 2)
        ss = tiny(32, 32)
        rs = tiny(64, 32)
        lam4 = tiny(96, 256).rearrange("p (v e) -> p v e", v=4)
        lam2 = tiny(352, 2)
        lam = tiny(354, 1)
        mx, nm, sums, rec = tiny(356, 8), tiny(364, 8), tiny(372, 8), tiny(380, 8)
        d_mx, d_nm, d_sums, d_rec = [mx, tiny(732, 8)], [nm, tiny(740, 8)], [sums, tiny(748, 8)], [rec, tiny(756, 8)]
        rec_all = tiny(388, 16)
        sink = tiny(404, 8)
        lg = tiny(412, 16)
        lg_t = tiny(428, 48).rearrange("p (a n) -> p a n", a=3)
        gq = tiny(476, 128).rearrange("p (a n) -> p a n", a=2)
        gsub = tiny(604, 128)
        top8 = tiny(96, 16).rearrange("p (t n) -> p t n", t=TT)
        logit = tiny(112, 16).rearrange("p (t n) -> p t n", t=TT)
        tw = tiny(128, 8).rearrange("p (t n) -> p t n", t=TT)
        idx_f = tiny(136, 16).rearrange("p (t n) -> p t n", t=TT)
        gate8 = tiny(152, 32).rearrange("p (a t n) -> p a t n", a=2, t=TT)
        sel8 = tiny(192, 32).rearrange("p (a t n) -> p a t n", a=2, t=TT)
        rank8 = tiny(224, 16).rearrange("p (t n) -> p t n", t=TT)
        counts8 = sb("counts8", [P, EXPERTS], mybir.dt.int32)
        idx_u = sb("idx_u", [P, TT, 8], U32)
        rw_hi = sb("rw_hi", [P, KT * 8], F32R)
        rw_lo = sb("rw_lo", [P, KT * 8], F32R)
        rw_raw = sb("rw_raw", [P, KT * 8])
        rb = tiny(184, 8)
        logit_t = sb("logit_t", [EXPERTS, T])
        spare = tiny(764, 1)

        raw_landed = [sem(f"raw_landed{i}") for i in range(RING)]
        raw_moe_landed = [raw_landed[(U_MOE + k) % RING] for k in range(RING)] + [sem(f"raw_moe_landed{i}") for i in range(RING)]
        hi_ready, lo_ready, unit_used = sem("hi_ready"), sem("lo_ready"), sem("unit_used")
        evacuated = [sem("evacuated0"), sem("evacuated1")]
        silu_ready, hid_ready, hid_hi = sem("silu_ready"), sem("hid_ready"), sem("hid_hi")
        acc_done = sem("acc_done")
        silued, hid_rows, hid_turned = sem("silued"), sem("hid_rows"), sem("hid_turned")
        hid_hi_m, hid_pair = sem("hid_hi_m"), sem("hid_pair")
        act_step, dve_step, pool_step = sem("act_step"), sem("dve_step"), sem("pool_step")
        x_landed = [sem(f"x_landed{t}") for t in range(TT)]
        consts_landed, small1_landed = sem("consts_landed"), sem("small1_landed")
        gb_landed, gb_used = sem("gb_landed"), sem("gb_used")
        var_ready, rstd_ready = sem("var_ready"), sem("rstd_ready")
        rows_ready, rows_turned, xt_hi_ready, xt_ready = sem("rows_ready"), sem("rows_turned"), sem("xt_hi_ready"), sem("xt_ready")
        zeroed = sem("zeroed")
        stored = sem("stored")
        S = {}

        def ev(name):
            if name not in S:
                S[name] = sem(name)
            return S[name]

        block = ctx.enter_context(nc.Block())

        class Chain:
            def __init__(self, engine, step):
                self.engine, self.step, self.n = engine, step, 0

            def __call__(self, ins):
                self.n += 1
                ins.then_inc(self.step, 1)
                self.engine.wait_ge(self.step, self.n)

        def wait_evacuated(eng, q):
            eng.wait_ge(evacuated[q % 2], q // 2 + 1)

        def k_major(w):
            return w.rearrange("(k p) n -> p k n", p=P)

        @block.sync
        def _(sp):
            for t in range(TT):
                sp.dma_start(x[:, t, :], A["x"][0, t * P:(t + 1) * P, :]).then_inc(x_landed[t], 16)
            sp.dma_start(ident, const_dram[:, 0:P]).then_inc(ev("ident_landed"), 16)

            def load(u, slot, first, second, width=1024):
                if not (isinstance(u, int) and u < RING):
                    sp.wait_ge(lo_ready, u - RING + 1)
                fill(raw[:, slot, :], raw_landed[slot], first, second, width)

            def fill(place, landed, first, second, width):
                for half, src in ((0, first), (1, second)):
                    dst = place[:, half * width:(half + 1) * width]
                    if len(src.shape) == 3:
                        dst = dst.rearrange("p (k n) -> p k n", k=src.shape[1])
                    elif len(src.shape) == 4:
                        dst = dst.rearrange("p (e k n) -> p e k n", e=src.shape[1], k=src.shape[2])
                    sp.dma_start(dst, src).then_inc(landed, 16)

            def load_square(u, w, c):
                v = k_major(w)
                load(u, u % RING, v[:, 0:4, c:c + 256], v[:, 4:8, c:c + 256])

            def load_short(u, w, c):
                v = k_major(w)
                load(u, u % RING, v[:, 0:2, c:c + 512], v[:, 2:4, c:c + 512])

            def load_ffn(u0, wg, wu, wd):
                gv, uv = k_major(wg), k_major(wu)
                with sp.Fori(0, FT_DENSE // 2) as i:
                    for j in range(2):
                        c = bass.ds(i * 256 + j * P, P)
                        load(u0 + j + i * 3, (u0 + j) % RING, gv[:, :, c], uv[:, :, c])
                    load(u0 + 2 + i * 3, (u0 + 2) % RING, wd[bass.ds(i * 256, P), :], wd[bass.ds(i * 256 + P, P), :])

            for n, (_, c) in enumerate(IN1):
                load_square(U_IN1 + n, A["w_in"][0], c)
            for n in range(4):
                load_square(U_WO + n, A["w_o"][0], n * 256)
            load_ffn(U_FFN1, A["w_gate"][0], A["w_up"][0], A["w_down"][0])
            for l in range(2):
                for n in range(19):
                    load_square(U_MIX[l] + n, A["w_in_2"][l], n * 256)
                for n in range(2):
                    load_short(U_MIX[l] + 19 + n, A["w_o_attn_2"][l], n * 512)
                for n in range(2):
                    load_short(U_MIX[l] + 21 + n, A["w_o_ret_2"][l], n * 512)
                for n in range(4):
                    load_square(U_MIX[l] + 23 + n, A["w_out_2"][l], n * 256)
                if l == 0:
                    load_ffn(U_FFN2, A["ffn_w1_2"][0], A["ffn_w3_2"][0], A["ffn_w2_2"][0])
            w1 = A["moe_w1_2"][0].rearrange("e (k p) n -> p e k n", p=P)
            w3 = A["moe_w3_2"][0].rearrange("e (k p) n -> p e k n", p=P)
            w2 = A["moe_w2_2"][0].rearrange("e f d -> (e f) d")

            def load_expert(e, first=False):
                own = (slice(None), bass.ds(e, 1))
                for p, (kind, i) in enumerate(EXPERT_UNITS):
                    slot = p % RAW_MOE
                    if not (first and p < RAW_MOE):
                        sp.wait_ge(lo_ready, U_MOE + e * PER_EXPERT + p - RAW_MOE + 1)
                    elif p < RING:
                        sp.wait_ge(lo_ready, U_MOE + p - RING + 1)
                    elif p == RING:
                        sp.wait_ge(ev("routing"), 1)
                    width = 1024
                    if kind in "GU":
                        w, c = (w1, w3)[kind == "U"], slice(i * 256, (i + 1) * 256)
                        halves = w[own + (slice(0, 4), c)], w[own + (slice(4, 8), c)]
                    elif kind == "M":
                        c = slice(1280, F_EXPERT)
                        halves = w1[own + (slice(None), c)], w3[own + (slice(None), c)]
                    elif kind == "D":
                        row = e * F_EXPERT + i * 256
                        halves = w2[bass.ds(row, P), :], w2[bass.ds(row + P, P), :]
                    else:
                        row, c, width = w2[bass.ds(e * F_EXPERT + 1280, P), :], 512 * (kind == "B"), 256
                        halves = row[:, c:c + 256], row[:, c + 256:c + 512]
                    fill(raw_moe[slot], raw_moe_landed[slot], *halves, width)

            load_expert(0, first=True)
            with sp.Fori(1, EXPERTS) as e:
                load_expert(e)
            for t in range(TT):
                sp.wait_ge(rows_ready, 2 * 6 + t + 1)
                sp.dma_start(out[0, t * P:(t + 1) * P, :], x[:, t, :]).then_inc(stored, 16)
            sp.wait_ge(stored, 16 * TT)

        @block.gpsimd
        def _(pool):
            def row(v, n):
                return v.rearrange("(a n) -> a n", a=1).partition_broadcast(P) if len(v.shape) == 1 else v.partition_broadcast(P)

            norms = [(A["attn_norm_g"][0], None), (A["ffn_norm_g"][0], None),
                     (A["ln_emb_g_2"], A["ln_emb_b_2"]),
                     (A["ln1_g_2"][0], A["ln1_b_2"][0]), (A["ln2_g_2"][0], A["ln2_b_2"][0]),
                     (A["ln1_g_2"][1], A["ln1_b_2"][1]), (A["ln2_g_2"][1], A["ln2_b_2"][1])]

            def load_norm(n):
                if n:
                    pool.wait_ge(gb_used, n)
                for i, v in enumerate(norms[n]):
                    if v is not None:
                        pool.dma_start(gb[:, i, :], row(v, D)).then_inc(gb_landed, 16)

            load_norm(0)
            pool.memset(zeros[:, :].bitcast(F32), 0.0).then_inc(zeroed, 1)
            pool.dma_start(const[:, P:], const_dram[:, P:]).then_inc(consts_landed, 16)
            for i, name in enumerate(("lambda_q1", "lambda_k1", "lambda_q2", "lambda_k2")):
                pool.dma_start(lam4[:, i, :], row(A[name][0], 64)).then_inc(small1_landed, 16)
            pool.dma_start(gq[:, 0, :], row(A["diff_q_norm_g"][0], 64)).then_inc(small1_landed, 16)
            pool.dma_start(gq[:, 1, :], row(A["diff_k_norm_g"][0], 64)).then_inc(small1_landed, 16)
            pool.dma_start(gsub, row(A["diff_subln_g"][0], P)).then_inc(small1_landed, 16)
            load_norm(1)
            load_norm(2)
            for l in range(2):
                pool.wait_ge(rows_ready, 2 * (2 + 2 * l) + 2)
                pool.dma_start(sink, row(A["sink_logits_2"][l], 8)).then_inc(ev("mix_small"), 16)
                pool.dma_start(lg_t[:, 0, 0:8], row(A["decay_fwd_2"][l], 8)).then_inc(ev("mix_small"), 16)
                pool.dma_start(lg_t[:, 0, 8:16], row(A["decay_bwd_2"][l], 8)).then_inc(ev("mix_small"), 16)
                load_norm(3 + 2 * l)
                if l == 0:
                    pool.dma_start(rw_raw[:, :].rearrange("p (k n) -> p k n", n=8), k_major(A["router_w_2"][0])).then_inc(ev("router_landed"), 16)
                    pool.dma_start(rb, row(A["router_b_2"][0], 8)).then_inc(ev("router_landed"), 16)
                for n in range(8):
                    if n >= 2:
                        wait_evacuated(pool, Q_MIX[l] + 11 + n - 2)
                    pool.dma_start(b_rows[:, n % 2, :], row(A["b_gate_2"][l, n * 256:(n + 1) * 256], 256)).then_inc(ev(f"b_row{n % 2}"), 16)
                load_norm(4 + 2 * l)

        @block.scalar
        def _(act):
            link = Chain(act, act_step)
            A_ = nc.scalar.activation

            def split_hi(u, slot, count):
                act.wait_ge(raw_landed[slot], count * 32)
                if not (isinstance(u, int) and u < RING):
                    act.wait_ge(unit_used, u - RING + 1)
                A_(w_hi[:, slot, :], raw[:, slot, :], ACT.Copy).then_inc(hi_ready, 1)

            def split_next(u):
                if u + RING < U_END:
                    split_hi(u + RING, u % RING, (u + RING) // RING + 1)

            def evac(u, q, dst, src, func=ACT.Copy):
                act.wait_ge(unit_used, u + 1)
                A_(dst, src, func).then_inc(evacuated[q % 2], 1)

            def fetch_table(func):
                A_(spare, table("ones")[:, 0:1], func)

            def norm(n, turned=True):
                if n:
                    fetch_table(ACT.Sqrt)
                for t in range(TT):
                    act.wait_ge(var_ready, 2 * n + t + 1)
                    A_(rstd[:, t:t + 1], ms[:, t:t + 1], ACT.Sqrt).then_inc(rstd_ready, 1)
                if n == 0:
                    split_hi(0, 0, 1)
                if turned:
                    for t in range(TT):
                        for half in range(2):
                            act.wait_ge(rows_turned, 4 * n + 2 * t + half + 1)
                            A_(xt_hi[:, 4 * half:4 * half + 4, t * P:(t + 1) * P],
                               ps[:, 2 + 2 * t + half, :].rearrange("p (k s) -> p k s", k=4), ACT.Copy).then_inc(xt_hi_ready, 1)

            def root(n, src, dst):
                act.wait_ge(ev("group_var"), n + 1)
                A_(dst, src, ACT.Sqrt).then_inc(ev("group_root"), 1)

            norm(0)
            for u in range(1, RING):
                split_hi(u, u, 1)
            act.wait_ge(consts_landed, 16)

            def unit1(n):
                q, kind = n, IN1[n][0]
                src = ps[:, q % 2, :]
                two = src.rearrange("p (t c) -> p t c", t=2)
                second = IN1[n][1] % 512 // 256
                dst = {"q": qT[:, 2 * second:2 * second + 2, :], "k": kT[:, 2 * second:2 * second + 2, :],
                       "v": v_sb[:, :, 256 * second:256 * second + 256],
                       "dq": dqk[0].rearrange("p t h e -> p t (h e)")[:, :, 256 * second:256 * second + 256],
                       "dk": dqk[1].rearrange("p t h e -> p t (h e)")[:, :, 256 * second:256 * second + 256],
                       "dv": dv[:, :, 256 * second:256 * second + 256]}[kind]
                evac(U_IN1 + n, q, dst, two)
                split_next(U_IN1 + n)

            def sb_z(g):
                act.wait_ge(ev("sb_z"), g + 1)
                if g:
                    act.wait_ge(ev("sb_pv"), g)
                link(A_(s_c, ps[:, 2:6, 0:384], ACT.Abs, scale=SCALE))
                link(A_(s_c, s_c, ACT.Exp, scale=-1.0))
                A_(s_c, s_c, ACT.Ln, bias=1.0).then_inc(ev("sb_ln"), 1)

            def sb_cum(g):
                act.wait_ge(ev("sb_sum"), g + 1)
                A_(s_c, s_a, ACT.Exp).then_inc(ev("sb_exp"), 1)

            def sb_pv(g):
                act.wait_ge(ev("sb_pv"), g + 1)
                A_(mt_hi[:, 2 * g:2 * g + 2, :], ps[:, 6 + g, :].rearrange("p (k t) -> p k t", k=2), ACT.Copy).then_inc(ev("sb_mt_hi"), 1)

            def rot(i):
                for q in HAS["dk" if i else "dq"]:
                    wait_evacuated(act, q)
                if i:
                    act.wait_ge(ev("rotated"), 1)
                A_(rt, dqk[i], ACT.Square).then_inc(ev("rot_squared"), 1)
                root(i, ss[:, 0:16], rs[:, 0:16])

            def d_t(_):
                for i in range(2):
                    act.wait_ge(ev("d_turned"), i + 1)
                    A_(dqkT[i], ps[:, 2 + 2 * i:4 + 2 * i, :].rearrange("p b (k t) -> p (b k) t", k=2), ACT.Copy).then_inc(ev("d_copied"), 1)

            def d_s(g):
                act.wait_ge(ev("d_max"), g + 1)
                for c in range(4):
                    A_(d_e[g][:, c, 0:P], d_a[g][:, c, 0:P], ACT.Exp, bias=d_nm[g][:, 2 * c:2 * c + 1], scale=SCALE,
                       accum_out=d_sums[g][:, 2 * c:2 * c + 1])
                    last = A_(d_e[g][:, c, P:384], d_a[g][:, c, P:384], ACT.Exp, bias=d_nm[g][:, 2 * c + 1:2 * c + 2], scale=SCALE,
                              accum_out=d_sums[g][:, 2 * c + 1:2 * c + 2])
                last.then_inc(ev("d_exp"), 1)

            def d_x(g):
                act.wait_ge(ev("d_probs_turned"), g + 1)
                A_(s_c[:, 2:4, :], ps[:, 6:8, 0:384], ACT.Copy).then_inc(ev("d_probsT"), 1)

            def d_norm(_):
                for b in range(2):
                    act.wait_ge(ev("d_out_turned"), b + 1)
                    A_(mt_hi[:, 4 + 2 * b:6 + 2 * b, :], ps[:, 2 + b, :].rearrange("p (k t) -> p k t", k=2), ACT.Copy).then_inc(ev("d_mt_hi"), 1)

            def wo(n):
                act.wait_ge(unit_used, U_WO + n + 1)
                split_next(U_WO + n)

            act.wait_ge(small1_landed, 16 * 7)
            act.wait_ge(ev("lam_sums"), 1)
            A_(lam2, lam2, ACT.Exp).then_inc(ev("lam_exp"), 1)
            tasks = {"unit": unit1, "sb_z": sb_z, "sb_cum": sb_cum, "sb_pv": sb_pv, "rot": rot, "d_t": d_t, "d_s": d_s,
                     "d_p": lambda g: None, "d_x": d_x, "d_pv": lambda g: None, "d_rows": lambda _: root(2, ss[:, 0:8], rs[:, 0:8]),
                     "d_norm": d_norm, "wo_half": lambda n: None, "wo": wo}
            for name, n in ORDER1:
                tasks[name](n)

            def ffn_pair(u, s0, h, count):
                for j in range(2):
                    act.wait_ge(unit_used, u + j + 1)
                    A_(silu_t[:, j, :], ps[:, (s0[1] + j) % 2, 0:T], ACT.Silu).then_inc(silu_ready, 1)
                    act.wait_ge(hid_ready, h + j + 1)
                    A_(h_hi_t[:, j, :], hid[:, j, :], ACT.Copy).then_inc(hid_hi, 1)
                    split_hi(u + j + RING, (s0[0] + j) % RING, count[j])
                split_hi(u + 2 + RING, (s0[0] + 2) % RING, count[2])

            def counts(u0, extra):
                return [(u0 + j + RING) // RING + 1 + extra for j in range(3)]

            def ffn(u0, q0, h0):
                with act.Fori(0, FT_DENSE // 2) as i:
                    ffn_pair(u0 + i * 3, (u0, q0), h0 + i * 2, [i + c for c in counts(u0, 0)])

            norm(1)
            ffn(U_FFN1, Q_FFN1, H_FFN1)
            norm(2)

            def mixer(l):
                U, Q = U_MIX[l], Q_MIX[l]

                def unit(n):
                    src = ps[:, (Q + n) % 2, :]
                    two = src.rearrange("p (t c) -> p t c", t=2)
                    act.wait_ge(unit_used, U + n + 1)
                    done = evacuated[(Q + n) % 2]
                    if n < 2:
                        A_(qaT[:, 2 * n:2 * n + 2, :], two, ACT.Copy).then_inc(done, 1)
                    elif n == 2:
                        for half in range(2):
                            for head in range(2):
                                A_(kaT[64 * half:64 * half + 64, head, :], src[64 * head:64 * head + 64, 0:T], ACT.Copy)
                        A_(va, src[:, T:2 * T].rearrange("p (t c) -> p t c", t=2), ACT.Copy).then_inc(done, 1)
                    elif n == 3:
                        A_(qrT, two, ACT.Copy).then_inc(done, 1)
                    elif n == 4:
                        A_(krT, two, ACT.Copy, scale=32 ** -0.5).then_inc(done, 1)
                    elif n < 7:
                        c = (n - 5) * 256
                        A_(vr[:, :, c:c + 256], two, ACT.Copy).then_inc(done, 1)
                    elif n < 11:
                        c = (n - 7) % 2 * 256
                        A_(sg[:, (n - 7) // 2, :, c:c + 256], two, ACT.Silu).then_inc(done, 1)
                    split_next(U + n)

                def sigmoid(c):
                    for n in (13, 14):
                        wait_evacuated(act, Q + n + 4 * c)
                    g = gates[:, :, c * D:(c + 1) * D]
                    A_(g, g, ACT.Sigmoid).then_inc(ev("gate_ready"), 1)

                def log_decay(_):
                    act.wait_ge(ev("mix_small"), 16 * 3 * (l + 1))
                    link(A_(lg_t[:, 1, :], lg_t[:, 0, :], ACT.Abs))
                    A_(lg_t[:, 1, :], lg_t[:, 1, :], ACT.Exp, scale=-1.0).then_inc(ev("lg_exp"), 1)
                    act.wait_ge(ev("lg_one"), l + 1)
                    A_(lg, lg_t[:, 2, :], ACT.Ln).then_inc(ev("lg_ln"), 1)

                def decays(n):
                    act.wait_ge(ev("lg_ready"), l + 1)
                    ahead = table("ahead").rearrange("p (d i) -> p d i", d=2)
                    for h in (2 * n, 2 * n + 1):
                        for way in range(2):
                            last = A_(decay[:, h, way, :], ahead[:, way, :], ACT.Exp, scale=lg[:, way * 8 + h:way * 8 + h + 1])
                    last.then_inc(ev("decay_exp"), 1)

                def gqa_s(g):
                    act.wait_ge(ev("g_max"), 2 * l + g + 1)
                    for c in range(8):
                        A_(g_s[:, c // 2, c % 2, :], g_s[:, c // 2, c % 2, :], ACT.Exp, bias=nm[:, c:c + 1],
                           scale=SCALE, accum_out=sums[:, c:c + 1])
                    A_(rec, rec, ACT.Exp).then_inc(ev("g_exp"), 1)

                def gqa_t(g):
                    act.wait_ge(ev("g_turned"), 2 * l + g + 1)
                    A_(g_t, ps[:, 2:6, :].rearrange("p h (k t) -> p h k t", k=2), ACT.Copy).then_inc(ev("g_probsT"), 1)

                def gqa_out(_):
                    for b in range(2):
                        act.wait_ge(ev("attn_turned"), 2 * l + b + 1)
                        A_(mt_hi[:, 2 * b:2 * b + 2, :], ps[:, 2 + b, :].rearrange("p (k t) -> p k t", k=2), ACT.Copy).then_inc(ev("attn_hi"), 1)

                def ret_mean(b):
                    act.wait_ge(ev("ret_centred"), 2 * l + b + 1)
                    A_(y_sq[b], y_n[b], ACT.Square).then_inc(ev("ret_squared"), 1)

                def ret_t(b):
                    act.wait_ge(ev("ret_turned"), 2 * l + b + 1)
                    A_(mt_hi[:, 4 + 2 * b:6 + 2 * b, :], ps[:, 2 + b, :].rearrange("p (k t) -> p k t", k=2), ACT.Copy).then_inc(ev("ret_hi"), 1)

                def merge(c):
                    for b in (2 * c, 2 * c + 1):
                        act.wait_ge(ev("merged_turned"), 4 * l + b + 1)
                        A_(xt_hi[:, 2 * b:2 * b + 2, :], ps[:, 2 + b, :].rearrange("p (k t) -> p k t", k=2), ACT.Copy).then_inc(ev("merged_hi"), 1)

                def out_unit(n):
                    act.wait_ge(unit_used, U + 23 + n + 1)
                    split_next(U + 23 + n)

                def nothing(n):
                    pass

                tasks = {"unit": unit, "log_decay": log_decay, "decay": decays, "gqa_s": gqa_s, "gqa_t": gqa_t,
                         "gqa_pv": nothing, "gqa_rows": nothing, "gqa_out": gqa_out, "ret_s": nothing, "ret_pv": nothing,
                         "sigmoid": sigmoid, "ret_mean": ret_mean, "ret_norm": nothing, "ret_t": ret_t,
                         "ret_var": lambda b: root(3 + 2 * l + b, ss[:, 0:16], rs[:, 0:16]),
                         "ya": nothing, "ya_out": nothing, "yr": nothing, "next": lambda n: split_next(U + n),
                         "merge": merge, "out": out_unit}
                for name, n in ORDER2:
                    tasks[name](n)

            mixer(0)
            norm(3)
            ffn(U_FFN2, Q_FFN2, H_FFN2)
            norm(4)
            act.wait_ge(ev("router_landed"), 32)
            A_(rw_hi[:, :], rw_raw[:, :], ACT.Copy).then_inc(ev("router_hi"), 1)
            mixer(1)
            norm(5)
            fetch_table(ACT.Exp)
            A_(xs_hi, x[:, :, :], ACT.Copy).then_inc(ev("xs_hi"), 1)
            act.wait_ge(ev("router_product"), 1)
            A_(logit_t[:, :], ps[0:EXPERTS, 2, 0:T], ACT.Copy).then_inc(ev("logit_t"), 1)
            act.wait_ge(ev("top_diff"), 1)
            A_(tw[:, :, 0:1], tw[:, :, 0:1], ACT.Exp).then_inc(ev("top_exp"), 1)

            def take_gathered(n):
                act.wait_ge(ev("gathered_hi"), n + 1)
                A_(xg_hi[:, :], ps[:, 2:4, :], ACT.Copy).then_inc(ev("xg_hi"), 1)

            take_gathered(0)
            act.wait_ge(ev("pick_turned"), 1)
            for half, bank in ((0, 6), (1, 2)):
                last = A_(pick_t[:, 4 * half:4 * half + 4, :], ps[:, bank:bank + 2, :].rearrange("p b (e t) -> p (b e) t", e=2), ACT.Copy)
            last.then_inc(ev("pick_t"), 1)

            def expert(e, dense, last):
                tiles = TT if dense else 1
                u, n = U_MOE + e * PER_EXPERT, e * PAIRS

                def silu(i, p):
                    act.wait_ge(unit_used, u + p + 1)
                    width = P if i == 5 else T
                    src = ps[:, 0, :].rearrange("p (t c) -> p t c", t=TT)[:, 0:tiles, 0:width]
                    A_(silu_t[:, 0:tiles, 0:width], src, ACT.Silu).then_inc(silued, 1)

                def take_hidden(i):
                    act.wait_ge(hid_turned, n + i + 1)
                    js = 1 if i == 5 else 2
                    src = ps[:, 1, :].rearrange("p (j t) -> p j t", j=2)[:, 0:js, 0:tiles * P]
                    A_(h_hi_t[:, 0:js, 0:tiles * P], src, ACT.Copy).then_inc(hid_hi_m, 1)

                def ahead(p):
                    q = p + RING
                    if q < PER_EXPERT or not last:
                        width = 512 if q < PER_EXPERT and EXPERT_UNITS[q][0] in "AB" else UNIT
                        k, slot = q % RAW_MOE, (U_MOE + q) % RING
                        before = (U_MOE + k) // RING if k < RING else 0
                        act.wait_ge(raw_moe_landed[k], 32 * (before + 1 + q // RAW_MOE + e * (PER_EXPERT // RAW_MOE)))
                        act.wait_ge(unit_used, u + p + 1)
                        A_(w_hi[:, slot, 0:width], raw_moe[k][:, 0:width], ACT.Copy).then_inc(hi_ready, 1)

                silu(0, 0)
                ahead(0)
                ahead(1)
                for i in range(1, 5):
                    p = 3 * i - 1
                    take_hidden(i - 1)
                    silu(i, p)
                    for q in range(p, p + 3):
                        ahead(q)
                take_hidden(4)
                silu(5, 14)
                ahead(14)
                ahead(15)
                take_hidden(5)
                if not dense and not last:
                    take_gathered(e + 1)
                act.wait_ge(unit_used, u + PER_EXPERT)
                if dense:
                    A_(ms[:, 0:1], ms[:, 1:2], ACT.Copy).then_inc(ev("y_hi"), 1)
                else:
                    A_(y_hi[:, :], ps[:, 6:8, :], ACT.Copy).then_inc(ev("y_hi"), 1)
                ahead(16)
                ahead(17)
                if dense and not last:
                    take_gathered(e + 1)

            def either(e, last=False):
                n = act.value_load(counts8[0:1, bass.ds(e, 1)], min_val=0, max_val=T)
                with act.If(n > SLOTS):
                    expert(e, True, last)
                with act.Else():
                    expert(e, False, last)

            act.wait_ge(ev("counts_ready"), 1)
            with act.Fori(0, EXPERTS - 1) as e:
                either(e)
            either(EXPERTS - 1, last=True)
            norm(6, turned=False)

        @block.vector
        def _(dve):
            link = Chain(dve, dve_step)
            TTo, TS, STT, CP = nc.vector.tensor_tensor, nc.vector.tensor_scalar, nc.vector.scalar_tensor_tensor, nc.vector.tensor_copy

            def split_lo(u, slot):
                dve.wait_ge(hi_ready, u + 1)
                TTo(w_lo[:, slot, :], raw[:, slot, :], w_hi[:, slot, :].bitcast(F32), ALU.subtract).then_inc(lo_ready, 1)

            def split_next(u):
                if u + RING < U_END:
                    split_lo(u + RING, u % RING)

            def low_of(dst_lo, dst_hi, bank, wait_for, count, done):
                dve.wait_ge(wait_for, count)
                TTo(dst_lo, ps[:, bank, :].rearrange("p (k t) -> p k t", k=2), dst_hi.bitcast(F32), ALU.subtract).then_inc(done, 1)

            def part_stats(t, c):
                return nc.vector.bn_stats(stats[:, t, c, :], x[:, t, c * 512:(c + 1) * 512])

            def norm(n, rms=False, turned=True, ready=None, begun=0, between=None, after=None):
                for t in range(TT):
                    if ready is not None:
                        ready(t)
                    for c in range(begun, 2):
                        last = part_stats(t, c)
                    link(last)
                    link(nc.vector.bn_aggr(mv[:, t, :], stats[:, t, :, :]))
                    if rms:
                        link(TTo(ms[:, t:t + 1], mv[:, t, 0:1], mv[:, t, 0:1], ALU.mult))
                        TS(ms[:, t:t + 1], ms[:, t:t + 1], mv[:, t, 1:2], RMS_EPS, ALU.add, ALU.add).then_inc(var_ready, 1)
                    else:
                        TS(ms[:, t:t + 1], mv[:, t, 1:2], LN_EPS, None, ALU.add).then_inc(var_ready, 1)
                dve.wait_ge(gb_landed, 16 * (n + 1 + max(n - 1, 0)))
                for t in range(TT):
                    dve.wait_ge(rstd_ready, 2 * n + t + 1)
                    link(nc.vector.reciprocal(rstd[:, t:t + 1], rstd[:, t:t + 1]))
                    if rms:
                        STT(normed[:, t, :], x[:, t, :], rstd[:, t:t + 1], gb[:, 0, :], ALU.mult, ALU.mult).then_inc(rows_ready, 1)
                    else:
                        link(STT(x[:, t, :], x[:, t, :], mv[:, t, 0:1], gb[:, 0, :], ALU.subtract, ALU.mult))
                        STT(x[:, t, :], x[:, t, :], rstd[:, t:t + 1], gb[:, 1, :], ALU.mult, ALU.add).then_inc(rows_ready, 1)
                dve.wait_ge(rows_ready, 2 * (n + 1))
                CP(ms[:, 0:1], rstd[:, 0:1]).then_inc(gb_used, 1)
                if between is not None:
                    between()
                if turned:
                    for t in range(TT):
                        for half in range(2):
                            dve.wait_ge(xt_hi_ready, 4 * n + 2 * t + half + 1)
                            k, s = slice(4 * half, 4 * half + 4), slice(t * P, (t + 1) * P)
                            TTo(xt_lo[:, k, s], ps[:, 2 + 2 * t + half, :].rearrange("p (k s) -> p k s", k=4),
                                xt_hi[:, k, s].bitcast(F32), ALU.subtract).then_inc(xt_ready, 1)
                if after is not None:
                    split_next(after)

            def group_rstd(n, eps, width, groups):
                TS(ss[:, 0:groups], ss[:, 0:groups], 1.0 / width, eps, ALU.mult, ALU.add).then_inc(ev("group_var"), 1)
                take_group_rstd(n, groups)

            def take_group_rstd(n, groups):
                dve.wait_ge(ev("group_root"), n + 1)
                link(nc.vector.reciprocal(rs[:, 0:groups], rs[:, 0:groups]))

            norm(0, rms=True, ready=lambda t: dve.wait_ge(x_landed[t], 16), between=lambda: split_lo(0, 0))
            for u in range(1, RING):
                split_lo(u, u)
            dve.wait_ge(small1_landed, 16 * 7)
            dve.wait_ge(consts_landed, 16)
            link(TTo(lam4[:, 0:3:2, :], lam4[:, 0:3:2, :], lam4[:, 1:4:2, :], ALU.mult))
            nc.vector.tensor_reduce(lam2, lam4[:, 0:3:2, :], AX.X, ALU.add).then_inc(ev("lam_sums"), 1)
            dve.wait_ge(ev("lam_exp"), 1)
            link(TTo(lam, lam2[:, 0:1], lam2[:, 1:2], ALU.subtract))
            link(TS(lam, lam, -1.0, -LAMBDA_INIT, ALU.mult, ALU.add))
            link(TS(gsub, gsub, 1.0 - LAMBDA_INIT, None, ALU.mult))
            turns = []
            for i in range(2):
                cos, sin = (gb[:, 1, (2 * i + c) * P:(2 * i + c + 1) * P].rearrange("p (t e) -> p t e", t=TT) for c in range(2))
                by_t = [table(n).rearrange("p (t e) -> p t e", t=TT) for n in ("cos", "sin")]
                g = gq[:, i, :].unsqueeze(1).to_broadcast([P, TT, 64])
                TTo(cos, by_t[0], g, ALU.mult)
                TTo(sin[:, :, 0:32], by_t[1][:, :, 0:32], g[:, :, 32:64], ALU.mult)
                link(TTo(sin[:, :, 32:64], by_t[1][:, :, 32:64], g[:, :, 0:32], ALU.mult))
                turns.append((cos, sin))

            def blocks(v):
                return v.rearrange("p h (b n) -> p h b n", n=P)[:, :, 0:3:2, :]

            mask4 = past.unsqueeze(1).unsqueeze(1).to_broadcast([P, 4, 2, P])
            causal4 = causal.unsqueeze(1).unsqueeze(1).to_broadcast([P, 4, 2, P])

            def unit1(n):
                split_next(U_IN1 + n)

            def sb_z(g):
                dve.wait_ge(ev("sb_ln"), g + 1)
                if g:
                    dve.wait_ge(ev("sb_acc"), g)
                link(TS(s_a, ps[:, 2:6, 0:384], SCALE, 0.0, ALU.mult, ALU.min))
                link(TTo(s_a, s_a, s_c, ALU.subtract))
                link(STT(s_b, ps[:, 2:6, 0:384], -SCALE, s_a, ALU.mult, ALU.add))
                TTo(blocks(s_b), blocks(s_b), mask4, ALU.mult).then_inc(ev("sb_logs"), 1)

            def sb_cum(g):
                dve.wait_ge(ev("sb_acc"), g + 1)
                TTo(s_a, ps[:, 2:6, 0:384], s_a, ALU.add).then_inc(ev("sb_sum"), 1)
                dve.wait_ge(ev("sb_exp"), g + 1)
                TTo(blocks(s_c), blocks(s_c), mask4, ALU.mult).then_inc(ev("sb_weights"), 1)

            def sb_pv(g):
                low_of(mt_lo[:, 2 * g:2 * g + 2, :], mt_hi[:, 2 * g:2 * g + 2, :], 6 + g, ev("sb_mt_hi"), g + 1, ev("sb_mt"))

            def rot(i):
                v = dqk[i]
                dve.wait_ge(ev("rot_squared"), i + 1)
                link(nc.vector.tensor_reduce(ss[:, 0:16].rearrange("p (t h) -> p t h", t=TT), rt, AX.X, ALU.add))
                group_rstd(i, RMS_EPS, 64, 16)
                link(TTo(v, v, rs[:, 0:16].rearrange("p (t h) -> p t h", t=TT).unsqueeze(3).to_broadcast([P, TT, 8, 64]), ALU.mult))
                cos, sin = (w.unsqueeze(2).to_broadcast([P, TT, 8, 64]) for w in turns[i])
                TTo(rt[:, :, :, 0:32], v[:, :, :, 32:64], sin[:, :, :, 0:32], ALU.mult)
                link(TTo(rt[:, :, :, 32:64], v[:, :, :, 0:32], sin[:, :, :, 32:64], ALU.mult))
                link(TTo(v, v, cos, ALU.mult))
                TTo(v, v, rt, ALU.add).then_inc(ev("rotated"), 1)

            def d_s(g):
                dve.wait_ge(ev("d_scores"), g + 1)
                a = d_a[g]
                TTo(blocks(a), blocks(ps[:, 2:6, 0:384]), causal4, ALU.add)
                link(CP(a[:, :, P:2 * P], ps[:, 2:6, P:2 * P]))
                m = d_mx[g].rearrange("p (c t) -> p c t", t=2)
                nc.vector.reduce_max(m[:, :, 0], a[:, :, 0:P], AX.X)
                link(nc.vector.reduce_max(m[:, :, 1], a[:, :, P:384], AX.X))
                TS(d_nm[g], d_mx[g], -SCALE, None, ALU.mult).then_inc(ev("d_max"), 1)

            def d_p(g):
                dve.wait_ge(ev("d_exp"), g + 1)
                if g:
                    dve.wait_ge(ev("d_probs_turned"), g)
                e, rec = d_e[g], d_rec[g]
                link(nc.vector.reciprocal(rec, d_sums[g]))
                r = rec.rearrange("p (h c t) -> p h c t", c=2, t=2)
                link(TS(r[:, :, 1, :], r[:, :, 1, :], lam, None, ALU.mult))
                span = ((0, P), (P, 384))
                for hh in range(2):
                    for t, (a, b) in enumerate(span):
                        k = 4 * hh + 2 + t
                        last = TS(s_c[:, hh, a:b], e[:, 2 * hh + 1, a:b], rec[:, k:k + 1], None, ALU.mult)
                link(last)
                for hh in range(2):
                    for t, (a, b) in enumerate(span):
                        k = 4 * hh + t
                        last = STT(s_c[:, hh, a:b], e[:, 2 * hh, a:b], rec[:, k:k + 1], s_c[:, hh, a:b], ALU.mult, ALU.add)
                last.then_inc(ev("d_probs"), 1)

            def d_pv(g):
                dve.wait_ge(ev("d_product"), g + 1)
                src = ps[:, 6, :].rearrange("p (t h e) -> p t h e", t=TT, h=2)
                CP(d_out[:, :, 2 * g:2 * g + 2, :], src).then_inc(ev("d_out_copied"), 1)

            def d_rows(_):
                dve.wait_ge(ev("d_out_copied"), 2)
                sq = rt.rearrange("p t h e -> p (t h e)").rearrange("p (t h e) -> p t h e", t=TT, h=4)
                link(TTo(sq, d_out, d_out, ALU.mult))
                link(nc.vector.tensor_reduce(ss[:, 0:8].rearrange("p (t h) -> p t h", t=TT), sq, AX.X, ALU.add))
                group_rstd(2, SUBLN_EPS, 128, 8)
                link(TTo(d_out, d_out, rs[:, 0:8].rearrange("p (t h) -> p t h", t=TT).unsqueeze(3).to_broadcast([P, TT, 4, P]), ALU.mult))
                TTo(d_out, d_out, gsub.unsqueeze(1).unsqueeze(1).to_broadcast([P, TT, 4, P]), ALU.mult).then_inc(ev("d_normed"), 1)

            def d_norm(_):
                for b in range(2):
                    low_of(mt_lo[:, 4 + 2 * b:6 + 2 * b, :], mt_hi[:, 4 + 2 * b:6 + 2 * b, :], 2 + b, ev("d_mt_hi"), b + 1, ev("d_mt"))

            def residual_whole(q):
                wait_evacuated(dve, q - 1)
                wait_evacuated(dve, q - 2)

            def add_unit(u, q, n, alpha):
                dve.wait_ge(unit_used, u + 1)
                v = x[:, :, n * 256:(n + 1) * 256]
                STT(v, v, alpha, ps[:, q % 2, :].rearrange("p (t c) -> p t c", t=2), ALU.mult, ALU.add).then_inc(evacuated[q % 2], 1)
                if n < 3:
                    split_next(u)
                if n == 1:
                    residual_whole(q + 1)
                    for t in range(TT):
                        last = part_stats(t, 0)
                    link(last)

            tasks = {"unit": unit1, "sb_z": sb_z, "sb_cum": sb_cum, "sb_pv": sb_pv, "rot": rot, "d_t": lambda n: None,
                     "d_s": d_s, "d_p": d_p, "d_x": lambda n: None, "d_pv": d_pv, "d_rows": d_rows, "d_norm": d_norm,
                     "wo_half": lambda n: None,
                     "wo": lambda n: add_unit(U_WO + n, 12 + n, n, 1.0)}
            for name, n in ORDER1:
                tasks[name](n)
            residual_whole(Q_FFN1)

            def ffn_pair(u, s0, h, last=False):
                for j in range(2):
                    bank = (s0[1] + j) % 2
                    dve.wait_ge(silu_ready, h + j + 1)
                    up = ps[:, bank, T:2 * T]
                    TTo(hid[:, j, :], up, silu_t[:, j, :], ALU.mult).then_inc(hid_ready, 1)
                    dve.wait_ge(hid_hi, h + j + 1)
                    TTo(h_lo_t[:, j, :], hid[:, j, :], h_hi_t[:, j, :].bitcast(F32), ALU.subtract).then_inc(evacuated[bank], 1)
                    split_lo(u + j + RING, (s0[0] + j) % RING)
                if not last:
                    split_lo(u + 2 + RING, (s0[0] + 2) % RING)

            def add_acc(n, alpha):
                def tile(t):
                    dve.wait_ge(acc_done, n + 1)
                    v = x[:, t, :].rearrange("p (c n) -> p c n", c=2)
                    link(STT(v, v, alpha, ps[:, 2 + 2 * t:4 + 2 * t, :], ALU.mult, ALU.add))
                return tile

            def ffn(u0, q0, h0):
                pairs = FT_DENSE // 2
                with dve.Fori(0, pairs - 1) as i:
                    ffn_pair(u0 + i * 3, (u0, q0), h0 + i * 2)
                ffn_pair(u0 + 3 * (pairs - 1), (u0, q0), h0 + 2 * (pairs - 1), last=True)

            norm(1, rms=True, begun=1, after=U_FFN1 - 1)
            ffn(U_FFN1, Q_FFN1, H_FFN1)
            norm(2, ready=add_acc(0, 1.0), after=U_MIX[0] - 1)

            def mixer(l):
                U, Q = U_MIX[l], Q_MIX[l]

                def unit(n):
                    if n >= 11:
                        k = n - 11
                        dve.wait_ge(unit_used, U + n + 1)
                        dve.wait_ge(ev(f"b_row{k % 2}"), 16 * (4 * l + k // 2 + 1))
                        row = b_rows[:, k % 2, :].unsqueeze(1).to_broadcast([P, TT, 256])
                        TTo(gates[:, :, k * 256:(k + 1) * 256], ps[:, (Q + n) % 2, :].rearrange("p (t c) -> p t c", t=2),
                            row, ALU.add).then_inc(evacuated[(Q + n) % 2], 1)
                    split_next(U + n)

                def log_decay(_):
                    dve.wait_ge(ev("lg_exp"), l + 1)
                    TS(lg_t[:, 2, :], lg_t[:, 1, :], 1.0, None, ALU.add).then_inc(ev("lg_one"), 1)
                    dve.wait_ge(ev("lg_ln"), l + 1)
                    link(TS(ss[:, 0:16], lg_t[:, 2, :], -1.0, -1.0, ALU.add, ALU.mult))
                    link(TTo(ss[:, 0:16], lg_t[:, 1, :], ss[:, 0:16], ALU.add))
                    link(nc.vector.reciprocal(rs[:, 0:16], lg_t[:, 2, :]))
                    link(TTo(ss[:, 0:16], ss[:, 0:16], rs[:, 0:16], ALU.mult))
                    link(TTo(lg, lg, ss[:, 0:16], ALU.add))
                    link(TS(lg_t[:, 0, :], lg_t[:, 0, :], 0.0, None, ALU.min))
                    TTo(lg, lg_t[:, 0, :], lg, ALU.subtract).then_inc(ev("lg_ready"), 1)

                def decays(n):
                    dve.wait_ge(ev("decay_exp"), 4 * l + (n + 1) % 4 + 1)
                    on = table("ahead_on").rearrange("p (d i) -> p d i", d=2)
                    two = decay[:, 2 * n:2 * n + 2]
                    link(TTo(two, two, on.unsqueeze(1).to_broadcast([P, 2, 2, T]), ALU.mult))

                def gqa_s(g):
                    dve.wait_ge(ev("g_scores"), 2 * l + g + 1)
                    if g:
                        dve.wait_ge(ev("g_turned"), 2 * l + g)
                    dist = table("dist").rearrange("p (t k) -> p t k", t=TT)
                    for h in range(4):
                        last = STT(g_s[:, h, :, :], dist, -SLOPES[4 * g + h] / SCALE,
                                   ps[:, 2 + h, :].rearrange("p (t k) -> p t k", t=TT), ALU.mult, ALU.add)
                    link(last)
                    link(nc.vector.reduce_max(mx.rearrange("p (h t) -> p h t", t=TT), g_s, AX.X))
                    link(TS(mx, mx, SCALE, None, ALU.mult))
                    dve.wait_ge(ev("mix_small"), 16 * 3 * (l + 1))
                    sk = sink[:, 4 * g:4 * g + 4].unsqueeze(2).to_broadcast([P, 4, TT])
                    mh = mx.rearrange("p (h t) -> p h t", t=TT)
                    link(TTo(mh, mh, sk, ALU.max))
                    TS(nm, mx, -1.0, None, ALU.mult)
                    TTo(rec.rearrange("p (h t) -> p h t", t=TT), sk, mh, ALU.subtract).then_inc(ev("g_max"), 1)
                    dve.wait_ge(ev("g_exp"), 2 * l + g + 1)
                    link(TTo(rec, rec, sums, ALU.add))
                    link(nc.vector.reciprocal(rec_all[:, 8 * g:8 * g + 8], rec))

                def gqa_rows(_):
                    dve.wait_ge(ev("g_product"), 2 * l + 2)
                    r = rec_all.rearrange("p (h t) -> p h t", t=TT)
                    for t in range(TT):
                        last = TTo(attn[:, t, :].rearrange("p (h e) -> p h e", e=64), ps[:, 6 + t, :].rearrange("p (h e) -> p h e", e=64),
                                   r[:, :, t].unsqueeze(2).to_broadcast([P, 8, 64]), ALU.mult)
                    last.then_inc(ev("attn_rows"), 1)

                def gqa_out(_):
                    for b in range(2):
                        low_of(mt_lo[:, 2 * b:2 * b + 2, :], mt_hi[:, 2 * b:2 * b + 2, :], 2 + b, ev("attn_hi"), 2 * l + b + 1, ev("attn_mt"))

                def ret_s(h):
                    n = 8 * l + h
                    dve.wait_ge(ev("r_scores"), n + 1)
                    if h >= 2:
                        dve.wait_ge(ev("r_product"), n - 1)
                    s = ps[:, 2 + h % 2, :]
                    w = r_w[:, h % 2, :, :]
                    TTo(w[:, 0, 0:T], s[:, 0:T], decay[:, h, 0, :], ALU.mult)
                    TTo(w[:, 0, T:384], s[:, T + P:2 * T], decay[:, h, 0, 0:P], ALU.mult)
                    TTo(w[:, 1, 0:T], s[:, T:2 * T], decay[:, h, 1, :], ALU.mult)
                    TTo(w[:, 1, T:384], s[:, 0:P], decay[:, h, 1, P:T], ALU.mult).then_inc(ev("r_weights"), 1)

                def ret_mean(b):
                    dve.wait_ge(ev("r_product"), 8 * l + 4 * b + 4)
                    src = ps[:, 4:8, b * 256:b * 256 + 256].rearrange("p w (h e) -> p w h e", e=64)
                    mean = ss[:, 16:32].rearrange("p (w h) -> p w h", h=4)
                    link(nc.vector.tensor_reduce(mean, src, AX.X, ALU.add))
                    link(TS(ss[:, 16:32], ss[:, 16:32], 1.0 / 64, None, ALU.mult))
                    TTo(y_n[b], src, mean.unsqueeze(3).to_broadcast([P, 2 * TT, 4, 64]), ALU.subtract).then_inc(ev("ret_centred"), 1)

                def ret_var(b):
                    dve.wait_ge(ev("ret_squared"), 2 * l + b + 1)
                    link(nc.vector.tensor_reduce(ss[:, 0:16].rearrange("p (w h) -> p w h", h=4), y_sq[b], AX.X, ALU.add))
                    TS(ss[:, 0:16], ss[:, 0:16], 1.0 / 64, LN_EPS, ALU.mult, ALU.add).then_inc(ev("group_var"), 1)

                def ret_norm(b):
                    take_group_rstd(3 + 2 * l + b, 16)
                    g = sg[:, :, :, b * 256:b * 256 + 256].rearrange("p d t (h e) -> p (d t) h e", e=64)
                    r4 = rs[:, 0:16].rearrange("p (w h) -> p w h", h=4).unsqueeze(3).to_broadcast([P, 2 * TT, 4, 64])
                    link(TTo(y_n[b], y_n[b], r4, ALU.mult))
                    link(TTo(g, g, y_n[b], ALU.mult))
                    c = slice(b * 256, b * 256 + 256)
                    TTo(sg[:, 0, :, c], sg[:, 0, :, c], sg[:, 1, :, c], ALU.add).then_inc(ev("ret_rows"), 1)

                def ret_t(b):
                    low_of(mt_lo[:, 4 + 2 * b:6 + 2 * b, :], mt_hi[:, 4 + 2 * b:6 + 2 * b, :], 2 + b, ev("ret_hi"), 2 * l + b + 1, ev("ret_mt"))

                def product_banks(n):
                    return ps[:, 6:8, :] if n % 2 else ps[:, 0:2, :]

                def ya_out(n):
                    q, c = Q + 19 + n, slice(n * 512, n * 512 + 512)
                    dve.wait_ge(unit_used, U + 19 + n + 1)
                    dve.wait_ge(ev("gate_ready"), 2 * l + 1)
                    TTo(y_mix[:, 0, :, c], product_banks(n), gates[:, :, c], ALU.mult).then_inc(evacuated[q % 2], 1)

                def yr(n):
                    q, c = Q + 21 + n, slice(n * 512, n * 512 + 512)
                    dve.wait_ge(unit_used, U + 21 + n + 1)
                    dve.wait_ge(ev("gate_ready"), 2 * l + 2)
                    TTo(y_mix[:, 1, :, c], product_banks(n), gates[:, :, D + n * 512:D + n * 512 + 512], ALU.mult).then_inc(evacuated[q % 2], 1)
                    wait_evacuated(dve, q - 2)
                    wait_evacuated(dve, q)
                    TTo(merged[:, :, c], y_mix[:, 0, :, c], y_mix[:, 1, :, c], ALU.add).then_inc(ev("merged_rows"), 1)

                def merge(c):
                    for b in (2 * c, 2 * c + 1):
                        low_of(xt_lo[:, 2 * b:2 * b + 2, :], xt_hi[:, 2 * b:2 * b + 2, :], 2 + b, ev("merged_hi"), 4 * l + b + 1, ev("merged_xt"))

                def nothing(n):
                    pass

                tasks = {"unit": unit, "log_decay": log_decay, "decay": decays, "gqa_s": gqa_s, "gqa_t": nothing,
                         "gqa_pv": nothing, "gqa_rows": gqa_rows, "gqa_out": gqa_out, "ret_s": ret_s, "ret_pv": nothing,
                         "sigmoid": nothing, "ret_mean": ret_mean, "ret_var": ret_var, "ret_norm": ret_norm, "ret_t": ret_t,
                         "ya": nothing, "ya_out": ya_out, "yr": yr, "next": lambda n: split_next(U + n), "merge": merge,
                         "out": lambda n: add_unit(U + 23 + n, Q + 23 + n, n, ALPHA)}
                for name, n in ORDER2:
                    tasks[name](n)
                residual_whole(Q + 27)

            mixer(0)
            norm(3, begun=1, after=U_FFN2 - 1)
            ffn(U_FFN2, Q_FFN2, H_FFN2)
            norm(4, ready=add_acc(1, ALPHA), after=U_MIX[1] - 1)
            dve.wait_ge(ev("router_hi"), 1)
            TTo(rw_lo[:, :], rw_raw[:, :], rw_hi[:, :].bitcast(F32), ALU.subtract).then_inc(ev("router_split"), 1)
            mixer(1)
            norm(5, begun=1, after=U_MOE - 1)
            dve.wait_ge(xt_ready, 4 * 6)
            CP(ms[:, 0:1], ms[:, 1:2]).then_inc(ev("routing"), 1)
            dve.wait_ge(ev("xs_hi"), 1)
            TTo(xs_lo, x[:, :, :], xs_hi.bitcast(F32), ALU.subtract).then_inc(ev("xs_ready"), 1)
            dve.wait_ge(ev("logit_turned"), 1)
            link(TTo(logit, ps[:, 3, 32:48].rearrange("p (t n) -> p t n", t=TT), rb.unsqueeze(1).to_broadcast([P, TT, 8]), ALU.add))
            for t in range(TT):
                last = nc.vector.max(top8[:, t, :], logit[:, t, :])
            link(last)
            for t in range(TT):
                last = nc.vector.max_index(idx_u[:, t, :], top8[:, t, :], logit[:, t, :])
            link(last)
            link(CP(idx_f, idx_u[:, :, :]))
            TTo(tw[:, :, 0:1], top8[:, :, 1:2], top8[:, :, 0:1], ALU.subtract).then_inc(ev("top_diff"), 1)
            dve.wait_ge(ev("top_exp"), 1)
            link(TS(tw[:, :, 1:2], tw[:, :, 0:1], 1.0, None, ALU.add))
            link(nc.vector.reciprocal(tw[:, :, 2:3], tw[:, :, 1:2]))
            link(TTo(tw[:, :, 3:4], tw[:, :, 0:1], tw[:, :, 2:3], ALU.mult))
            for t in range(TT):
                for a in range(2):
                    last = TS(gate8[:, a, t, :], table("slot")[:, 0:EXPERTS], idx_f[:, t, a:a + 1], tw[:, t, 2 + a:3 + a], ALU.is_equal, ALU.mult)
            for t in range(TT):
                for a in range(2):
                    last = TS(sel8[:, a, t, :], table("slot")[:, 0:EXPERTS], idx_f[:, t, a:a + 1], None, ALU.is_equal)
            link(last)
            TTo(gate8[:, 0, :, :], gate8[:, 0, :, :], gate8[:, 1, :, :], ALU.add)
            TTo(sel8[:, 0, :, :], sel8[:, 0, :, :], sel8[:, 1, :, :], ALU.add).then_inc(ev("selected"), 1)
            dve.wait_ge(ev("ranked"), 1)
            CP(counts8[:, :], ps[:, 3, 16:24]).then_inc(ev("counts_ready"), 1)
            link(CP(rank8, ps[:, 3, 0:16].rearrange("p (t n) -> p t n", t=TT)))
            for e in range(EXPERTS):
                for t in range(TT):
                    last = TS(pick[:, t, e, :], table("slot"), rank8[:, t, e:e + 1], sel8[:, 0, t, e:e + 1], ALU.is_equal, ALU.mult)
                if e in (0, EXPERTS - 1):
                    last.then_inc(ev("picks"), 1)
            dve.wait_ge(ev("xs_ready"), 1)
            TS(x[:, :, :], x[:, :, :], ALPHA, None, ALU.mult).then_inc(ev("moe_added"), 1)

            def take_gathered(n):
                dve.wait_ge(ev("gathered_lo"), n + 1)
                CP(xg_lo[:, :], ps[:, 4:6, :]).then_inc(ev("xg_ready"), 1)

            take_gathered(0)
            dve.wait_ge(ev("pick_t"), 1)
            pick_flat = pick_t.rearrange("p e t -> p (e t)")
            gates_flat = gate8[:, 0, :, :].rearrange("p t n -> p (t n)")

            def expert(e, dense, last):
                tiles = TT if dense else 1
                u, n = U_MOE + e * PER_EXPERT, e * PAIRS

                def gate_up(i, p):
                    dve.wait_ge(unit_used, u + p + 1)
                    dve.wait_ge(silued, n + i + 1)
                    width, bank, at = (P, 0, P) if i == 5 else (T, 1, 0)
                    src = ps[:, bank, :].rearrange("p (t c) -> p t c", t=TT)[:, 0:tiles, at:at + width]
                    TTo(hid[:, 0:tiles, 0:width], src, silu_t[:, 0:tiles, 0:width], ALU.mult).then_inc(hid_rows, 1)

                def take_hidden(i):
                    dve.wait_ge(hid_hi_m, n + i + 1)
                    js = 1 if i == 5 else 2
                    src = ps[:, 1, :].rearrange("p (j t) -> p j t", j=2)[:, 0:js, 0:tiles * P]
                    TTo(h_lo_t[:, 0:js, 0:tiles * P], src, h_hi_t[:, 0:js, 0:tiles * P].bitcast(F32), ALU.subtract).then_inc(hid_pair, 1)

                def ahead(p):
                    q = p + RING
                    if q < PER_EXPERT or not last:
                        slot = (U_MOE + q) % RING
                        width = 512 if q < PER_EXPERT and EXPERT_UNITS[q][0] in "AB" else UNIT
                        dve.wait_ge(hi_ready, u + q + 1)
                        TTo(w_lo[:, slot, 0:width], raw_moe[q % RAW_MOE][:, 0:width], w_hi[:, slot, 0:width].bitcast(F32),
                            ALU.subtract).then_inc(lo_ready, 1)

                def add():
                    dve.wait_ge(ev("sum_ready"), e + 1)
                    for t, bank in ((0, 2), (1, 4 if dense else 6)):
                        v = x[:, t, :].rearrange("p (c n) -> p c n", c=2)
                        last_add = STT(v, ps[:, bank:bank + 2, :], gates_flat[:, bass.ds(e + t * EXPERTS, 1)], v, ALU.mult, ALU.add)
                    last_add.then_inc(ev("moe_added"), 1)

                if not dense:
                    CP(pick_now[:, :], pick_flat[:, bass.ds(e * T, T)])
                ahead(0)
                gate_up(0, 1)
                take_hidden(0)
                ahead(1)
                for i in range(1, 5):
                    p = 3 * i - 1
                    ahead(p)
                    gate_up(i, p + 2)
                    ahead(p + 1)
                    take_hidden(i)
                    ahead(p + 2)
                gate_up(5, 14)
                ahead(14)
                take_hidden(5)
                ahead(15)
                dve.wait_ge(ev("y_hi"), e + 1)
                if dense:
                    CP(ms[:, 0:1], ms[:, 1:2]).then_inc(ev("y_ready"), 1)
                    add()
                    if not last:
                        take_gathered(e + 1)
                    ahead(16)
                else:
                    TTo(y_lo[:, :], ps[:, 6:8, :].rearrange("p b n -> p (b n)"), y_hi[:, :].bitcast(F32), ALU.subtract).then_inc(ev("y_ready"), 1)
                    if not last:
                        take_gathered(e + 1)
                    ahead(16)
                    add()
                ahead(17)

            def either(e, last=False):
                n = dve.value_load(counts8[0:1, bass.ds(e, 1)], min_val=0, max_val=T)
                with dve.If(n > SLOTS):
                    expert(e, True, last)
                with dve.Else():
                    expert(e, False, last)

            with dve.Fori(0, EXPERTS - 1) as e:
                either(e)
            either(EXPERTS - 1, last=True)
            dve.wait_ge(ev("moe_added"), EXPERTS + 1)
            norm(6, turned=False)

        @block.tensor
        def _(pe):
            MM, TR = nc.tensor.matmul, nc.tensor.transpose

            def product(dst, a_hi, a_lo, b_hi, b_lo, start, stop):
                MM(dst, a_hi, b_hi, start=start, stop=False)
                MM(dst, a_hi, b_lo, start=False, stop=False)
                return MM(dst, a_lo, b_hi, start=False, stop=stop)

            def weights_still(s, col, dst, xh=xt_hi, xl=xt_lo, step=256, fresh=None):
                for k in range(KT):
                    if fresh is not None and k % 4 == 0:
                        pe.wait_ge(xt_ready, 4 * fresh + 3 + k // 4)
                    w = slice(k * step + col, k * step + col + P)
                    last = product(dst, w_hi[:, s, w], w_lo[:, s, w], xh[:, k, :], xl[:, k, :], k == 0, k == KT - 1)
                return last

            def tokens_still(s, t, dst, xh=xt_hi, xl=xt_lo, k0=0, nk=KT, step=256, col=0, width=256):
                for k in range(nk):
                    w = slice(k * step + col, k * step + col + width)
                    tok = slice(t * P, (t + 1) * P)
                    last = product(dst, xh[:, k0 + k, tok], xl[:, k0 + k, tok], w_hi[:, s, w], w_lo[:, s, w], k == 0, k == nk - 1)
                return last

            def begin(u, q):
                pe.wait_ge(lo_ready, u + 1)
                if q >= 2:
                    wait_evacuated(pe, q - 2)

            def turn_rows(n, rows):
                for t in range(TT):
                    pe.wait_ge(rows_ready, 2 * n + t + 1)
                    for k in range(KT):
                        last = TR(ps[:, 2 + 2 * t + k // 4, k % 4 * P:(k % 4 + 1) * P], rows[:, t, k * P:(k + 1) * P], ident)
                        if k % 4 == 3:
                            last.then_inc(rows_turned, 1)

            def turn_four(src, done):
                for k in range(4):
                    for t in range(TT):
                        last = TR(ps[:, 2 + k // 2, k % 2 * T + t * P:k % 2 * T + (t + 1) * P], src[:, t, k * P:(k + 1) * P], ident)
                    if k % 2:
                        last.then_inc(done, 1)

            pe.wait_ge(ev("ident_landed"), 16)
            turn_rows(0, normed)

            def unit1(n):
                s = n % RING
                begin(n, n)
                for c in range(2):
                    dst = ps[:, n % 2, c * 256:(c + 1) * 256]
                    last = weights_still(s, c * P, dst, fresh=0 if n == 0 else None) if IN1[n][0] in "qk" else tokens_still(s, c, dst)
                last.then_inc(unit_used, 1)

            def sb_z(g):
                for kind in "qk":
                    wait_evacuated(pe, HAS[kind][g])
                if g:
                    pe.wait_ge(ev("sb_sum"), g)
                for i in range(4):
                    h = 4 * g + i
                    r = slice(h % 2 * 64, h % 2 * 64 + 64)
                    MM(ps[:, 2 + i, 0:T], kT[r, h // 2, 0:P], qT[r, h // 2, :], start=True, stop=True)
                    last = MM(ps[:, 2 + i, T:384], kT[r, h // 2, P:T], qT[r, h // 2, P:T], start=True, stop=True)
                last.then_inc(ev("sb_z"), 1)

            def sb_cum(g):
                pe.wait_ge(ev("sb_logs"), g + 1)
                for i in range(4):
                    MM(ps[:, 2 + i, 0:P], later, s_b[:, i, 0:P], start=True, stop=True)
                    MM(ps[:, 2 + i, P:T], later, s_b[:, i, P:T], start=True, stop=False)
                    MM(ps[:, 2 + i, P:T], ones, s_b[:, i, T:384], start=False, stop=True)
                    last = MM(ps[:, 2 + i, T:384], later, s_b[:, i, T:384], start=True, stop=True)
                last.then_inc(ev("sb_acc"), 1)

            def sb_pv(g):
                for q in HAS["v"]:
                    wait_evacuated(pe, q)
                pe.wait_ge(ev("sb_weights"), g + 1)
                for i in range(4):
                    h = 4 * g + i
                    r = slice(h % 2 * 64, h % 2 * 64 + 64)
                    c = i // 2 * 256
                    e = slice(h * 64, h * 64 + 64)
                    MM(ps[r, 6 + g, c:c + P], v_sb[:, 0, e], s_c[:, i, 0:P], start=True, stop=True)
                    MM(ps[r, 6 + g, c + P:c + T], v_sb[:, 0, e], s_c[:, i, P:T], start=True, stop=False)
                    last = MM(ps[r, 6 + g, c + P:c + T], v_sb[:, 1, e], s_c[:, i, T:384], start=False, stop=True)
                last.then_inc(ev("sb_pv"), 1)

            def d_t(_):
                pe.wait_ge(ev("sb_sum"), 2)
                for i in range(2):
                    pe.wait_ge(ev("rotated"), i + 1)
                    v = dqk[i].rearrange("p t h e -> p t (h e)")
                    for h in range(4):
                        for t in range(TT):
                            last = TR(ps[:, 2 + 2 * i + h // 2, h % 2 * T + t * P:h % 2 * T + (t + 1) * P], v[:, t, h * P:(h + 1) * P], ident)
                    last.then_inc(ev("d_turned"), 1)

            def d_s(g):
                pe.wait_ge(ev("d_copied"), 2)
                if g:
                    pe.wait_ge(ev("d_max"), g)
                for c in range(4):
                    h = 2 * g + c // 2
                    r = slice(c % 2 * 64, c % 2 * 64 + 64)
                    MM(ps[:, 2 + c, 0:P], dqkT[0][r, h, 0:P], dqkT[1][r, h, 0:P], start=True, stop=True)
                    last = MM(ps[:, 2 + c, P:384], dqkT[0][r, h, P:T], dqkT[1][r, h, :], start=True, stop=True)
                last.then_inc(ev("d_scores"), 1)

            def d_x(g):
                pe.wait_ge(ev("d_probs"), g + 1)
                if g:
                    pe.wait_ge(ev("d_out_copied"), g)
                else:
                    pe.wait_ge(ev("sb_mt"), 2)
                for i in range(2):
                    for b in range(3):
                        last = TR(ps[:, 6 + i, b * P:(b + 1) * P], s_c[:, i, b * P:(b + 1) * P], ident)
                last.then_inc(ev("d_probs_turned"), 1)

            def d_pv(g):
                for q in HAS["dv"]:
                    wait_evacuated(pe, q)
                pe.wait_ge(ev("d_probsT"), g + 1)
                for i in range(2):
                    e = slice((2 * g + i) * P, (2 * g + i + 1) * P)
                    MM(ps[:, 6, i * P:(i + 1) * P], s_c[:, 2 + i, 0:P], dv[:, 0, e], start=True, stop=True)
                    MM(ps[:, 6, T + i * P:T + (i + 1) * P], s_c[:, 2 + i, P:T], dv[:, 0, e], start=True, stop=False)
                    last = MM(ps[:, 6, T + i * P:T + (i + 1) * P], s_c[:, 2 + i, T:384], dv[:, 1, e], start=False, stop=True)
                last.then_inc(ev("d_product"), 1)

            def d_norm(_):
                pe.wait_ge(ev("d_normed"), 1)
                turn_four(d_out.rearrange("p t h e -> p t (h e)"), ev("d_out_turned"))

            def wo_half(n):
                if n == 0:
                    pe.wait_ge(ev("sb_mt"), 2)
                    pe.wait_ge(zeroed, 1)
                begin(U_WO + n, 12 + n)
                MM(ps[:, (12 + n) % 2, :], zeros[:, 0:P], zeros[:, :], start=True, stop=False)
                for t in range(TT):
                    for k in range(KT // 2):
                        w = slice(k * 256, k * 256 + 256)
                        tok, s = slice(t * P, (t + 1) * P), (U_WO + n) % RING
                        product(ps[:, (12 + n) % 2, t * 256:(t + 1) * 256], mt_hi[:, k, tok], mt_lo[:, k, tok],
                                w_hi[:, s, w], w_lo[:, s, w], False, False)

            def wo(n):
                u = U_WO + n
                if n == 0:
                    pe.wait_ge(ev("d_mt"), 2)
                begin(u, 12 + n)
                for t in range(TT):
                    for k in range(KT // 2 if n < 2 else 0, KT):
                        w = slice(k * 256, k * 256 + 256)
                        tok, s = slice(t * P, (t + 1) * P), u % RING
                        last = product(ps[:, (12 + n) % 2, t * 256:(t + 1) * 256], mt_hi[:, k, tok], mt_lo[:, k, tok],
                                       w_hi[:, s, w], w_lo[:, s, w], n >= 2 and k == 0, n >= 2 and k == KT - 1)
                if n < 2:
                    last = MM(ps[:, (12 + n) % 2, :], zeros[:, 0:P], zeros[:, :], start=False, stop=True)
                last.then_inc(unit_used, 1)

            tasks = {"unit": unit1, "sb_z": sb_z, "sb_cum": sb_cum, "sb_pv": sb_pv, "rot": lambda n: None, "d_t": d_t,
                     "d_s": d_s, "d_p": lambda n: None, "d_x": d_x, "d_pv": d_pv, "d_rows": lambda n: None, "d_norm": d_norm,
                     "wo_half": wo_half, "wo": wo}
            for name, n in ORDER1:
                tasks[name](n)

            def ffn_pair(u, s0, half_q, fresh=None):
                for j in range(2):
                    s, bank = (s0[0] + j) % RING, (s0[1] + j) % 2
                    pe.wait_ge(lo_ready, u + j + 1)
                    pe.wait_ge(evacuated[bank], half_q[j])
                    weights_still(s, 0, ps[:, bank, 0:T], step=P, fresh=fresh if j == 0 else None)
                    for k in range(KT):
                        w = slice(1024 + k * P, 1024 + (k + 1) * P)
                        last = product(ps[:, bank, T:2 * T], w_hi[:, s, w], w_lo[:, s, w], xt_hi[:, k, :], xt_lo[:, k, :], k == 0, k == KT - 1)
                    last.then_inc(unit_used, 1)
                if fresh is not None:
                    clear_acc()
                s = (s0[0] + 2) % RING
                pe.wait_ge(lo_ready, u + 3)
                for j in range(2):
                    pe.wait_ge(evacuated[(s0[1] + j) % 2], half_q[j] + 1)
                    for t in range(TT):
                        tok = slice(t * P, (t + 1) * P)
                        for c in range(2):
                            w = slice(j * 1024 + c * 512, j * 1024 + (c + 1) * 512)
                            dst = ps[:, 2 + 2 * t + c, :]
                            MM(dst, h_hi_t[:, j, tok], w_hi[:, s, w], start=False, stop=False)
                            MM(dst, h_hi_t[:, j, tok], w_lo[:, s, w], start=False, stop=False)
                            last = MM(dst, h_lo_t[:, j, tok], w_hi[:, s, w], start=False, stop=False)
                last.then_inc(unit_used, 1)

            def clear_acc():
                pe.wait_ge(zeroed, 1)
                for b in range(4):
                    MM(ps[:, 2 + b, :], zeros[:, 0:P], zeros[:, :], start=True, stop=False)

            def close_acc():
                for b in range(4):
                    last = MM(ps[:, 2 + b, :], zeros[:, 0:P], zeros[:, :], start=False, stop=True)
                last.then_inc(acc_done, 1)

            def ffn(u0, q0, fresh):
                ffn_pair(u0, (u0, q0), [(q0 + j) // 2 for j in range(2)], fresh)
                with pe.Fori(1, FT_DENSE // 2) as i:
                    ffn_pair(u0 + i * 3, (u0, q0), [i + (q0 + j) // 2 for j in range(2)])
                close_acc()

            turn_rows(1, normed)
            ffn(U_FFN1, Q_FFN1, 1)
            turn_rows(2, x)

            def mixer(l):
                U, Q = U_MIX[l], Q_MIX[l]

                def unit(n):
                    u, q = U + n, Q + n
                    s = u % RING
                    begin(u, q)
                    if n == 2:
                        weights_still(s, 0, ps[:, q % 2, 0:T])
                        for t in range(TT):
                            last = tokens_still(s, t, ps[:, q % 2, T + t * P:T + (t + 1) * P], col=P, width=P)
                    else:
                        for c in range(2):
                            dst = ps[:, q % 2, c * 256:(c + 1) * 256]
                            last = weights_still(s, c * P, dst, fresh=2 + 2 * l if n == 0 else None) if n in (0, 1, 3, 4) else tokens_still(s, c, dst)
                    last.then_inc(unit_used, 1)

                def gqa_s(g):
                    for q in range(3):
                        wait_evacuated(pe, Q + q)
                    if g:
                        pe.wait_ge(ev("g_probsT"), 2 * l + g)
                    for i in range(4):
                        h = 4 * g + i
                        r = slice(h % 2 * 64, h % 2 * 64 + 64)
                        for t in range(TT):
                            last = MM(ps[:, 2 + i, t * T:(t + 1) * T], qaT[r, h // 2, t * P:(t + 1) * P], kaT[r, h // 4, :], start=True, stop=True)
                    last.then_inc(ev("g_scores"), 1)

                def gqa_t(g):
                    pe.wait_ge(ev("g_exp"), 2 * l + g + 1)
                    for i in range(4):
                        for k in range(2):
                            for t in range(TT):
                                last = TR(ps[:, 2 + i, k * T + t * P:k * T + (t + 1) * P], g_s[:, i, t, k * P:(k + 1) * P], ident)
                    last.then_inc(ev("g_turned"), 1)

                def gqa_pv(g):
                    pe.wait_ge(ev("g_probsT"), 2 * l + g + 1)
                    for i in range(4):
                        h = 4 * g + i
                        for t in range(TT):
                            for k in range(2):
                                last = MM(ps[:, 6 + t, h * 64:(h + 1) * 64], g_t[:, i, k, t * P:(t + 1) * P], va[:, k, g * 64:(g + 1) * 64],
                                          start=k == 0, stop=k == 1)
                    last.then_inc(ev("g_product"), 1)

                def gqa_out(_):
                    pe.wait_ge(ev("attn_rows"), l + 1)
                    turn_four(attn, ev("attn_turned"))

                def ret_s(h):
                    n = 8 * l + h
                    for q in (3, 4):
                        wait_evacuated(pe, Q + q)
                    if h < 2:
                        pe.wait_ge(ev("attn_mt"), 2 * l + 2)
                    else:
                        pe.wait_ge(ev("r_weights"), n - 1)
                    r = slice(h % 4 * 32, h % 4 * 32 + 32)
                    for k in range(2):
                        last = MM(ps[:, 2 + h % 2, k * T:(k + 1) * T], krT[r, h // 4, k * P:(k + 1) * P], qrT[r, h // 4, :], start=True, stop=True)
                    last.then_inc(ev("r_scores"), 1)

                def ret_pv(h):
                    n = 8 * l + h
                    for q in (5, 6):
                        wait_evacuated(pe, Q + q)
                    if h == 4:
                        pe.wait_ge(ev("ret_centred"), 2 * l + 1)
                    pe.wait_ge(ev("r_weights"), n + 1)
                    e = slice(h * 64, h * 64 + 64)
                    w = r_w[:, h % 2, :, :]
                    for way in range(2):
                        near, far = way, 1 - way
                        own = slice(near * P, near * P + P)
                        both = slice(far * P, far * P + P)
                        MM(ps[:, 4 + 2 * way + near, e], w[:, way, own], vr[:, near, e], start=True, stop=True)
                        MM(ps[:, 4 + 2 * way + far, e], w[:, way, both], vr[:, near, e], start=True, stop=False)
                        last = MM(ps[:, 4 + 2 * way + far, e], w[:, way, T:384], vr[:, far, e], start=False, stop=True)
                    last.then_inc(ev("r_product"), 1)

                def ret_t(b):
                    if b == 0:
                        pe.wait_ge(ev("r_weights"), 8 * l + 8)
                    pe.wait_ge(ev("ret_rows"), 2 * l + b + 1)
                    for k in range(2):
                        for t in range(TT):
                            last = TR(ps[:, 2 + b, k * T + t * P:k * T + (t + 1) * P], sg[:, 0, t, (2 * b + k) * P:(2 * b + k + 1) * P], ident)
                    last.then_inc(ev("ret_turned"), 1)

                def half_product(n):
                    u, q = U + 19 + n, Q + 19 + n
                    if n == 0:
                        pe.wait_ge(ev("attn_mt"), 2 * l + 2)
                    if n == 2:
                        pe.wait_ge(ev("ret_mt"), 2 * l + 2)
                    if n == 1:
                        pe.wait_ge(ev("ret_centred"), 2 * l + 2)
                    begin(u, q)
                    if n == 0:
                        wait_evacuated(pe, q - 1)
                    for t in range(TT):
                        last = tokens_still(u % RING, t, ps[:, n % 2 * 6 + t, :], mt_hi, mt_lo, k0=n // 2 * 4, nk=4, step=512, width=512)
                    last.then_inc(unit_used, 1)

                def merge(c):
                    pe.wait_ge(ev("merged_rows"), 2 * l + c + 1)
                    if c:
                        pe.wait_ge(ev("ret_centred"), 2 * l + 2)
                    for k in range(4 * c, 4 * c + 4):
                        for t in range(TT):
                            last = TR(ps[:, 2 + k // 2, k % 2 * T + t * P:k % 2 * T + (t + 1) * P], merged[:, t, k * P:(k + 1) * P], ident)
                        if k % 2:
                            last.then_inc(ev("merged_turned"), 1)

                def out_unit(n):
                    u, q = U + 23 + n, Q + 23 + n
                    if n == 0:
                        pe.wait_ge(ev("merged_xt"), 4 * l + 4)
                    begin(u, q)
                    for t in range(TT):
                        last = tokens_still(u % RING, t, ps[:, q % 2, t * 256:(t + 1) * 256])
                    last.then_inc(unit_used, 1)

                def nothing(n):
                    pass

                tasks = {"unit": unit, "log_decay": nothing, "decay": nothing, "gqa_s": gqa_s, "gqa_t": gqa_t, "gqa_pv": gqa_pv,
                         "gqa_rows": nothing, "gqa_out": gqa_out, "ret_s": ret_s, "ret_pv": ret_pv, "sigmoid": nothing,
                         "ret_mean": nothing, "ret_var": nothing, "ret_norm": nothing, "ret_t": ret_t,
                         "ya": half_product, "ya_out": nothing, "yr": lambda n: half_product(2 + n), "next": nothing,
                         "merge": merge, "out": out_unit}
                for name, n in ORDER2:
                    tasks[name](n)

            mixer(0)
            turn_rows(3, x)
            ffn(U_FFN2, Q_FFN2, 3)
            turn_rows(4, x)
            mixer(1)
            turn_rows(5, x)
            pe.wait_ge(xt_ready, 4 * 6)
            pe.wait_ge(ev("router_split"), 1)
            for k in range(KT):
                w = slice(k * 8, k * 8 + 8)
                last = product(ps[0:EXPERTS, 2, 0:T], rw_hi[:, w], rw_lo[:, w], xt_hi[:, k, :], xt_lo[:, k, :], k == 0, k == KT - 1)
            last.then_inc(ev("router_product"), 1)
            pe.wait_ge(ev("logit_t"), 1)
            for t in range(TT):
                last = TR(ps[:, 3, 32 + t * 8:40 + t * 8], logit_t[:, t * P:(t + 1) * P], ident[0:EXPERTS, 0:EXPERTS])
            last.then_inc(ev("logit_turned"), 1)
            pe.wait_ge(ev("selected"), 1)
            first, second = sel8[:, 0, 0, :], sel8[:, 0, 1, :]
            MM(ps[:, 3, 0:8], past, first, start=True, stop=True)
            MM(ps[:, 3, 8:16], past, second, start=True, stop=False)
            MM(ps[:, 3, 8:16], ones, first, start=False, stop=True)
            MM(ps[:, 3, 16:24], ones, first, start=True, stop=False)
            MM(ps[:, 3, 16:24], ones, second, start=False, stop=True).then_inc(ev("ranked"), 1)
            pick_cols = pick_r[:, :]

            def gather_part(e, part):
                src = (xs_hi, xs_lo)[part]
                for k in range(KT):
                    dst = ps[:, 2 + 2 * part + k // 4, k % 4 * P:k % 4 * P + P]
                    for t in range(TT):
                        last = MM(dst, src[:, t, k * P:(k + 1) * P], pick_cols[:, bass.ds(e * P + t * EXPERTS * P, P)],
                                  start=t == 0, stop=t == 1)
                last.then_inc(ev("gathered_lo" if part else "gathered_hi"), 1)

            pe.wait_ge(ev("xs_ready"), 1)
            pe.wait_ge(ev("picks"), 1)
            pe.wait_ge(ev("counts_ready"), 1)
            gather_part(0, 0)
            gather_part(0, 1)
            pe.wait_ge(ev("picks"), 2)
            for e in range(EXPERTS):
                if e == EXPERTS // 2:
                    pe.wait_ge(ev("xg_hi"), 1)
                for t in range(TT):
                    last = TR(ps[:, (6, 7, 2, 3)[e // 2], e % 2 * T + t * P:e % 2 * T + (t + 1) * P], pick[:, t, e, :].bitcast(F32), ident)
            last.then_inc(ev("pick_turned"), 1)
            pe.wait_ge(ev("xg_ready"), 1)
            xg = [v[:, :].rearrange("p (k s) -> p k s", k=KT) for v in (xg_hi, xg_lo)]

            def expert(e, dense, last_one):
                xh, xl, tiles = (xt_hi, xt_lo, TT) if dense else (*xg, 1)
                u, n = U_MOE + e * PER_EXPERT, e * PAIRS
                sums = [(t, c, 2 + 2 * t + c) for t in range(TT) for c in range(2)] if dense else [(0, c, 6 + c) for c in range(2)]

                def rows(p, bank, halfway=None):
                    s = (U_MOE + p) % RING
                    kind = EXPERT_UNITS[p][0]
                    if kind == "M":
                        w = [v[:, s, :].rearrange("p (a k n) -> p k a n", a=2, k=KT) for v in (w_hi, w_lo)]
                    else:
                        w = [v[:, s, :].rearrange("p (k n) -> p k n", k=KT) for v in (w_hi, w_lo)]
                    pe.wait_ge(lo_ready, u + p + 1)
                    for t in range(tiles):
                        dst = ps[:, bank, t * T:(t + 1) * T]
                        if kind == "M":
                            dst = dst.rearrange("p (a n) -> p a n", a=2)
                        tok = slice(t * P, (t + 1) * P)
                        for k in range(KT):
                            last = product(dst, xh[:, k, tok], xl[:, k, tok], w[0][:, k], w[1][:, k], k == 0, k == KT - 1)
                            if t == 0 and k == 3 and halfway is not None:
                                halfway()
                    last.then_inc(unit_used, 1)

                def turn_hidden(i):
                    pe.wait_ge(hid_rows, n + i + 1)
                    for j in range(1 if i == 5 else 2):
                        for t in range(tiles):
                            last = TR(ps[:, 1, j * T + t * P:j * T + (t + 1) * P], hid[:, t, j * P:(j + 1) * P], ident)
                    last.then_inc(hid_turned, 1)

                def down(j, p, at, c_of=None, first=False, final=False):
                    s = (U_MOE + p) % RING
                    for t, c, bank in sums:
                        if c_of in (None, c):
                            tok = slice(t * P, (t + 1) * P)
                            w = slice(at, at + 512) if c_of is not None else slice(at + c * 512, at + (c + 1) * 512)
                            last = product(ps[:, bank, :], h_hi_t[:, j, tok], h_lo_t[:, j, tok], w_hi[:, s, w], w_lo[:, s, w], first, final)
                    return last

                def down_pair(i, p):
                    pe.wait_ge(lo_ready, u + p + 1)
                    pe.wait_ge(hid_pair, n + i + 1)
                    if i == 0:
                        pe.wait_ge(ev("pick_t"), 1)
                        pe.wait_ge(ev("moe_added"), e + 1)
                    down(0, p, 0, first=i == 0)
                    down(1, p, 1024).then_inc(unit_used, 1)

                rows(0, 0)
                rows(1, 1)
                for i in range(1, 5):
                    p = 3 * i - 1
                    pe.wait_ge(silued, n + i)
                    rows(p, 0, lambda: turn_hidden(i - 1))
                    down_pair(i - 1, p + 1)
                    rows(p + 2, 1)
                pe.wait_ge(silued, n + 5)
                rows(14, 0, lambda: turn_hidden(4))
                down_pair(4, 15)
                turn_hidden(5)
                if not dense and not last_one:
                    gather_part(e + 1, 0)
                pe.wait_ge(hid_pair, n + 6)
                for c in range(2):
                    pe.wait_ge(lo_ready, u + 17 + c)
                    down(0, 16 + c, 0, c, final=not dense).then_inc(unit_used, 1)
                if dense:
                    for _, _, bank in sums:
                        last = MM(ps[:, bank, :], zeros[:, 0:P], zeros[:, :], start=False, stop=True)
                    last.then_inc(ev("sum_ready"), 1)
                if dense and not last_one:
                    pe.wait_ge(ev("moe_added"), e + 2)
                    gather_part(e + 1, 0)
                    gather_part(e + 1, 1)
                    pe.wait_ge(ev("xg_hi"), e + 2)
                    pe.wait_ge(ev("xg_ready"), e + 2)
                if not dense:
                    if not last_one:
                        gather_part(e + 1, 1)
                        pe.wait_ge(ev("xg_hi"), e + 2)
                    pe.wait_ge(ev("y_ready"), e + 1)
                    for t, bank in ((0, 2), (1, 6)):
                        for c in range(2):
                            tok, w = slice(t * P, (t + 1) * P), slice(c * 512, (c + 1) * 512)
                            MM(ps[:, bank + c, :], pick_now[:, tok], y_hi[:, w], start=True, stop=False)
                            last = MM(ps[:, bank + c, :], pick_now[:, tok], y_lo[:, w], start=False, stop=True)
                    last.then_inc(ev("sum_ready"), 1)
                    if not last_one:
                        pe.wait_ge(ev("xg_ready"), e + 2)

            def either(e, last=False):
                n = pe.value_load(counts8[0:1, bass.ds(e, 1)], min_val=0, max_val=T)
                with pe.If(n > SLOTS):
                    expert(e, True, last)
                with pe.Else():
                    expert(e, False, last)

            with pe.Fori(0, EXPERTS - 1) as e:
                either(e)
            either(EXPERTS - 1, last=True)


_INS = ["x", "attn_norm_g", "w_in", "diff_q_norm_g", "diff_k_norm_g", "lambda_q1", "lambda_k1", "lambda_q2",
        "lambda_k2", "diff_subln_g", "w_o", "ffn_norm_g", "w_gate", "w_up", "w_down", "ln_emb_g_2", "ln_emb_b_2",
        "w_in_2", "b_gate_2", "sink_logits_2", "decay_fwd_2", "decay_bwd_2", "w_o_attn_2", "w_o_ret_2", "w_out_2",
        "ln1_g_2", "ln1_b_2", "ffn_w1_2", "ffn_w3_2", "ffn_w2_2", "router_w_2", "router_b_2", "moe_w1_2", "moe_w3_2",
        "moe_w2_2", "ln2_g_2", "ln2_b_2"]


def kernel(**inputs):
    import numpy as _np
    import concourse.bacc as _bacc
    from concourse.bass_utils import run_bass_kernel_spmd as _run

    nc = _bacc.Bacc("TRN2", target_bir_lowering=False, num_devices=1)
    arrays, aps = {}, {}
    for name in _INS:
        a = _np.ascontiguousarray(inputs[name])
        arrays[f"in_{name}_dram"] = a
        aps[name] = nc.dram_tensor(f"in_{name}_dram", a.shape, mybir.dt.from_np(a.dtype), kind="ExternalInput").ap()
    arrays["const_dram"] = CONST_TABLE
    const = nc.dram_tensor("const_dram", CONST_TABLE.shape, F32, kind="ExternalInput").ap()
    out = nc.dram_tensor("out_dram", (1, T, D), F32, kind="ExternalOutput").ap()
    two_blocks(nc, aps, const, out)
    r = _run(nc, [arrays], core_ids=[0])
    return r.results[0]["out_dram"]
```
